# Optimizing a Trainium2 kernel written in Bass

```python
import math
import jax, jax.numpy as jnp
from jax import lax
import numpy as np

D_MODEL = 1024
BATCH = 1
SEQ = 256
DEPTH = 1

GRID_W = 64
CTX_LEN = 256
MIX_W = D_MODEL
POOL_W = MIX_W // 2
SSM_W = MIX_W - POOL_W
POOL_WINDOWS = (2, 4, 8, 16)
POOL_GROUPS = len(POOL_WINDOWS)
POOL_GW = POOL_W // POOL_GROUPS
SSM_GROUP = 16
SSM_GROUPS = SSM_W // SSM_GROUP
SSM_STATE = 64
N_EXPERTS = 32
N_EXPERT_GROUPS = 4
EXPERTS_PER_GROUP = N_EXPERTS // N_EXPERT_GROUPS
TOP_K = 2
D_EXPERT = D_MODEL // 2
ROUTE_BLOCK = 128
EPS = 1e-6
DT_MIN = 0.001
DT_MAX = 0.1
N_MOD = 6

kernel_name = "hybrid_pool_s5_moe_prefix_dit"

def rmsnorm(x, g):
    xf = x.astype(jnp.float32)
    y = xf * lax.rsqrt(jnp.mean(xf * xf, axis=-1, keepdims=True) + EPS)
    return (y * g.astype(jnp.float32)).astype(x.dtype)

def modulate(h, shift, scale):
    return h * (1 + scale) + shift

def centred_mean(u, w):
    n = u.shape[-2]
    cs = jnp.cumsum(u.astype(jnp.float32), axis=-2)
    cs = jnp.concatenate([jnp.zeros_like(cs[..., :1, :]), cs], axis=-2)
    t = np.arange(n)
    lo = np.maximum(t - w // 2, 0)
    hi = np.minimum(t + w // 2, n)
    s = jnp.take(cs, hi, axis=-2) - jnp.take(cs, lo, axis=-2)
    cnt = (hi - lo).astype(np.float32)[:, None]
    return (s / cnt).astype(u.dtype)

def pool_mixer(u, w_pool, s_pool):
    parts = []
    for g, w in enumerate(POOL_WINDOWS):
        ug = u[..., g * POOL_GW:(g + 1) * POOL_GW]
        parts.append(centred_mean(ug, w) - ug)
    p = jnp.stack(parts, axis=-2)
    y = jnp.einsum('...ngc,gcd->...ngd', p, w_pool)
    return y.reshape(u.shape) * s_pool

def ssm_discretise(a_re, a_im, log_dt, b_re, b_im):
    a_re = jnp.minimum(a_re.astype(jnp.float32), -1e-4)
    a_im = a_im.astype(jnp.float32)
    dt = jnp.exp(log_dt.astype(jnp.float32))[:, None]
    mag = jnp.exp(a_re * dt)
    lb_re = mag * jnp.cos(a_im * dt)
    lb_im = mag * jnp.sin(a_im * dt)
    num_re = lb_re - 1.0
    num_im = lb_im
    den = a_re * a_re + a_im * a_im
    k_re = (num_re * a_re + num_im * a_im) / den
    k_im = (num_im * a_re - num_re * a_im) / den
    b_re = b_re.astype(jnp.float32)
    b_im = b_im.astype(jnp.float32)
    bb_re = k_re[..., None] * b_re - k_im[..., None] * b_im
    bb_im = k_re[..., None] * b_im + k_im[..., None] * b_re
    return lb_re, lb_im, bb_re, bb_im

def _combine(e1, e2):
    a1r, a1i, b1r, b1i = e1
    a2r, a2i, b2r, b2i = e2
    return (a2r * a1r - a2i * a1i,
            a2r * a1i + a2i * a1r,
            a2r * b1r - a2i * b1i + b2r,
            a2r * b1i + a2i * b1r + b2i)

def ssm_scan(u, disc, h0, reverse):
    lb_re, lb_im, bb_re, bb_im = disc
    bsz, n, _ = u.shape
    ug = u.astype(jnp.float32).reshape(bsz, n, SSM_GROUPS, SSM_GROUP)
    bu_re = jnp.einsum('bngi,gpi->bngp', ug, bb_re)
    bu_im = jnp.einsum('bngi,gpi->bngp', ug, bb_im)
    if h0 is not None:
        h0r, h0i = h0
        idx = n - 1 if reverse else 0
        bu_re = bu_re.at[:, idx].add(lb_re * h0r - lb_im * h0i)
        bu_im = bu_im.at[:, idx].add(lb_re * h0i + lb_im * h0r)
    a_re = jnp.broadcast_to(lb_re, bu_re.shape)
    a_im = jnp.broadcast_to(lb_im, bu_im.shape)
    _, _, h_re, h_im = lax.associative_scan(_combine, (a_re, a_im, bu_re, bu_im), reverse=reverse, axis=1)
    return h_re, h_im

def ssm_readout(h, c_re, c_im):
    h_re, h_im = h
    return (jnp.einsum('bngp,gip->bngi', h_re, c_re.astype(jnp.float32))
            - jnp.einsum('bngp,gip->bngi', h_im, c_im.astype(jnp.float32)))

def ssm_output(u, hf, hb, cf_re, cf_im, cb_re, cb_im, d, w_glu, b_glu):
    bsz, n, _ = u.shape
    y = ssm_readout(hf, cf_re, cf_im) + ssm_readout(hb, cb_re, cb_im)
    y = y.reshape(bsz, n, SSM_W) + d.astype(jnp.float32) * u.astype(jnp.float32)
    y = jax.nn.gelu(y).astype(u.dtype)
    return y * jax.nn.sigmoid(y @ w_glu + b_glu)

def route(h, w_router, b_router):
    t = h.shape[0]
    s = jax.nn.sigmoid(h.astype(jnp.float32) @ w_router.astype(jnp.float32))
    sel = (s + b_router.astype(jnp.float32)).reshape(t, N_EXPERT_GROUPS, EXPERTS_PER_GROUP)
    gscore = lax.top_k(sel, 2)[0].sum(-1)
    gidx = jnp.argmax(gscore, axis=-1)
    gmask = (gidx[:, None] == jnp.arange(N_EXPERT_GROUPS))[:, :, None]
    masked = jnp.where(gmask, sel, -jnp.inf).reshape(t, N_EXPERTS)
    _, eidx = lax.top_k(masked, TOP_K)
    w = jnp.take_along_axis(s, eidx, axis=-1)
    w = w / jnp.sum(w, axis=-1, keepdims=True)
    return eidx, w

def moe(h, eidx, gate, w_gate, w_up, w_down):
    t, d = h.shape
    a = t * TOP_K
    e_flat = eidx.reshape(a)
    tok = jnp.repeat(jnp.arange(t), TOP_K)
    g_flat = gate.reshape(a)
    order = jnp.argsort(e_flat)
    e_s = e_flat[order]
    tok_s = tok[order]
    g_s = g_flat[order]
    counts = jnp.bincount(e_flat, length=N_EXPERTS)
    offs = jnp.cumsum(counts) - counts
    padded = (counts + ROUTE_BLOCK - 1) // ROUTE_BLOCK * ROUTE_BLOCK
    pend = jnp.cumsum(padded)
    pstart = pend - padded
    dest = pstart[e_s] + (jnp.arange(a) - offs[e_s])
    rows = (a + ROUTE_BLOCK - 1) // ROUTE_BLOCK * ROUTE_BLOCK + N_EXPERTS * ROUTE_BLOCK
    nb = rows // ROUTE_BLOCK
    buf = jnp.zeros((rows, d), h.dtype).at[dest].set(h[tok_s])
    blk_e = jnp.minimum(jnp.searchsorted(pend, jnp.arange(nb) * ROUTE_BLOCK, side='right'), N_EXPERTS - 1)

    def expert_block(args):
        xb, e = args
        hid = jax.nn.silu(xb @ w_gate[e]) * (xb @ w_up[e])
        return hid @ w_down[e]

    out = lax.map(expert_block, (buf.reshape(nb, ROUTE_BLOCK, d), blk_e)).reshape(rows, d)
    y = out[dest] * g_s[:, None].astype(out.dtype)
    return jnp.zeros_like(h).at[tok_s].add(y)

def setup_inputs(seed: int = 0) -> dict:
    key = jax.random.key(seed)
    ks = jax.random.split(key, 32)
    nrm = lambda k, shape, s: jax.random.normal(k, shape, jnp.float32) * s
    D = D_MODEL
    G, P, I = SSM_GROUPS, SSM_STATE, SSM_GROUP
    a_im_init = jnp.broadcast_to(math.pi * jnp.arange(P, dtype=jnp.float32), (DEPTH, 2, G, P))
    return {
        "x": nrm(ks[0], (BATCH, SEQ, D), 1.0),
        "c": nrm(ks[1], (BATCH, D), 1.0),
        "ctx": nrm(ks[2], (BATCH, CTX_LEN, D), 1.0),
        "c_ctx": nrm(ks[3], (D,), 1.0),
        "w_mod": nrm(ks[4], (DEPTH, D, N_MOD * D), 0.5 * D ** -0.5),
        "b_mod": nrm(ks[5], (DEPTH, N_MOD * D), 0.02),
        "g_mix": 1.0 + nrm(ks[6], (DEPTH, D), 0.02),
        "g_ffn": 1.0 + nrm(ks[7], (DEPTH, D), 0.02),
        "w_in": nrm(ks[8], (DEPTH, D, MIX_W), D ** -0.5),
        "w_out": nrm(ks[9], (DEPTH, MIX_W, D), MIX_W ** -0.5),
        "w_pool": nrm(ks[10], (DEPTH, POOL_GROUPS, POOL_GW, POOL_GW), POOL_GW ** -0.5),
        "s_pool": 1.0 + nrm(ks[11], (DEPTH, POOL_W), 0.02),
        "ssm_a_re": -0.5 + nrm(ks[12], (DEPTH, 2, G, P), 0.01),
        "ssm_a_im": a_im_init + nrm(ks[13], (DEPTH, 2, G, P), 0.01),
        "ssm_log_dt": jax.random.uniform(ks[14], (DEPTH, 2, G), jnp.float32, math.log(DT_MIN), math.log(DT_MAX)),
        "ssm_b_re": nrm(ks[15], (DEPTH, 2, G, P, I), (2 * I) ** -0.5),
        "ssm_b_im": nrm(ks[16], (DEPTH, 2, G, P, I), (2 * I) ** -0.5),
        "ssm_c_re": nrm(ks[17], (DEPTH, 2, G, I, P), (2 * P) ** -0.5),
        "ssm_c_im": nrm(ks[18], (DEPTH, 2, G, I, P), (2 * P) ** -0.5),
        "ssm_d": nrm(ks[19], (DEPTH, SSM_W), 1.0),
        "w_glu": nrm(ks[20], (DEPTH, SSM_W, SSM_W), SSM_W ** -0.5),
        "b_glu": nrm(ks[21], (DEPTH, SSM_W), 0.02),
        "w_router": nrm(ks[22], (D, N_EXPERTS), D ** -0.5),
        "b_router": nrm(ks[23], (N_EXPERTS,), 0.01),
        "w_gate": nrm(ks[24], (DEPTH, N_EXPERTS, D, D_EXPERT), D ** -0.5),
        "w_up": nrm(ks[25], (DEPTH, N_EXPERTS, D, D_EXPERT), D ** -0.5),
        "w_down": nrm(ks[26], (DEPTH, N_EXPERTS, D_EXPERT, D), D_EXPERT ** -0.5),
        "g_final": 1.0 + nrm(ks[27], (D,), 0.02),
    }

def reference(x, c, ctx, c_ctx, w_mod, b_mod, g_mix, g_ffn, w_in, w_out, w_pool, s_pool,
              ssm_a_re, ssm_a_im, ssm_log_dt, ssm_b_re, ssm_b_im, ssm_c_re, ssm_c_im, ssm_d,
              w_glu, b_glu, w_router, b_router, w_gate, w_up, w_down, g_final):
    bsz, seq_len, d = x.shape
    ctx_len = ctx.shape[1]
    ROWS = seq_len // GRID_W
    cx = ctx
    for l in range(DEPTH):
        last = l == DEPTH - 1
        mod_x = (jax.nn.silu(c) @ w_mod[l] + b_mod[l])[:, None, :]
        mod_c = jax.nn.silu(c_ctx) @ w_mod[l] + b_mod[l]
        x_sh1, x_sc1, x_g1, x_sh2, x_sc2, x_g2 = jnp.split(mod_x, N_MOD, axis=-1)
        c_sh1, c_sc1, c_g1, c_sh2, c_sc2, c_g2 = jnp.split(mod_c, N_MOD, axis=-1)

        hx = modulate(rmsnorm(x, g_mix[l]), x_sh1, x_sc1)
        hc = modulate(rmsnorm(cx, g_mix[l]), c_sh1, c_sc1)
        ux = hx @ w_in[l]
        uc = hc @ (w_in[l][:, POOL_W:] if last else w_in[l])
        ux_ssm = ux[..., POOL_W:]
        uc_ssm = uc[..., -SSM_W:]
        disc_f = ssm_discretise(ssm_a_re[l, 0], ssm_a_im[l, 0], ssm_log_dt[l, 0], ssm_b_re[l, 0], ssm_b_im[l, 0])
        disc_b = ssm_discretise(ssm_a_re[l, 1], ssm_a_im[l, 1], ssm_log_dt[l, 1], ssm_b_re[l, 1], ssm_b_im[l, 1])
        hcf = ssm_scan(uc_ssm, disc_f, None, False)
        hcb = ssm_scan(uc_ssm, disc_b, None, True)
        hxf = ssm_scan(ux_ssm, disc_f, (hcf[0][:, -1], hcf[1][:, -1]), False)
        hxb = ssm_scan(ux_ssm, disc_b, (hcb[0][:, 0], hcb[1][:, 0]), True)
        ssm_x = ssm_output(ux_ssm, hxf, hxb, ssm_c_re[l, 0], ssm_c_im[l, 0], ssm_c_re[l, 1], ssm_c_im[l, 1],
                           ssm_d[l], w_glu[l], b_glu[l])
        pool_x = pool_mixer(ux[..., :POOL_W].reshape(bsz, ROWS, GRID_W, POOL_W), w_pool[l], s_pool[l])
        pool_x = pool_x.reshape(bsz, seq_len, POOL_W)
        x = x + x_g1 * (jnp.concatenate([pool_x, ssm_x], axis=-1) @ w_out[l])
        if not last:
            ssm_cc = ssm_output(uc_ssm, hcf, hcb, ssm_c_re[l, 0], ssm_c_im[l, 0], ssm_c_re[l, 1], ssm_c_im[l, 1],
                                ssm_d[l], w_glu[l], b_glu[l])
            pool_cc = pool_mixer(uc[..., :POOL_W], w_pool[l], s_pool[l])
            cx = cx + c_g1 * (jnp.concatenate([pool_cc, ssm_cc], axis=-1) @ w_out[l])

        hx2 = modulate(rmsnorm(x, g_ffn[l]), x_sh2, x_sc2).reshape(bsz * seq_len, d)
        if last:
            tokens = hx2
        else:
            hc2 = modulate(rmsnorm(cx, g_ffn[l]), c_sh2, c_sc2).reshape(bsz * ctx_len, d)
            tokens = jnp.concatenate([hx2, hc2], axis=0)
        eidx, gate = route(tokens, w_router, b_router)
        y = moe(tokens, eidx, gate, w_gate[l], w_up[l], w_down[l])
        x = x + x_g2 * y[:bsz * seq_len].reshape(bsz, seq_len, d)
        if not last:
            cx = cx + c_g2 * y[bsz * seq_len:].reshape(bsz, ctx_len, d)
    return rmsnorm(x, g_final)


_drawn_inputs = setup_inputs


def setup_inputs(seed=0):
    import zlib

    import numpy as np

    out = dict(_drawn_inputs(seed))
    spreads = {}
    factors = {'ctx': 47.864,
     'c_ctx': 29.344,
     'g_mix': 3.061,
     's_pool': 3.651,
     'ssm_a_re': 62.56,
     'ssm_a_im': 19.977,
     'ssm_log_dt': 27.597,
     'ssm_b_re': 24.272,
     'ssm_b_im': 29.68,
     'ssm_c_re': 58.885,
     'ssm_c_im': 23.416,
     'b_glu': 46.817,
     'g_final': 9.646,
     'g_ffn': 4.044}
    for name, (base, spread) in spreads.items():
        noise = np.random.default_rng([zlib.crc32(name.encode()), seed]).standard_normal(out[name].shape)
        drawn = base * np.exp(spread * noise) if base else spread * noise
        out[name] = __import__('jax').numpy.asarray(drawn.astype(out[name].dtype))
    for name, factor in factors.items():
        out[name] = (out[name] * factor).astype(out[name].dtype)
    return out
```

```python
from contextlib import ExitStack

import numpy as np
import concourse.bass as bass
from concourse import mybir

ALU = mybir.AluOpType
ACT = mybir.ActivationFunctionType
AX = mybir.AxisListType
F32 = mybir.dt.float32
I32 = mybir.dt.int32

P = 128
GRID = 64
WINDOWS = (2, 4, 8, 16)
L = 8
SG = 16
SLOTS = 64
BIG = 65536.0
HUGE = 1e30
EPS = 1e-6
MAGIC = 12582912.0
TWO_PI = 6.283185307179586
PI_A = 6.28125
PI_B = float(np.float32(int((TWO_PI - PI_A) * 2 ** 21) / 2 ** 21))
PI_C = float(np.float32(TWO_PI - PI_A - PI_B))

C_ID, C_UP, C_ONE, C_IOTA, C_CNT = 0, 128, 256, 384, 512
C_COLS = 512 + 4 * GRID
V_C, V_CC, V_GM, V_GF, V_SP, V_D, V_BG = 0, 8, 16, 24, 32, 36, 40
V_ROWS = 44


def shape_constants():
    k = np.zeros((P, C_COLS), np.float32)
    k[:, C_ID:C_ID + P] = np.eye(P)
    k[:, C_UP:C_UP + P] = np.triu(np.ones((P, P)), 1)
    k[:, C_ONE:C_ONE + P] = 1.0
    k[:, C_IOTA:C_IOTA + 2 * SLOTS] = np.arange(2 * SLOTS) % SLOTS
    t = np.arange(GRID)
    for g, w in enumerate(WINDOWS):
        k[:, C_CNT + g * GRID:C_CNT + (g + 1) * GRID] = 1.0 / (np.minimum(t + w // 2, GRID) - np.maximum(t - w // 2, 0))
    return k


def hybrid_block(nc, x, c, ctx, c_ctx, w_mod, b_mod, g_mix, g_ffn, w_in, w_out, w_pool, s_pool,
                 a_re, a_im, log_dt, b_re, b_im, c_re, c_im, ssm_d, w_glu, b_glu, w_router, b_router,
                 w_gate, w_up, w_down, g_final, consts, out):
    D = x.shape[2]
    KD = D // P
    T = x.shape[1]
    NT = T // P
    NE = w_router.shape[1]
    NGRP = 4
    EPG = NE // NGRP
    F = w_gate.shape[3]
    FC = F // P
    NC = T // L
    DG = 32
    GP = 16

    with ExitStack() as stack:
        def sb(name, floats, dt=F32):
            return stack.enter_context(nc.sbuf_tensor(name, [P, floats], dt))

        sems = {}

        def S(name):
            if name not in sems:
                sems[name] = stack.enter_context(nc.semaphore(name))
            return sems[name]

        wts = sb("wts", 2 * 12288)
        ra = sb("ra", 8192)
        rc = sb("rc", 8192)
        cb = sb("cb", 4096)
        ut = sb("ut", 2048)
        r2 = sb("r2", 2048)
        mr = sb("mr", 1536)
        cst = sb("cst", C_COLS)
        vt = sb("vt", V_ROWS)
        mcol = sb("mcol", 96)
        lam = sb("lam", 9 * 64)
        pws = sb("pws", 512)
        sil = sb("sil", KD * 32)
        aux = sb("aux", 160)
        small = sb("small", 48)
        npair = sb("npair", 2, I32)
        ms, rstd, mhalf = small[:, 0:4], small[:, 4:8], small[:, 8:9]
        ms2, rstd2 = small[:, 12:16], small[:, 16:20]
        ps = stack.enter_context(nc.psum_tensor("ps", [P, 8, 512], F32))

        ident = cst[:, C_ID:C_ID + P]
        upper = cst[:, C_UP:C_UP + P]
        ones = cst[:, C_ONE:C_ONE + P]
        iota = cst[:, C_IOTA:C_IOTA + 2 * SLOTS]

        wm = [wts[:, 0:2048], wts[:, 2048:4096], r2[:, :]]
        ST = wts[:, 4096:12288].rearrange("p (d r g m) -> p d r g m", d=2, r=2, g=GP)
        WB = wts[:, 12288:12288 + 8192].rearrange("p (k n) -> p k n", k=KD)
        TT = wts[:, 20480:24576].rearrange("p (t n) -> p t n", t=L)
        scr = 4096
        tA = wts[:, scr:scr + 1024]
        tB = wts[:, scr + 1024:scr + 2048]
        E = wts[:, scr + 2048:scr + 2048 + 17 * 64]
        wglu = wts[:, scr + 3200:scr + 5248].rearrange("p (k n) -> p k n", k=4)
        cat = wts[:, scr + 5248:scr + 7296].rearrange("p (k t) -> p k t", k=KD)
        wpool = wts[:, scr + 7296:scr + 7808].rearrange("p (g n) -> p g n", g=4)

        xc = ra[:, 0:4096].rearrange("p (t d) -> p t d", t=4)
        hT = ra[:, 4096:8192].rearrange("p (k t) -> p k t", k=KD)
        U8 = ra[:, 0:2048].rearrange("p (g q h c) -> p g q h c", g=8, q=4, h=2)
        SS = ra[:, 2048:6144]
        HP = ra[:, 6144:8192].rearrange("p (r g c) -> p r g c", r=2, g=DG)

        SA = rc[:, :].rearrange("p (d r g s j) -> p d r g s j", d=2, r=2, g=GP, s=L)
        MO = rc[:, :].rearrange("p (d r g n) -> p d r g n", d=2, r=2, g=GP)
        Br = cb[:, 0:1024].rearrange("p (d r g j) -> p d r g j", d=2, r=2, g=GP)
        CT = cb[:, 1024:2048].rearrange("p (d r g j) -> p d r g j", d=2, r=2, g=GP)
        CB = cb[:, 2048:4096].rearrange("p (d r g j) -> p d r g j", d=2, r=2, g=GP)
        PADW = GRID + 16
        pad = [cb[:, i * 1280:(i + 1) * 1280].rearrange("p (g r t) -> p g r t", g=4, r=4) for i in range(2)]
        pT = cb[:, 2560:3584].rearrange("p (g t) -> p g t", g=4)
        Craw = wts[:, 21504:23552].rearrange("p (d r q n) -> p d r q n", d=2, r=2, q=4)
        tmpv = ut[:, 1024:2048].rearrange("p (n w) -> p n w", w=32)
        UTs = ut[:, :].rearrange("p (s q h c) -> p s q h c", s=L, q=4, h=2)
        KS = ra[:, 0:1024].rearrange("p (d q s j) -> p d q s j", d=2, q=4, s=L)
        KT = ra[:, 1024:2048].rearrange("p (d n) -> p d n", d=2)
        vrow = wts[:, 20480:20608]
        par_rows = wts[0:DG, 20608:20864].rearrange("p (n m) -> p n m", n=2)
        ldt_rows = wts[0:DG, 20864:20866]
        ldt_x = wts[0:DG, 20868:20996].rearrange("p (a m) -> p a m", a=2)
        modrow = mr[:, :].rearrange("p (r n) -> p r n", r=3)
        LP = lam[:, :].rearrange("p (k r g) -> p k r g", k=9, r=2)
        PW = pws[:, :].rearrange("p (d r g s) -> p d r g s", d=2, r=2, g=GP)
        silc = sil[:, :].rearrange("p (k m) -> p k m", k=KD)
        MC = mcol[:, :].rearrange("p (v k q) -> p v k q", v=6, k=KD)
        wrt = ut[:, 1024:1024 + KD * NE].rearrange("p (k e) -> p k e", k=KD)

        ysb = rc[:, 0:1024]
        ysum = rc[:, 1024:2048].rearrange("p (q t c) -> p q t c", q=4, t=L)
        G = rc[:, 2048:3072].rearrange("p (q t c) -> p q t c", q=4, t=L)
        sg = rc[:, 3072:4096].rearrange("p (q t c) -> p q t c", q=4, t=L)
        g1b = rc[:, 4096:5120]
        g2b = rc[:, 5120:6144]
        gfb = rc[:, 6144:7168]
        x2 = r2[:, :].rearrange("p (t d) -> p t d", t=NT)

        xn2 = ra[:, 0:2048].rearrange("p (t d) -> p t d", t=NT)
        h2T = ra[:, 2048:4096].rearrange("p (k t) -> p k t", k=KD)
        gu = ra[:, 4096:4608]
        xg = ra[:, 4608:5120]
        xm0 = ra[:, 5120:5632].rearrange("p (b h s) -> p b h s", b=4, h=2)
        xm = ra[:, 5632:6144].rearrange("p (b h s) -> p b h s", b=4, h=2)
        silg = ra[:, 6144:6400].rearrange("p (f s) -> p f s", f=FC)
        hid = ra[:, 6400:6656].rearrange("p (f s) -> p f s", f=FC)
        oS = ra[:, 6656:7168]
        Pm = ra[:, 7168:7296].rearrange("p (t s) -> p t s", t=NT)
        PG = ra[:, 7296:7552].rearrange("p (t s) -> p t s", t=NT)
        PTg = cb[:, 0:1024].rearrange("p (b h t) -> p b h t", b=2, h=2)
        rt = cb[:, 2048:4096]
        NCOL = 4 * NE + 4
        posx = ut[:, 0:NT * NCOL].rearrange("p (t e) -> p t e", t=NT)
        wx = ut[:, 512:512 + NT * NCOL].rearrange("p (t e) -> p t e", t=NT)
        A1 = aux[:, 0:16].rearrange("p (k q) -> p k q", q=2)
        A2, sh2 = aux[:, 16:24], aux[:, 24:32]
        tmp32 = [aux[:, 32 + 32 * n:64 + 32 * n] for n in range(4)]
        CBv = cb[:, 2048:4096].rearrange("p (d r g m) -> p d r g m", d=2, r=2, g=GP)
        SSv = SS.rearrange("p (n w) -> p n w", w=64)
        small_pw = pws
        (T_ARE, T_AIM, T_LDT, T_DT, T_ADT, T_MAG, T_SIN, T_SHF, T_ANG, T_TH, T_K, T_D1, T_D2, T_T1, T_T2, T_KR,
         T_KI) = range(17)

        def tv(n):
            return tmpv[:, n, :]

        brb = rt[:, 0:NE]
        sc = rt[:, 32:96].rearrange("p (t e) -> p t e", t=NT)
        sel = rt[:, 96:160].rearrange("p (t e) -> p t e", t=NT)
        one1 = rt[:, 160:224].rearrange("p (t e) -> p t e", t=NT)
        one2 = rt[:, 224:288].rearrange("p (t e) -> p t e", t=NT)
        msk = rt[:, 288:352].rearrange("p (t e) -> p t e", t=NT)
        gw = rt[:, 352:416].rearrange("p (t e) -> p t e", t=NT)
        top8 = rt[:, 416:480].rearrange("p (t g n) -> p t g n", t=NT, g=NGRP)
        gs = rt[:, 480:488].rearrange("p (t g) -> p t g", t=NT)
        gm = rt[:, 488:496].rearrange("p (t g) -> p t g", t=NT)
        rank = rt[:, 496:528]
        best = rt[:, 528:530]
        pcount = rt[:, 530:531]
        lgT = rt[0:NE, 544:800]
        Wg = [wts[:, 12288 * b:12288 * b + 4096].rearrange("p (k f) -> p k f", k=KD) for b in range(2)]
        Wu = [wts[:, 12288 * b + 4096:12288 * b + 8192].rearrange("p (k f) -> p k f", k=KD) for b in range(2)]
        Wd = [wts[:, 12288 * b + 8192:12288 * b + 12288].rearrange("p (k d) -> p k d", k=FC) for b in range(2)]

        u_dram = nc.dram_tensor("u_scratch", [P, 2048], F32).ap()

        block = stack.enter_context(nc.Block())

        def expert_load(eng, b, e, what):
            if what == "gate":
                eng.dma_start(Wg[b], w_gate[0, e].rearrange("(k p) f -> p k f", p=P)).then_inc(S(f"gate_in{b}"), 16)
            elif what == "up":
                eng.dma_start(Wu[b], w_up[0, e].rearrange("(k p) f -> p k f", p=P)).then_inc(S(f"up_in{b}"), 16)
            else:
                eng.dma_start(Wd[b], w_down[0, e].rearrange("(k p) d -> p k d", p=P)).then_inc(S(f"down_in{b}"), 16)

        @block.sync
        def _(sp):
            sp.dma_start(cst[:, :], consts).then_inc(S("cst_in"), 16)
            xv = [ctx[0, 0:P], ctx[0, P:2 * P], x[0, 0:P], x[0, P:2 * P]]
            for t in range(4):
                sp.dma_start(xc[:, t, :], xv[t]).then_inc(S(f"x_in{t}"), 16)

            def mod_chunk(r, k):
                n = r * KD + k
                if n >= 3:
                    sp.wait_ge(S("mod_used"), n - 2)
                sp.dma_start(wm[n % 3], w_mod[0, k * P:(k + 1) * P, 2048 * r:2048 * (r + 1)]).then_inc(S(f"wmod_in{n % 3}"), 16)

            w_in_v = w_in[0].rearrange("(k p) n -> p k n", p=P)
            for k in range(3):
                mod_chunk(0, k)
            sp.dma_start(WB[:, :, 512:1024], w_in_v[:, :, 512:1024]).then_inc(S("win_ssm_in"), 16)
            for k in range(3, KD):
                mod_chunk(0, k)
            sp.dma_start(WB[:, :, 0:512], w_in_v[:, :, 0:512]).then_inc(S("win_pool_in"), 16)
            for r in (1, 2):
                for k in range(KD):
                    mod_chunk(r, k)
            sp.wait_ge(S("u_pool_mm"), 4)
            sp.dma_start(WB, w_out[0].rearrange("(k p) n -> p k n", p=P)).then_inc(S("wout_in"), 16)
            sp.wait_ge(S("s_mm"), 8)
            sp.dma_start(wpool, w_pool[0].rearrange("g c d -> c g d")).then_inc(S("wpool_in"), 16)
            sp.dma_start(wglu, w_glu[0].rearrange("(k p) n -> p k n", p=P)).then_inc(S("wglu_in"), 16)
            sp.wait_ge(S("mod_used"), 24)
            for t in range(NT):
                sp.dma_start(x2[:, t, :], x[0, t * P:(t + 1) * P]).then_inc(S(f"xres_in{t}"), 16)
            expert_load(sp, 0, 0, "gate")
            sp.wait_ge(S("mix_mm"), 4)
            expert_load(sp, 0, 0, "up")
            expert_load(sp, 0, 0, "down")
            for what in ("gate", "up", "down"):
                expert_load(sp, 1, 1, what)
            sp.wait_ge(S("passes_ready"), 1)
            n2 = sp.value_load(npair[0:1, 0:1], min_val=NE // 2, max_val=2 * NE)
            with sp.Fori(0, n2 - 1) as i:
                for b in range(2):
                    nxt = (2 * i + b + 2) % NE
                    sp.wait_ge(S("gu_mm"), 2 * i + b + 1)
                    expert_load(sp, b, nxt, "gate")
                    expert_load(sp, b, nxt, "up")
                    sp.wait_ge(S("down_mm"), 2 * i + b + 2)
                    expert_load(sp, b, nxt, "down")
            for t in range(2 * NT):
                sp.wait_ge(S("fin_ready"), t + 1)
                tt, h = t // 2, t % 2
                sp.dma_start(out[0, tt * P:(tt + 1) * P, 512 * h:512 * (h + 1)],
                             xn2[:, tt, 512 * h:512 * (h + 1)]).then_inc(S("out_done"), 16)
            sp.wait_ge(S("out_done"), 16 * 2 * NT)

        @block.gpsimd
        def _(gp):
            gp.dma_start(vrow[V_C:V_C + 8, :], c.rearrange("a (k p) -> (a k) p", p=P)).then_inc(S("vec_in"), 16)
            for at, ap1 in ((V_CC, c_ctx), (V_GM, g_mix[0]), (V_GF, g_ffn[0]), (V_SP, s_pool[0]), (V_D, ssm_d[0]),
                            (V_BG, b_glu[0])):
                n = ap1.shape[0] // P
                gp.dma_start(vrow[at:at + n, :], ap1.rearrange("(k p) -> k p", p=P)).then_inc(S("vec_in"), 16)
            for n, src in enumerate((a_re, a_im)):
                gp.dma_start(par_rows[:, n, :], src[0].rearrange("d (g a) p -> (d g) (a p)", a=2)).then_inc(S("par_in"), 16)
            gp.dma_start(ldt_rows, log_dt[0].rearrange("d (g a) -> (d g) a", a=2)).then_inc(S("par_in"), 16)
            for r, src in enumerate((b_re, b_im)):
                for d in range(2):
                    gp.dma_start(Br[:, d, r], src[0, d].rearrange("(g a) p j -> (a p) g j", a=2)).then_inc(S("b_in"), 16)
            for r, src in enumerate((c_re, c_im)):
                for d in range(2):
                    for a in range(2):
                        gp.dma_start(Craw[:, d, r, :, 64 * a:64 * a + 64],
                                     src[0, d].rearrange("(q g) i p -> (g i) q p", q=4)).then_inc(S("c_in"), 16)
            gp.wait_ge(S("modrow_zero"), 1)
            for q in range(2):
                for j in range(4):
                    gp.dma_start(modrow[32 * j + q:32 * j + q + 1, :, :],
                                 b_mod[0].rearrange("(r j n) -> j r n", r=3, j=4)[j:j + 1]).then_inc(S("bmod_in"), 16)

            gp.wait_ge(S("mhalf_set"), 1)
            for t in range(4):
                gp.wait_ge(S("ms_ready"), t + 1)
                gp.tensor_tensor(rstd[:, t:t + 1], ms[:, t:t + 1], mhalf, ALU.pow).then_inc(S("rstd_ready"), 1)

            gp.wait_ge(S("kt_ready"), 2)
            for t in range(L):
                if t:
                    gp.dma_start(TT[0:SG * t, t, :], KT[SG * (L - 1 - t):SG * (L - 1), 0, :]).then_inc(S("toep_in"), 16)
                gp.dma_start(TT[SG * t:P, t, :], KT[0:SG * (L - t), 1, :]).then_inc(S("toep_in"), 16)
            gp.wait_ge(S("toep_in"), 16 * (2 * L - 1))

            gp.wait_ge(S("u_ssm_ev"), 4)
            gp.dma_start(u_dram, ut[:, :]).then_inc(S("u_out"), 16)
            gp.wait_ge(S("u_out"), 16)
            for s in range(L):
                gp.dma_start(ra[SG * s:SG * (s + 1), 0:2048].rearrange("i (g n) -> i g n", g=8),
                             u_dram.rearrange("(g i) (s n) -> s i g n", g=8, s=L)[s]).then_inc(S("u8_in"), 16)

            gp.wait_ge(S("u_pool_ev"), 4)
            reach = ((1, 0), (1, 1), (2, 2), (4, 4))
            span = ((1, 80), (2, 79), (4, 77), (8, 72))
            for i in range(4):
                src, dst = pad[i % 2], pad[1 - i % 2]
                (lo, hi), (a, b) = reach[i], span[i]
                gp.tensor_tensor(dst[:, i:4, :, a:b], src[:, i:4, :, a - lo:b - lo],
                                 src[:, i:4, :, a + hi:b + hi], ALU.add).then_inc(S("win"), 1)
                gp.wait_ge(S("win"), 3 * i + 1)
                cnt = cst[:, C_CNT + i * GRID:C_CNT + (i + 1) * GRID].unsqueeze(1).broadcast_to([P, 4, GRID])
                mid = dst[:, i, :, 8:8 + GRID]
                gp.tensor_tensor(mid, mid, cnt, ALU.mult).then_inc(S("win"), 1)
                gp.wait_ge(S("win"), 3 * i + 2)
                pv = pT[:, i].rearrange("p (r t) -> p r t", r=4)
                gp.tensor_tensor(pv, pv, mid, ALU.add).then_inc(S("win"), 1)
            gp.wait_ge(S("y_mm"), 1)
            gp.dma_start(gfb, g_final.rearrange("(a d) -> a d", a=1).broadcast_to([P, D])).then_inc(S("gf_in"), 16)
            gp.dma_start(brb, b_router.rearrange("(a d) -> a d", a=1).broadcast_to([P, NE])).then_inc(S("br_in"), 16)
            gp.wait_ge(S("ysum_ready"), 4)
            gp.dma_start(wrt, w_router.rearrange("(k p) e -> p k e", p=P)).then_inc(S("wr_in"), 16)
            mh2 = mhalf.broadcast_to([P, 2])
            gp.wait_ge(S("ms2_ready"), 1)
            gp.tensor_tensor(rstd2[:, 0:2], ms2[:, 0:2], mh2, ALU.pow).then_inc(S("rstd2_ready"), 1)
            gp.wait_ge(S("ms2_ready"), 2)
            gp.tensor_tensor(rstd2[:, 2:4], ms2[:, 2:4], mh2, ALU.pow).then_inc(S("rstd2_ready"), 1)

        @block.tensor
        def _(pe):
            pe.wait_ge(S("cst_in"), 16)
            pe.wait_ge(S("vec_in"), 16 * 7)
            pe.transpose(ps[:, 0, 0:V_ROWS], vrow[0:V_ROWS, :], ident[0:V_ROWS, 0:V_ROWS]).then_inc(S("vec_t"), 1)
            pe.wait_ge(S("par_in"), 16 * 3)
            pe.wait_ge(S("ldt_x"), 1)
            for n in range(2):
                pe.transpose(ps[:, 1, 32 * n:32 * n + 32], par_rows[:, n, :], ident[0:DG, 0:DG])
            pe.transpose(ps[:, 1, 64:96], ldt_x.rearrange("p a m -> p (a m)"), ident[0:DG, 0:DG]).then_inc(S("par_t"), 1)
            pe.wait_ge(S("c_in"), 16 * 8)
            pe.wait_ge(S("col_copy"), 1)
            for n in range(4):
                d, r = n // 2, n % 2
                for q in range(4):
                    mm = pe.transpose(ps[:, (0, 1, 5, 6)[n], P * q:P * q + P],
                                      Craw[:, d, r, q, :], ident)
                mm.then_inc(S("c_t"), 1)

            def mod_chunk(r, k, bank):
                n = r * KD + k
                pe.wait_ge(S(f"wmod_in{n % 3}"), 16 * (n // 3 + 1))
                for j in range(4):
                    mm = pe.matmul(ps[32 * j:32 * j + 32, bank, :], silc[:, k, :], wm[n % 3][:, 512 * j:512 * j + 512],
                                   start=(k == 0), stop=(k == KD - 1))
                mm.then_inc(S("mod_used"), 1)

            def mod_turn(r, bank):
                pe.wait_ge(S("modrow"), r + 1)
                for b in range(4):
                    mm = pe.transpose(ps[:, bank, 128 * b:128 * b + 128], modrow[:, r, 128 * b:128 * b + 128], ident)
                mm.then_inc(S("mod_t"), 1)

            pe.wait_ge(S("sil_ready"), 1)
            for k in range(KD):
                mod_chunk(0, k, 4)
            pe.wait_ge(S("ct_copy"), 4)
            mod_turn(0, 0)

            pe.wait_ge(S("xn_ready"), 4)
            for k in range(KD):
                if k == 0:
                    pass
                elif k == 1:
                    pe.wait_ge(S("mod_col"), 1)
                else:
                    pe.wait_ge(S("ht_ready"), 2 * (k - 1))
                for t in range(4):
                    mm = pe.transpose(ps[:, (k + 1) % 2, 128 * t:128 * t + 128], xc[:, t, P * k:P * k + P], ident)
                mm.then_inc(S("x_t"), 1)

            n = 0
            for d in range(2):
                pe.wait_ge(S("sa_ready"), d + 1)
                for r in range(2):
                    for g4 in range(4):
                        if n < 2:
                            pe.wait_ge(S("ht_ready"), 2 * (7 + n))
                        else:
                            pe.wait_ge(S("st_copy"), n - 1)
                        for g in range(4):
                            mm = pe.transpose(ps[:, (n + 1) % 2, 128 * g:128 * g + 128],
                                              SA[:, d, r, 4 * g4 + g].rearrange("p s j -> p (s j)"), ident)
                        mm.then_inc(S("sa_t"), 1)
                        n += 1
            pe.wait_ge(S("cb_ready"), 1)
            for d in range(2):
                for q in range(4):
                    for r in range(2):
                        for g in range(4):
                            mm = pe.matmul(ps[32 * g:32 * g + 32, 5 + d, 128 * q:128 * q + 128], CBv[:, d, r, 4 * q + g, :],
                                           SA[:, d, r, 4 * q + g].rearrange("p s j -> p (s j)"),
                                           start=(r == 0), stop=(r == 1), skip_group_check=True)
                mm.then_inc(S("kk_mm"), 1)
            pe.wait_ge(S("ks_ready"), 2)
            pe.wait_ge(S("st_copy"), 16)
            for d in range(2):
                for q in range(4):
                    mm = pe.transpose(ps[:, d, 128 * q:128 * q + 128], KS[:, d, q].rearrange("p s j -> p (s j)"), ident)
                mm.then_inc(S("kt_t"), 1)

            spare = [(r, k) for r in (1, 2) for k in range(KD)]
            pe.wait_ge(S("kt_ready"), 2)
            pe.wait_ge(S("win_ssm_in"), 16)
            pe.wait_ge(S("ht_ready"), 2 * KD)
            for q in range(4):
                for k in range(KD):
                    mm = pe.matmul(ps[:, 4 + q, :], WB[:, k, 512 + P * q:512 + P * q + P], hT[:, k, :],
                                   start=(k == 0), stop=(k == KD - 1))
                    if k == KD - 1:
                        mm.then_inc(S("u_ssm_mm"), 1)
                    if k % 4 == 3:
                        r_, k_ = spare.pop(0)
                        mod_chunk(r_, k_, r_ - 1)
            pe.wait_ge(S("win_pool_in"), 16)
            for g in range(4):
                pe.wait_ge(S("u_ssm_ev"), g // 2 + 1)
                for k in range(KD):
                    mm = pe.matmul(ps[:, 4 + g // 2, 256 * (g % 2):256 * (g % 2) + 256], WB[:, k, P * g:P * g + P],
                                   hT[:, k, 256:512], start=(k == 0), stop=(k == KD - 1))
                    if k == KD - 1:
                        mm.then_inc(S("u_pool_mm"), 1)
                    if k % 4 == 3:
                        r_, k_ = spare.pop(0)
                        mod_chunk(r_, k_, r_ - 1)

            pe.wait_ge(S("u8_in"), 16 * L)
            n = 0
            for d in range(2):
                for r in range(2):
                    for h in range(2):
                        if n < 2:
                            pe.wait_ge(S("u_pool_ev"), 2 * n + 2)
                        elif n < 4:
                            pe.wait_ge(S("u_ssm_ev"), n + 1)
                        else:
                            pe.wait_ge(S("s_ev"), n - 3)
                        for g in range(8):
                            gpair = 8 * h + g
                            for a in range(2):
                                grp = 2 * gpair + a
                                mm = pe.matmul(ps[64 * a:64 * a + 64, 4 + n % 4, 64 * g:64 * g + 64],
                                               ST[:, d, r, gpair, 64 * a:64 * a + 64],
                                               U8[:, grp % 8, grp // 8].rearrange("p h c -> p (h c)"),
                                               start=True, stop=True, skip_group_check=True)
                        mm.then_inc(S("s_mm"), 1)
                        n += 1

            pe.wait_ge(S("wpool_in"), 16)
            pe.wait_ge(S("win"), 12)
            pe.wait_ge(S("s_ev"), 6)
            for g in range(4):
                mm = pe.matmul(ps[:, 4 + g // 2, 256 * (g % 2):256 * (g % 2) + 256], wpool[:, g, :], pT[:, g, :],
                               start=True, stop=True, skip_group_check=True)
            mm.then_inc(S("pool_mm"), 1)
            pe.wait_ge(S("s_ev"), 8)
            for r in (1, 2):
                mod_turn(r, 5 + r)

            def mix(ks, last):
                for t in range(NT):
                    for h in range(2):
                        for k in ks:
                            mm = pe.matmul(ps[:, 2 * t + h, :], cat[:, k, P * t:P * t + P], WB[:, k, 512 * h:512 * h + 512],
                                           start=(k == 0), stop=(k == KD - 1))
                        if last:
                            mm.then_inc(S("mix_mm"), 1)

            pe.wait_ge(S("wout_in"), 16)
            pe.wait_ge(S("cat_pool"), 1)
            pe.wait_ge(S("modrow"), 3)
            pe.wait_ge(S("mo_ready"), 1)
            mix(range(4), False)

            pe.wait_ge(S("toep_in"), 16 * (2 * L - 1))
            for g in range(8):
                for q in range(4):
                    grp = 8 * q + g
                    pe.matmul(ps[32 * q:32 * q + 32, 4 + g % 2, 128 * (g // 2):128 * (g // 2) + 128], U8[:, g, q, 1, :],
                              TT[:, :, SG * grp:SG * grp + SG], start=(g < 2), stop=False, skip_group_check=True)
            pe.wait_ge(S("hp_ready"), 1)
            for g in range(8):
                for d in range(2):
                    for r in range(2):
                        for q in range(4):
                            grp = 8 * q + g
                            gpair, a = grp // 2, grp % 2
                            mm = pe.matmul(ps[32 * q:32 * q + 32, 4 + g % 2, 128 * (g // 2):128 * (g // 2) + 128],
                                           HP[64 * a:64 * a + 64, r, 16 * d + gpair, :],
                                           MO[64 * a:64 * a + 64, d, r, gpair, :],
                                           start=False, stop=(d == 1 and r == 1), skip_group_check=True)
            mm.then_inc(S("y_mm"), 1)
            pe.wait_ge(S("ysb_ready"), 1)
            pe.wait_ge(S("mod_col"), 3)
            for t in range(L):
                mm = pe.transpose(ps[:, 6 + t // 4, 128 * (t % 4):128 * (t % 4) + 128], ysb[:, P * t:P * t + P], ident)
            mm.then_inc(S("y_t"), 1)

            def spread(v_r, j0):
                for h in range(2):
                    j = j0 + h
                    mm = pe.matmul(ps[:, 4 + h, :], ones[32 * j:32 * j + 1, :], modrow[32 * j:32 * j + 1, v_r, :],
                                   start=True, stop=True)
                mm.then_inc(S("spread_mm"), 1)

            spread(1, 0)
            pe.wait_ge(S("g1_ready"), 1)
            spread(2, 2)
            pe.wait_ge(S("wglu_in"), 16)
            pe.wait_ge(S("gelu"), 1)
            for m in range(4):
                for q in range(4):
                    mm = pe.matmul(ps[:, 6 + m // 2, 256 * (m % 2):256 * (m % 2) + 256], wglu[:, q, P * m:P * m + P],
                                   G[:, q].rearrange("p t c -> p (t c)"), start=(q == 0), stop=(q == 3),
                                   skip_group_check=True)
            mm.then_inc(S("glu_mm"), 1)
            pe.wait_ge(S("cat_ssm"), 4)
            mix(range(4, 8), True)

            pe.wait_ge(S("xn2_ready"), 1)
            pe.wait_ge(S("g2_ready"), 1)
            for k in range(KD):
                for t in range(NT):
                    mm = pe.transpose(ps[:, 4 + k // 2, 256 * (k % 2) + P * t:256 * (k % 2) + P * t + P],
                                      xn2[:, t, P * k:P * k + P], ident)
                mm.then_inc(S("h2_t"), 1)
            pe.wait_ge(S("wr_in"), 16)
            for k in range(KD):
                pe.wait_ge(S("h2_ready"), k + 1)
                mm = pe.matmul(ps[0:NE, 0, 0:T], wrt[:, k, :], h2T[:, k, :], start=(k == 0), stop=(k == KD - 1))
            mm.then_inc(S("logit_mm"), 1)
            pe.wait_ge(S("logit_copy"), 1)
            for t in range(NT):
                mm = pe.transpose(ps[:, 1, NE * t:NE * t + NE], lgT[:, P * t:P * t + P], ident[0:NE, 0:NE])
            mm.then_inc(S("logit_t"), 1)
            pe.wait_ge(S("chosen"), 1)
            pe.matmul(ps[:, 2, 0:NE], upper, msk[:, 0, :], start=True, stop=True, skip_group_check=True)
            pe.matmul(ps[:, 2, NE:2 * NE], upper, msk[:, 1, :], start=True, stop=False, skip_group_check=True)
            pe.matmul(ps[:, 2, NE:2 * NE], ones, msk[:, 0, :], start=False, stop=True, skip_group_check=True)
            pe.matmul(ps[:, 2, 2 * NE:3 * NE], ones, msk[:, 0, :], start=True, stop=False, skip_group_check=True)
            pe.matmul(ps[:, 2, 2 * NE:3 * NE], ones, msk[:, 1, :], start=False, stop=True, skip_group_check=True).then_inc(S("count_mm"), 1)

            def gather():
                for t in range(NT):
                    for h in range(2):
                        mm = pe.matmul(ps[64 * h:64 * h + 64, 5, :], Pm[:, t, :], xn2[:, t, 512 * h:512 * h + 512],
                                       start=(t == 0), stop=(t == NT - 1))
                mm.then_inc(S("gather_mm"), 1)

            def turn_x():
                for b in range(4):
                    mm = pe.transpose(ps[:, 6, P * b:P * b + P], xg[:, P * b:P * b + P], ident)
                mm.then_inc(S("x_turn"), 1)

            def scatter(b):
                for t in range(NT):
                    for h in range(2):
                        mm = pe.matmul(ps[:, 2 * t + h, :], PTg[:, b, h, P * t:P * t + P], oS, start=False, stop=False,
                                       skip_group_check=True)
                mm.then_inc(S("scatter_mm"), 1)

            pe.wait_ge(S("slots"), 1)
            pe.wait_ge(S("h2_ready"), KD)
            gather()
            pe.wait_ge(S("zeroed"), 1)
            pe.wait_ge(S("pos_ready"), 1)
            for n in range(4):
                mm = pe.matmul(ps[:, n, :], PTg[:, 1, n % 2, 0:P], oS, start=True, stop=False, skip_group_check=True)
            mm.then_inc(S("scatter_mm"), 1)
            pe.sem_inc(S("hid_turn"), 1)
            pe.sem_inc(S("down_mm"), 1)
            pe.wait_ge(S("xg_copy"), 1)
            turn_x()
            pe.wait_ge(S("passes_ready"), 1)
            n2 = pe.value_load(npair[0:1, 0:1], min_val=NE // 2, max_val=2 * NE)
            with pe.Fori(0, n2) as i:
                for b in range(2):
                    e = 2 * i + b
                    pe.wait_ge(S(f"gate_in{b}"), 16 * i + 16)
                    pe.wait_ge(S(f"up_in{b}"), 16 * i + 16)
                    pe.wait_ge(S("xm_ready"), e + 1)
                    pe.wait_ge(S("gu_copy"), e + 1)
                    for k in range(KD):
                        pe.matmul(ps[0:64, 4, :], xm[:, k % 4, k // 4, :], Wg[b][:, k, :], start=(k == 0), stop=(k == KD - 1))
                        mm = pe.matmul(ps[64:128, 4, :], xm[:, k % 4, k // 4, :], Wu[b][:, k, :], start=(k == 0), stop=(k == KD - 1))
                    mm.then_inc(S("gu_mm"), 1)
                    for t in range(NT):
                        mm = pe.transpose(ps[:, 6, P * t:P * t + P], PG[:, t, :], ident)
                    mm.then_inc(S("pt_turn"), 1)
                    pe.wait_ge(S("slots"), e + 2)
                    pe.wait_ge(S("xg_copy"), e + 1)
                    gather()
                    pe.wait_ge(S("gu_copy"), e + 2)
                    pe.wait_ge(S("pt_copy"), e + 1)
                    for f in range(FC):
                        mm = pe.transpose(ps[:, 6, P * f:P * f + P], gu[:, P * f:P * f + P], ident)
                    mm.then_inc(S("hid_turn"), 1)
                    pe.wait_ge(S("out_copy"), e + 1)
                    scatter(1 - b)
                    pe.wait_ge(S("xg_copy"), e + 2)
                    pe.wait_ge(S("hid_ready"), e + 2)
                    turn_x()
                    pe.wait_ge(S(f"down_in{b}"), 16 * i + 16)
                    for f in range(FC):
                        for h in range(2):
                            mm = pe.matmul(ps[64 * h:64 * h + 64, 7, :], hid[:, f, :], Wd[b][:, f, 512 * h:512 * h + 512],
                                           start=(f == 0), stop=(f == FC - 1))
                    mm.then_inc(S("down_mm"), 1)
            pe.wait_ge(S("out_copy"), 2 * n2 + 1)
            scatter(1)

        @block.scalar
        def _(act):
            act.wait_ge(S("par_copy"), 1)
            act.activation(tv(T_DT), tv(T_LDT), ACT.Exp).then_inc(S("dt_ready"), 1)
            act.wait_ge(S("adt_ready"), 1)
            act.activation(tv(T_MAG), tv(T_ADT), ACT.Exp).then_inc(S("mag_ready"), 1)
            act.wait_ge(S("ang_ready"), 1)
            act.activation(tv(T_SIN), tv(T_ANG), ACT.Sin)
            act.activation(tv(T_SHF), tv(T_ANG), ACT.Sin, scale=0.5).then_inc(S("sin_ready"), 1)
            act.wait_ge(S("sil_zero"), 1)
            act.wait_ge(S("vec_copy"), 1)
            act.activation(silc[:, :, 0:2].rearrange("p k q -> p q k"), vt[:, V_C:V_C + 16].rearrange("p (q k) -> p q k", q=2),
                           ACT.Silu).then_inc(S("sil_ready"), 1)
            for t in range(4):
                act.wait_ge(S(f"x_in{t}"), 16)
                if t:
                    act.wait_ge(S("ss_ready"), t)
                act.activation(hT[:, 0:2, :], xc[:, t, :].rearrange("p (a b) -> p a b", a=2), ACT.Square, accum_out=ms[:, t:t + 1]).then_inc(S("ss_ready"), 1)
            act.wait_ge(S("a1_ready"), 1)
            for k in range(KD):
                act.wait_ge(S("x_t"), k + 1)
                for q in (1, 0):
                    act.activation(hT[:, k, 256 * (1 - q):256 * (2 - q)], ps[:, (k + 1) % 2, 256 * (1 - q):256 * (2 - q)],
                                   ACT.Identity, bias=MC[:, 0, k, q:q + 1], scale=A1[:, k, q:q + 1]).then_inc(S("ht_ready"), 1)
            for n in range(16):
                act.wait_ge(S("sa_t"), n + 1)
                d, r, g4 = n // 8, n // 4 % 2, n % 4
                act.copy(ST[:, d, r, 4 * g4:4 * g4 + 4, :], ps[:, (n + 1) % 2, :].rearrange("p (g m) -> p g m", g=4)).then_inc(S("st_copy"), 1)
            for d in range(2):
                act.wait_ge(S("kt_t"), d + 1)
                act.copy(KT[:, d, :], ps[:, d, :]).then_inc(S("kt_ready"), 1)
            act.wait_ge(S("mo_ready"), 1)
            for q in range(4):
                act.wait_ge(S("u_ssm_mm"), q + 1)
                for h in range(2):
                    mm = act.copy(UTs[:, :, q, h, :], ps[:, 4 + q, 256 * h:256 * h + 256].rearrange("p (c s) -> p s c", s=L))
                mm.then_inc(S("u_ssm_ev"), 1)
            act.wait_ge(S("pad_zero"), 1)
            for g in range(4):
                act.wait_ge(S("u_pool_mm"), 2 * (g // 2) + 2)
                v = ps[:, 4 + g // 2, 256 * (g % 2):256 * (g % 2) + 256]
                act.copy(pad[0][:, g, :, 8:8 + GRID], v.rearrange("p (r t) -> p r t", r=4))
                act.mul(pT[:, g, :], v, -1.0).then_inc(S("u_pool_ev"), 1)
            for n in range(8):
                act.wait_ge(S("s_mm"), n + 1)
                d, r, h = n // 4, n // 2 % 2, n % 2
                v = ps[:, 4 + n % 4, :].rearrange("p (g n) -> p g n", g=8)
                at = 32 * r + 16 * d + 8 * h
                dst = SSv[:, :, at:at + 8].rearrange("p n g -> p g n")
                if d == 0:
                    mm = act.copy(dst, v)
                else:
                    act.copy(dst[:, :, 0:NC], v[:, :, 0:NC][:, :, ::-1])
                    mm = act.copy(dst[:, :, NC:2 * NC], v[:, :, NC:2 * NC][:, :, ::-1])
                mm.then_inc(S("s_ev"), 1)
            act.wait_ge(S("pool_mm"), 1)
            for g in range(4):
                mm = act.activation(cat[:, g, :], ps[:, 4 + g // 2, 256 * (g % 2):256 * (g % 2) + 256], ACT.Copy,
                                    scale=vt[:, V_SP + g:V_SP + g + 1])
            mm.then_inc(S("cat_pool"), 1)
            act.wait_ge(S("y_mm"), 1)
            for a in range(2):
                mm = act.copy(ysb.rearrange("p (t g a i) -> p a g t i", g=4, a=2, t=L)[:, a],
                              ps[:, 4 + a, :].rearrange("p (g t i) -> p g t i", g=4, t=L))
            mm.then_inc(S("ysb_ready"), 1)
            act.wait_ge(S("spread_mm"), 1)
            act.copy(g1b, ps[:, 4:6, :].rearrange("p a n -> p (a n)")).then_inc(S("g1_ready"), 1)
            act.wait_ge(S("ysum_ready"), 4)
            act.activation(G, ysum, ACT.Gelu_apprx_tanh).then_inc(S("gelu"), 1)
            act.wait_ge(S("spread_mm"), 2)
            act.copy(g2b, ps[:, 4:6, :].rearrange("p a n -> p (a n)")).then_inc(S("g2_ready"), 1)
            act.wait_ge(S("glu_mm"), 1)
            for m in range(4):
                act.activation(sg[:, m], ps[:, 6 + m // 2, 256 * (m % 2):256 * (m % 2) + 256].rearrange("p (t c) -> p t c", t=L),
                               ACT.Sigmoid, bias=vt[:, V_BG + m:V_BG + m + 1]).then_inc(S("sig_ready"), 1)
            for t in range(NT):
                act.wait_ge(S("x2_ready"), t + 1)
                if t:
                    act.wait_ge(S("ss2_ready"), t)
                act.activation(ra[:, 4096:5120], x2[:, t, :], ACT.Square, accum_out=ms2[:, t:t + 1]).then_inc(S("ss2_ready"), 1)
            act.wait_ge(S("a2_ready"), 1)
            for k in range(KD):
                act.wait_ge(S("h2_t"), 2 * (k // 2) + 2)
                act.activation(h2T[:, k, :], ps[:, 4 + k // 2, 256 * (k % 2):256 * (k % 2) + 256], ACT.Identity,
                               bias=MC[:, 3, k, 0:1], scale=A2[:, k:k + 1]).then_inc(S("h2_ready"), 1)
            act.wait_ge(S("logit_mm"), 1)
            act.copy(lgT, ps[0:NE, 0, 0:T]).then_inc(S("logit_copy"), 1)
            act.wait_ge(S("logit_t"), 1)
            act.activation(sc.rearrange("p t e -> p (t e)"), ps[:, 1, 0:2 * NE], ACT.Sigmoid).then_inc(S("score"), 1)
            act.wait_ge(S("gather_mm"), 1)
            act.copy(xg, ps[:, 5, :]).then_inc(S("xg_copy"), 1)
            act.wait_ge(S("passes_ready"), 1)
            n2 = act.value_load(npair[0:1, 0:1], min_val=NE // 2, max_val=2 * NE)
            act.sem_inc(S("gu_copy"), 1)
            act.sem_inc(S("out_copy"), 1)
            with act.Fori(0, n2) as i:
                for b in range(2):
                    e = 2 * i + b
                    act.wait_ge(S("gu_mm"), e + 1)
                    act.wait_ge(S("hid_turn"), e + 1)
                    act.copy(gu, ps[:, 4, :]).then_inc(S("gu_copy"), 1)
                    act.wait_ge(S("pt_turn"), e + 1)
                    act.wait_ge(S("scatter_mm"), e + 1)
                    for h in range(2):
                        mm = act.copy(PTg[64 * h:64 * h + 64, b, h, :], ps[64 * h:64 * h + 64, 6, 0:T])
                    mm.then_inc(S("pt_copy"), 1)
                    act.wait_ge(S("gather_mm"), e + 2)
                    act.wait_ge(S("x_turn"), e + 1)
                    act.copy(xg, ps[:, 5, :]).then_inc(S("xg_copy"), 1)
                    act.wait_ge(S("hid_turn"), e + 2)
                    act.wait_ge(S("hid_ready"), e + 1)
                    act.activation(silg, ps[:, 6, :].rearrange("p (f n) -> p f n", f=FC)[:, :, 0:SLOTS], ACT.Silu).then_inc(S("silg_ready"), 1)
                    act.wait_ge(S("down_mm"), e + 2)
                    act.wait_ge(S("scatter_mm"), e + 2)
                    act.copy(oS, ps[:, 7, :]).then_inc(S("out_copy"), 1)
            for t in range(NT):
                act.wait_ge(S("x3_ready"), t + 1)
                if t:
                    act.wait_ge(S("ss3_ready"), t)
                act.activation(ra[:, 4096:5120], x2[:, t, :], ACT.Square, accum_out=ms2[:, 2 + t:3 + t]).then_inc(S("ss3_ready"), 1)

        @block.vector
        def _(dve):
            chain = [0]

            def link(ins):
                chain[0] += 1
                ins.then_inc(S("dve_link"), 1)
                dve.wait_ge(S("dve_link"), chain[0])

            def tt(o, a, b, op):
                return dve.tensor_tensor(o, a, b, op)

            dve.memset(sil[:, :], 0.0).then_inc(S("sil_zero"), 1)
            dve.memset(mr[:, :], 0.0).then_inc(S("modrow_zero"), 1)
            dve.memset(mhalf, -0.5).then_inc(S("mhalf_set"), 1)
            dve.memset(cb[:, 2048:4096], 0.0).then_inc(S("cb_zero"), 1)
            dve.wait_ge(S("par_in"), 48)
            dve.tensor_copy(ldt_x, ldt_rows.unsqueeze(2).broadcast_to([DG, 2, 64])).then_inc(S("ldt_x"), 1)
            dve.wait_ge(S("vec_t"), 1)
            dve.tensor_copy(vt[:, :], ps[:, 0, 0:V_ROWS]).then_inc(S("vec_copy"), 1)
            dve.wait_ge(S("vec_copy"), 1)
            dve.wait_ge(S("par_t"), 1)
            dve.tensor_copy(tmpv[:, 0:3, :], ps[:, 1, 0:96].rearrange("p (n w) -> p n w", n=3)).then_inc(S("par_copy"), 1)
            dve.wait_ge(S("par_copy"), 1)
            dve.sem_inc(S("col_copy"), 1)
            link(dve.tensor_scalar(tv(T_ARE), tv(T_ARE), -1e-4, None, ALU.min))
            dve.wait_ge(S("dt_ready"), 1)
            tt(tv(T_ADT), tv(T_ARE), tv(T_DT), ALU.mult).then_inc(S("adt_ready"), 1)
            link(tt(tv(T_TH), tv(T_AIM), tv(T_DT), ALU.mult))
            link(dve.tensor_scalar(tv(T_K), tv(T_TH), 1.0 / TWO_PI, MAGIC, ALU.mult, ALU.add))
            link(dve.tensor_scalar(tv(T_K), tv(T_K), -MAGIC, None, ALU.add))
            for part in (PI_A, PI_B, PI_C):
                link(dve.scalar_tensor_tensor(tv(T_TH), tv(T_K), -part, tv(T_TH), ALU.mult, ALU.add))
            dve.tensor_scalar(tv(T_ANG), tv(T_TH), 3.1415925, -3.1415925, ALU.min, ALU.max).then_inc(S("ang_ready"), 1)
            link(tt(tv(T_D1), tv(T_ARE), tv(T_ARE), ALU.mult))
            link(tt(tv(T_D2), tv(T_AIM), tv(T_AIM), ALU.mult))
            link(tt(tv(T_D1), tv(T_D1), tv(T_D2), ALU.add))
            link(dve.reciprocal(tv(T_D1), tv(T_D1)))
            dve.wait_ge(S("mag_ready"), 1)
            dve.wait_ge(S("sin_ready"), 1)
            link(tt(tv(T_D2), tv(T_SHF), tv(T_SHF), ALU.mult))
            link(dve.tensor_scalar(tv(T_D2), tv(T_D2), -2.0, 1.0, ALU.mult, ALU.add))
            link(dve.memset(LP[:, 0, 0, :], 1.0))
            link(dve.memset(LP[:, 0, 1, :], 0.0))
            link(tt(LP[:, 1, 0, :], tv(T_MAG), tv(T_D2), ALU.mult))
            link(tt(LP[:, 1, 1, :], tv(T_MAG), tv(T_SIN), ALU.mult))
            link(dve.tensor_scalar(tv(T_K), LP[:, 1, 0, :], -1.0, None, ALU.add))
            link(tt(tv(T_T1), tv(T_K), tv(T_ARE), ALU.mult))
            link(tt(tv(T_T2), LP[:, 1, 1, :], tv(T_AIM), ALU.mult))
            link(tt(tv(T_T1), tv(T_T1), tv(T_T2), ALU.add))
            link(tt(tv(T_KR), tv(T_T1), tv(T_D1), ALU.mult))
            link(tt(tv(T_T1), LP[:, 1, 1, :], tv(T_ARE), ALU.mult))
            link(tt(tv(T_T2), tv(T_K), tv(T_AIM), ALU.mult))
            link(tt(tv(T_T1), tv(T_T1), tv(T_T2), ALU.subtract))
            link(tt(tv(T_KI), tv(T_T1), tv(T_D1), ALU.mult))
            for lo, n in ((1, 1), (2, 2), (4, 4)):
                a_r, a_i = LP[:, 1:1 + n, 0, :], LP[:, 1:1 + n, 1, :]
                b_r = LP[:, lo, 0, :].unsqueeze(1).broadcast_to([P, n, DG])
                b_i = LP[:, lo, 1, :].unsqueeze(1).broadcast_to([P, n, DG])
                o_r, o_i = LP[:, lo + 1:lo + 1 + n, 0, :], LP[:, lo + 1:lo + 1 + n, 1, :]
                t = ps[:, 2, 0:n * DG].rearrange("p (n g) -> p n g", n=n)
                u = ps[:, 2, 256:256 + n * DG].rearrange("p (n g) -> p n g", n=n)
                tt(o_r, a_r, b_r, ALU.mult)
                tt(o_i, a_r, b_i, ALU.mult)
                tt(t, a_i, b_i, ALU.mult)
                link(tt(u, a_i, b_r, ALU.mult))
                tt(o_r, o_r, t, ALU.subtract)
                link(tt(o_i, o_i, u, ALU.add))
            LPv = LP.rearrange("p k r (d g) -> p d r g k", d=2)
            for r in range(2):
                dve.tensor_copy(PW[:, 0, r], LPv[:, 0, r, :, 0:L][:, :, ::-1])
                link(dve.tensor_copy(PW[:, 1, r], LPv[:, 1, r, :, 0:L]))

            for n in range(4):
                d, r = n // 2, n % 2
                dve.wait_ge(S("c_t"), n + 1)
                v = ps[:, (0, 1, 5, 6)[n], :].rearrange("p (g a i) -> p a g i", g=GP, a=2)
                for a in range(2):
                    mm = dve.tensor_copy(CT[64 * a:64 * a + 64, d, r], v[64 * a:64 * a + 64, a])
                mm.then_inc(S("ct_copy"), 1)
            dve.wait_ge(S("ct_copy"), 4)
            dve.wait_ge(S("cb_zero"), 1)
            for a in range(2):
                for r in range(2):
                    for d in range(2):
                        mm = dve.tensor_scalar(CBv[64 * a:64 * a + 64, d, r, :, 16 * a:16 * a + 16],
                                               CT[64 * a:64 * a + 64, d, r], 1.0 if r == 0 else -1.0, None, ALU.mult)
            mm.then_inc(S("cb_ready"), 1)

            for t in range(4):
                dve.wait_ge(S("ss_ready"), t + 1)
                dve.tensor_scalar(ms[:, t:t + 1], ms[:, t:t + 1], 1.0 / D, EPS, ALU.mult, ALU.add).then_inc(S("ms_ready"), 1)
            for t in range(4):
                dve.wait_ge(S("rstd_ready"), t + 1)
                dve.tensor_scalar(xc[:, t, :], xc[:, t, :], rstd[:, t:t + 1], None, ALU.mult).then_inc(S("xn_ready"), 1)

            dve.wait_ge(S("b_in"), 16 * 4)
            for d in range(2):
                kr = tv(T_KR)[:, 16 * d:16 * d + 16].unsqueeze(2).broadcast_to([P, GP, SG])
                ki = tv(T_KI)[:, 16 * d:16 * d + 16].unsqueeze(2).broadcast_to([P, GP, SG])
                br_, bi_ = Br[:, d, 0], Br[:, d, 1]
                t = ps[:, 2, 0:256].rearrange("p (g j) -> p g j", g=GP)
                u = ps[:, 2, 256:512].rearrange("p (g j) -> p g j", g=GP)
                tt(t, bi_, ki, ALU.mult)
                link(tt(u, br_, ki, ALU.mult))
                tt(br_, br_, kr, ALU.mult)
                link(tt(bi_, bi_, kr, ALU.mult))
                tt(br_, br_, t, ALU.subtract)
                link(tt(bi_, bi_, u, ALU.add))

            def powers_times(dst, pw, m, r, sign_im, done):
                for d in range(2):
                    for rr in r:
                        for h in range(2):
                            g = slice(8 * h, 8 * h + 8)
                            pr = pw[:, d, 0, g].unsqueeze(3).broadcast_to([P, 8, L, SG])
                            pi = pw[:, d, 1, g].unsqueeze(3).broadcast_to([P, 8, L, SG])
                            mr_ = m[:, d, 0, g].unsqueeze(2).broadcast_to([P, 8, L, SG])
                            mi_ = m[:, d, 1, g].unsqueeze(2).broadcast_to([P, 8, L, SG])
                            o = dst[:, d, rr, g]
                            t = ps[:, 2:4, :].rearrange("p a (g s j) -> p (a g) s j", g=4, s=L)
                            if rr == 0:
                                tt(o, pr, mr_, ALU.mult)
                                link(tt(t, pi, mi_, ALU.mult))
                                ins = tt(o, o, t, ALU.subtract)
                            else:
                                tt(o, pr, mi_, ALU.mult)
                                link(tt(t, pi, mr_, ALU.mult))
                                if sign_im > 0:
                                    ins = tt(o, o, t, ALU.add)
                                else:
                                    ins = dve.scalar_tensor_tensor(o.rearrange("p g s j -> p (g s j)"), o.rearrange("p g s j -> p (g s j)"), -1.0,
                                                                   t.rearrange("p g s j -> p (g s j)"), ALU.mult, ALU.subtract)
                            if (rr, h) != (1, 1):
                                link(ins)
                    ins.then_inc(S(done), 1)
                    dve.wait_ge(S(done), d + 1)

            powers_times(SA, PW, Br, (0, 1), 1, "sa_ready")

            def modrow_add(r, bank):
                dve.wait_ge(S("mod_used"), KD * (r + 1))
                if r == 0:
                    dve.wait_ge(S("bmod_in"), 16 * 8)
                tt(modrow[:, r, :], modrow[:, r, :], ps[:, bank, :], ALU.add).then_inc(S("modrow"), 1)

            def mod_columns(r, bank):
                dve.wait_ge(S("mod_t"), r + 1)
                v = ps[:, bank, :].rearrange("p (b j m) -> p b j m", b=4, j=4)[:, :, :, 0:2]
                o = mcol[:, 32 * r:32 * r + 32].rearrange("p (j b q) -> p b j q", j=4, b=4)
                dve.tensor_copy(o, v).then_inc(S("mod_col"), 1)

            modrow_add(0, 4)
            mod_columns(0, 0)
            dve.wait_ge(S("mod_col"), 1)
            for q in range(2):
                ins = dve.scalar_tensor_tensor(A1[:, :, q], MC[:, 1, :, q], 1.0, vt[:, V_GM:V_GM + 8], ALU.add, ALU.mult)
            ins.then_inc(S("a1_ready"), 1)

            dve.wait_ge(S("x_t"), KD)
            for d in range(2):
                dve.wait_ge(S("kk_mm"), d + 1)
                link(dve.tensor_copy(KS[:, d].rearrange("p q s j -> p (q s j)"), ps[:, 5 + d, :]))
                if d == 0:
                    dve.sem_inc(S("ks_ready"), 1)
            tt(KS[:, 1, :, 0, :], KS[:, 1, :, 0, :], KS[:, 0, :, L - 1, :], ALU.add).then_inc(S("ks_ready"), 1)

            for r in range(2):
                dve.tensor_copy(PW[:, 0, r], LPv[:, 0, r, :, 1:L + 1])
                link(dve.tensor_copy(PW[:, 1, r], LPv[:, 1, r, :, 1:L + 1][:, :, ::-1]))
            dve.wait_ge(S("sa_t"), 16)
            powers_times(MO.rearrange("p d r g (s j) -> p d r g s j", s=L), PW, CT, (0, 1), -1, "mo_half")
            dve.wait_ge(S("mo_half"), 2)
            dve.sem_inc(S("mo_ready"), 1)
            dve.memset(cb[:, 0:1280], 0.0).then_inc(S("pad_zero"), 1)
            modrow_add(1, 0)
            modrow_add(2, 1)

            pw_re = [small_pw[:, 128 * k:128 * k + 64] for k in range(4)]
            pw_im = [small_pw[:, 128 * k + 64:128 * k + 128] for k in range(4)]

            dve.wait_ge(S("sa_t"), 16)
            pr, pi = LP[:, 8, 0, :], LP[:, 8, 1, :]
            for k in range(4):
                if k:
                    a_r, a_i = pw_re[k - 1][:, 0:32], pw_im[k - 1][:, 32:64]
                    tt(tmp32[0], a_r, LP[:, 8, 0, :], ALU.mult)
                    tt(tmp32[1], a_i, LP[:, 8, 1, :], ALU.mult)
                    tt(tmp32[2], a_r, LP[:, 8, 1, :], ALU.mult)
                    link(tt(tmp32[3], a_i, LP[:, 8, 0, :], ALU.mult))
                    tt(tmp32[0], tmp32[0], tmp32[1], ALU.subtract)
                    link(tt(tmp32[2], tmp32[2], tmp32[3], ALU.add))
                    pr, pi = tmp32[0], tmp32[2]
                dve.tensor_copy(pw_re[k][:, 0:32], pr)
                dve.tensor_copy(pw_re[k][:, 32:64], pr)
                dve.tensor_scalar(pw_im[k][:, 0:32], pi, -1.0, None, ALU.mult)
                link(dve.tensor_copy(pw_im[k][:, 32:64], pi))

            def pair(v):
                return v.rearrange("p n (r g) -> p n r g", r=2)

            dve.wait_ge(S("s_mm"), 8)
            link(dve.memset(E[:, 0:64], 0.0))
            dve.wait_ge(S("s_ev"), 8)
            S4 = SSv.rearrange("p (b k) w -> p k b w", k=4)
            tAv = tA.rearrange("p (n w) -> p n w", w=64)
            tBv = tB.rearrange("p (n w) -> p n w", w=64)
            for k in range(1, 4):
                prev = S4[:, k - 1]
                pre = pw_re[0].unsqueeze(1).broadcast_to([P, 16, 64])
                for r in range(2):
                    tt(tBv[:, :, 32 * r:32 * r + 32], prev[:, :, 32 * (1 - r):32 * (1 - r) + 32],
                       pw_im[0][:, 32 * r:32 * r + 32].unsqueeze(1).broadcast_to([P, 16, 32]), ALU.mult)
                link(tt(tAv, prev, pre, ALU.mult))
                link(tt(tAv, tAv, S4[:, k], ALU.add))
                link(tt(S4[:, k], tAv, tBv, ALU.add))
            Ev = E.rearrange("p (n w) -> p n w", w=64)
            for n in range(15):
                prev = Ev[:, n]
                tt(tB[:, 0:64].rearrange("p (r g) -> p r g", r=2), prev.rearrange("p (r g) -> p r g", r=2)[:, ::-1, :],
                   pw_im[3].rearrange("p (r g) -> p r g", r=2), ALU.mult)
                link(tt(tA[:, 0:64], prev, pw_re[3], ALU.mult))
                link(tt(tA[:, 0:64], tA[:, 0:64], S4[:, 3, n], ALU.add))
                link(tt(Ev[:, n + 1], tA[:, 0:64], tB[:, 0:64], ALU.add))
            HPv = HP.rearrange("p r g (b k) -> p k b (r g)", k=4)
            HPd = [HP[:, :, 0:16, :].rearrange("p r g (b k) -> p k b r g", k=4),
                   HP[:, :, 16:32, ::-1].rearrange("p r g (b k) -> p k b r g", k=4)]
            x8 = Ev[:, 8:16]
            for k in range(4):
                if k == 0:
                    for d in range(2):
                        ins = dve.tensor_copy(HPd[d][:, 0], pair(x8)[:, :, :, 16 * d:16 * d + 16])
                    continue
                a8, b8 = tAv[:, 0:8], tBv[:, 0:8]
                for r in range(2):
                    tt(b8[:, :, 32 * r:32 * r + 32], x8[:, :, 32 * (1 - r):32 * (1 - r) + 32],
                       pw_im[k - 1][:, 32 * r:32 * r + 32].unsqueeze(1).broadcast_to([P, 8, 32]), ALU.mult)
                link(tt(a8, x8, pw_re[k - 1].unsqueeze(1).broadcast_to([P, 8, 64]), ALU.mult))
                link(tt(a8, a8, S4[:, k - 1, 8:16], ALU.add))
                for d in range(2):
                    ins = tt(HPd[d][:, k], pair(a8)[:, :, :, 16 * d:16 * d + 16], pair(b8)[:, :, :, 16 * d:16 * d + 16], ALU.add)
                if k < 3:
                    link(ins)
            ins.then_inc(S("hp_ready"), 1)

            for r in (1, 2):
                mod_columns(r, 5 + r)
            dve.wait_ge(S("mod_col"), 3)
            dve.scalar_tensor_tensor(A2, MC[:, 4, :, 0], 1.0, vt[:, V_GF:V_GF + 8], ALU.add, ALU.mult).then_inc(S("a2_ready"), 1)
            dve.wait_ge(S("y_t"), 1)
            yv = ps[:, 6:8, :].rearrange("p a (t q c) -> p q (a t) c", t=4, q=4)
            for q in range(4):
                dve.scalar_tensor_tensor(ysum[:, q], UTs[:, :, q, 1, :], vt[:, V_D + q:V_D + q + 1], yv[:, q],
                                         ALU.mult, ALU.add).then_inc(S("ysum_ready"), 1)
            for m in range(4):
                dve.wait_ge(S("sig_ready"), m + 1)
                tt(cat[:, 4 + m, :].rearrange("p (c t) -> p t c", t=L), G[:, m], sg[:, m], ALU.mult).then_inc(S("cat_ssm"), 1)

            dve.wait_ge(S("g1_ready"), 1)
            for t in range(NT):
                dve.wait_ge(S("mix_mm"), 2 * t + 2)
                dve.wait_ge(S(f"xres_in{t}"), 16)
                tmp = ra[:, 5120 + 1024 * t:6144 + 1024 * t]
                link(tt(tmp, ps[:, 2 * t:2 * t + 2, :].rearrange("p a n -> p (a n)"), g1b, ALU.mult))
                tt(x2[:, t, :], x2[:, t, :], tmp, ALU.add).then_inc(S("x2_ready"), 1)
            dve.wait_ge(S("ss2_ready"), 2)
            dve.tensor_scalar(ms2[:, 0:2], ms2[:, 0:2], 1.0 / D, EPS, ALU.mult, ALU.add).then_inc(S("ms2_ready"), 1)
            dve.wait_ge(S("rstd2_ready"), 1)
            dve.wait_ge(S("x2_ready"), 2)
            for t in range(NT):
                ins = dve.tensor_scalar(xn2[:, t, :], x2[:, t, :], rstd2[:, t:t + 1], None, ALU.mult)
            ins.then_inc(S("xn2_ready"), 1)
            dve.memset(PTg, 0.0)
            dve.memset(oS, 0.0).then_inc(S("zeroed"), 1)

            dve.wait_ge(S("br_in"), 16)
            dve.wait_ge(S("score"), 1)
            link(tt(sel, sc, brb.unsqueeze(1).broadcast_to([P, NT, NE]), ALU.add))
            for t in range(NT):
                for g in range(NGRP):
                    ins = dve.max(top8[:, t, g, :], sel[:, t, EPG * g:EPG * g + EPG])
            link(ins)
            link(tt(gs, top8[:, :, :, 0], top8[:, :, :, 1], ALU.add))

            def first_best(dst, score, rank, n):
                link(dve.tensor_reduce(best, score, AX.X, ALU.max))
                link(tt(dst, score, best.unsqueeze(2).broadcast_to([P, NT, n]), ALU.is_equal))
                link(tt(dst, dst, rank.unsqueeze(1).broadcast_to([P, NT, n]), ALU.mult))
                link(dve.tensor_reduce(best, dst, AX.X, ALU.max))
                link(tt(dst, dst, best.unsqueeze(2).broadcast_to([P, NT, n]), ALU.is_equal))

            link(dve.tensor_scalar(rank, iota[:, 0:NE], -1.0, float(NE), ALU.mult, ALU.add))
            first_best(gm, gs, rank[:, 0:NGRP], NGRP)
            gmx = gm.unsqueeze(3).broadcast_to([P, NT, NGRP, EPG])
            sel4 = sel.rearrange("p t (g e) -> p t g e", g=NGRP)
            link(tt(sel4, sel4, gmx, ALU.mult))
            link(dve.tensor_scalar(gm, gm, HUGE, -HUGE, ALU.mult, ALU.add))
            link(tt(sel4, sel4, gmx, ALU.add))
            first_best(one1, sel, rank, NE)
            link(dve.scalar_tensor_tensor(sel.rearrange("p t e -> p (t e)"), one1.rearrange("p t e -> p (t e)"), -HUGE * 4,
                                          sel.rearrange("p t e -> p (t e)"), ALU.mult, ALU.add))
            first_best(one2, sel, rank, NE)
            tt(msk, one1, one2, ALU.add).then_inc(S("chosen"), 1)
            dve.wait_ge(S("chosen"), 1)
            link(tt(gw, msk, sc, ALU.mult))
            link(dve.tensor_reduce(best, gw, AX.X, ALU.add))
            link(dve.reciprocal(best, best))
            link(tt(gw, gw, best.unsqueeze(2).broadcast_to([P, NT, NE]), ALU.mult))
            dve.wait_ge(S("count_mm"), 1)
            link(dve.tensor_scalar(sel, msk, -BIG, BIG, ALU.mult, ALU.add))
            link(tt(sel, sel, ps[:, 2, 0:2 * NE].rearrange("p (t e) -> p t e", t=NT), ALU.add))
            for n in range(4):
                dve.tensor_scalar(posx[:, :, NE * n:NE * n + NE], sel, float(-SLOTS * n), None, ALU.add)
                dve.tensor_copy(wx[:, :, NE * n:NE * n + NE], gw)
            dve.memset(posx[:, :, 4 * NE:NCOL], BIG)
            link(dve.memset(wx[:, :, 4 * NE:NCOL], 0.0))
            link(dve.tensor_reduce(best[:, 0:1], ps[:, 2, 2 * NE:3 * NE], AX.X, ALU.max))
            link(dve.tensor_scalar(best[:, 1:2], best[:, 0:1], float(SLOTS), None, ALU.is_gt))
            for n in (2, 3):
                link(dve.tensor_scalar(pcount, best[:, 0:1], float(SLOTS * n), None, ALU.is_gt))
                link(tt(best[:, 1:2], best[:, 1:2], pcount, ALU.add))
            dve.tensor_scalar(npair[:, 0:1], best[:, 1:2], float(NE // 2), float(NE // 2), ALU.mult, ALU.add).then_inc(S("passes_ready"), 1)

            def slots(col):
                for t in range(NT):
                    dve.tensor_scalar(Pm[:, t, :], iota[:, 0:SLOTS], posx[:, t, col], None, ALU.is_equal)
                    ins = dve.tensor_scalar(PG[:, t, :], iota, posx[:, t, col], wx[:, t, col], ALU.is_equal, ALU.mult)
                ins.then_inc(S("slots"), 1)

            def modulate():
                v = ps[:, 6, :].rearrange("p (b h s) -> p b h s", b=4, h=2)
                a2 = A2.rearrange("p (h b) -> p b h", h=2).unsqueeze(3).broadcast_to([P, 4, 2, SLOTS])
                s2 = sh2.rearrange("p (h b) -> p b h", h=2).unsqueeze(3).broadcast_to([P, 4, 2, SLOTS])
                tt(xm0, v, a2, ALU.mult).then_inc(S("xm0_ready"), 1)
                return s2

            dve.tensor_copy(sh2, MC[:, 3, :, 0]).then_inc(S("pos_ready"), 1)
            dve.wait_ge(S("pos_ready"), 1)
            slots(slice(0, 1))
            dve.wait_ge(S("x_turn"), 1)
            s2 = modulate()
            dve.wait_ge(S("xm0_ready"), 1)
            tt(xm, xm0, s2, ALU.add).then_inc(S("xm_ready"), 1)
            dve.wait_ge(S("passes_ready"), 1)
            n2 = dve.value_load(npair[0:1, 0:1], min_val=NE // 2, max_val=2 * NE)
            dve.sem_inc(S("hid_ready"), 1)
            with dve.Fori(0, n2) as i:
                for b in range(2):
                    e = 2 * i + b
                    dve.wait_ge(S("pt_turn"), e + 1)
                    dve.wait_ge(S("gather_mm"), e + 1)
                    slots(bass.ds(e + 1, 1))
                    dve.wait_ge(S("silg_ready"), e + 1)
                    dve.wait_ge(S("down_mm"), e + 1)
                    tt(hid, silg, ps[:, 6, :].rearrange("p (f n) -> p f n", f=FC)[:, :, SLOTS:2 * SLOTS], ALU.mult).then_inc(S("hid_ready"), 1)
                    dve.wait_ge(S("x_turn"), e + 2)
                    s2 = modulate()
                    dve.wait_ge(S("xm0_ready"), e + 2)
                    dve.wait_ge(S("gu_mm"), e + 1)
                    tt(xm, xm0, s2, ALU.add).then_inc(S("xm_ready"), 1)

            dve.wait_ge(S("scatter_mm"), 2 * n2 + 2)
            dve.wait_ge(S("g2_ready"), 1)
            for t in range(NT):
                tmp = rc[:, 1024 * t:1024 * t + 1024]
                link(tt(tmp, ps[:, 2 * t:2 * t + 2, :].rearrange("p a n -> p (a n)"), g2b, ALU.mult))
                tt(x2[:, t, :], x2[:, t, :], tmp, ALU.add).then_inc(S("x3_ready"), 1)
            dve.wait_ge(S("ss3_ready"), 2)
            dve.tensor_scalar(ms2[:, 2:4], ms2[:, 2:4], 1.0 / D, EPS, ALU.mult, ALU.add).then_inc(S("ms2_ready"), 1)
            dve.wait_ge(S("rstd2_ready"), 2)
            dve.wait_ge(S("gf_in"), 16)
            dve.wait_ge(S("x3_ready"), 2)
            for t in range(NT):
                for h in range(2):
                    c0 = slice(512 * h, 512 * h + 512)
                    dve.scalar_tensor_tensor(xn2[:, t, c0], x2[:, t, c0], rstd2[:, 2 + t:3 + t], gfb[:, c0],
                                             ALU.mult, ALU.mult).then_inc(S("fin_ready"), 1)


_INS = ["x", "c", "ctx", "c_ctx", "w_mod", "b_mod", "g_mix", "g_ffn", "w_in", "w_out", "w_pool", "s_pool",
        "ssm_a_re", "ssm_a_im", "ssm_log_dt", "ssm_b_re", "ssm_b_im", "ssm_c_re", "ssm_c_im", "ssm_d",
        "w_glu", "b_glu", "w_router", "b_router", "w_gate", "w_up", "w_down", "g_final"]


def kernel(**inputs):
    import concourse.bacc as bacc
    from concourse.bass_utils import run_bass_kernel_spmd

    nc = bacc.Bacc("TRN2", target_bir_lowering=False, num_devices=1)
    arrays, args = {}, []
    for name in _INS:
        a = np.ascontiguousarray(inputs[name])
        arrays[f"in_{name}"] = a
        args.append(nc.dram_tensor(f"in_{name}", a.shape, mybir.dt.from_np(a.dtype), kind="ExternalInput").ap())
    arrays["in_constants"] = shape_constants()
    args.append(nc.dram_tensor("in_constants", arrays["in_constants"].shape, F32, kind="ExternalInput").ap())
    shape = inputs["x"].shape
    args.append(nc.dram_tensor("out_x", shape, F32, kind="ExternalOutput").ap())
    hybrid_block(nc, *args)
    r = run_bass_kernel_spmd(nc, [arrays], core_ids=[0])
    return r.results[0]["out_x"]
```

```python
from contextlib import ExitStack

import numpy as np
import concourse.bass as bass
from concourse import mybir

ALU = mybir.AluOpType
ACT = mybir.ActivationFunctionType
AX = mybir.AxisListType
F32 = mybir.dt.float32
I32 = mybir.dt.int32

P = 128
GRID = 64
WINDOWS = (2, 4, 8, 16)
L = 8
SG = 16
SLOTS = 64
BIG = 65536.0
HUGE = 1e30
EPS = 1e-6
MAGIC = 12582912.0
TWO_PI = 6.283185307179586
PI_A = 6.28125
PI_B = float(np.float32(int((TWO_PI - PI_A) * 2 ** 21) / 2 ** 21))
PI_C = float(np.float32(TWO_PI - PI_A - PI_B))

C_ID, C_UP, C_ONE, C_IOTA, C_CNT = 0, 128, 256, 384, 512
C_COLS = 512 + 4 * GRID
V_C, V_CC, V_GM, V_GF, V_SP, V_D, V_BG = 0, 8, 16, 24, 32, 36, 40
V_ROWS = 44


def shape_constants():
    k = np.zeros((P, C_COLS), np.float32)
    k[:, C_ID:C_ID + P] = np.eye(P)
    k[:, C_UP:C_UP + P] = np.triu(np.ones((P, P)), 1)
    k[:, C_ONE:C_ONE + P] = 1.0
    k[:, C_IOTA:C_IOTA + 2 * SLOTS] = np.arange(2 * SLOTS) % SLOTS
    t = np.arange(GRID)
    for g, w in enumerate(WINDOWS):
        k[:, C_CNT + g * GRID:C_CNT + (g + 1) * GRID] = 1.0 / (np.minimum(t + w // 2, GRID) - np.maximum(t - w // 2, 0))
    return k


def hybrid_block(nc, x, c, ctx, c_ctx, w_mod, b_mod, g_mix, g_ffn, w_in, w_out, w_pool, s_pool,
                 a_re, a_im, log_dt, b_re, b_im, c_re, c_im, ssm_d, w_glu, b_glu, w_router, b_router,
                 w_gate, w_up, w_down, g_final, consts, out):
    D = x.shape[2]
    KD = D // P
    T = x.shape[1]
    NT = T // P
    NE = w_router.shape[1]
    NGRP = 4
    EPG = NE // NGRP
    F = w_gate.shape[3]
    FC = F // P
    NC = T // L
    DG = 32
    GP = 16

    with ExitStack() as stack:
        def sb(name, floats, dt=F32):
            return stack.enter_context(nc.sbuf_tensor(name, [P, floats], dt))

        sems = {}

        def S(name):
            if name not in sems:
                sems[name] = stack.enter_context(nc.semaphore(name))
            return sems[name]

        wts = sb("wts", 2 * 12288)
        ra = sb("ra", 8192)
        rc = sb("rc", 8192)
        cb = sb("cb", 4096)
        ut = sb("ut", 2048)
        r2 = sb("r2", 2048)
        mr = sb("mr", 1536)
        cst = sb("cst", C_COLS)
        vt = sb("vt", V_ROWS)
        mcol = sb("mcol", 96)
        lam = sb("lam", 9 * 64)
        pws = sb("pws", 512)
        sil = sb("sil", KD * 32)
        aux = sb("aux", 160)
        small = sb("small", 48)
        npair = sb("npair", 2, I32)
        ms, rstd, mhalf = small[:, 0:4], small[:, 4:8], small[:, 8:9]
        ms2, rstd2 = small[:, 12:16], small[:, 16:20]
        ps = stack.enter_context(nc.psum_tensor("ps", [P, 8, 512], F32))

        ident = cst[:, C_ID:C_ID + P]
        upper = cst[:, C_UP:C_UP + P]
        ones = cst[:, C_ONE:C_ONE + P]
        iota = cst[:, C_IOTA:C_IOTA + 2 * SLOTS]

        wm = [wts[:, 0:2048], wts[:, 2048:4096], r2[:, :]]
        ST = wts[:, 4096:12288].rearrange("p (d r g m) -> p d r g m", d=2, r=2, g=GP)
        WB = wts[:, 12288:12288 + 8192].rearrange("p (k n) -> p k n", k=KD)
        TT = ra[:, 4096:8192].rearrange("p (t n) -> p t n", t=L)
        scr = 4096
        tA = wts[:, scr:scr + 1024]
        tB = wts[:, scr + 1024:scr + 2048]
        E = wts[:, scr + 2048:scr + 2048 + 17 * 64]
        wpool = wts[:, scr + 3136:scr + 3648].rearrange("p (g n) -> p g n", g=4)
        wo_pool = wts[:, scr + 3648:scr + 7744].rearrange("p (k n) -> p k n", k=4)
        wo_ssm = wts[:, 12288:16384].rearrange("p (k n) -> p k n", k=4)
        wglu = wts[:, 16384:18432].rearrange("p (k n) -> p k n", k=4)
        cat = wts[:, 18432:20480].rearrange("p (k t) -> p k t", k=KD)

        xc = ra[:, 0:4096].rearrange("p (t d) -> p t d", t=4)
        hT = ra[:, 4096:8192].rearrange("p (k t) -> p k t", k=KD)
        U8 = ra[:, 0:2048].rearrange("p (g q h c) -> p g q h c", g=8, q=4, h=2)
        SS = wts[:, 20480:24576]
        HP = ra[:, 2048:4096].rearrange("p (r g c) -> p r g c", r=2, g=DG)

        SA = rc[:, :].rearrange("p (d r g s j) -> p d r g s j", d=2, r=2, g=GP, s=L)
        MO = rc[:, :].rearrange("p (d r g n) -> p d r g n", d=2, r=2, g=GP)
        Br = cb[:, 0:1024].rearrange("p (d r g j) -> p d r g j", d=2, r=2, g=GP)
        CT = cb[:, 1024:2048].rearrange("p (d r g j) -> p d r g j", d=2, r=2, g=GP)
        CB = cb[:, 2048:4096].rearrange("p (d r g j) -> p d r g j", d=2, r=2, g=GP)
        PADW = GRID + 16
        pad = [cb[:, i * 1280:(i + 1) * 1280].rearrange("p (g r t) -> p g r t", g=4, r=4) for i in range(2)]
        pT = cb[:, 2560:3584].rearrange("p (g t) -> p g t", g=4)
        Craw = wts[:, 21504:23552].rearrange("p (d r q n) -> p d r q n", d=2, r=2, q=4)
        tmpv = ut[:, 1024:2048].rearrange("p (n w) -> p n w", w=32)
        UTs = ut[:, :].rearrange("p (s q h c) -> p s q h c", s=L, q=4, h=2)
        KS = wts[:, 20480:21504].rearrange("p (d q s j) -> p d q s j", d=2, q=4, s=L)
        KT = ra[:, 2048:3072].rearrange("p (d n) -> p d n", d=2)
        vrow = wts[:, 20480:20608]
        par_rows = wts[0:DG, 20608:20864].rearrange("p (n m) -> p n m", n=2)
        ldt_rows = wts[0:DG, 20864:20866]
        ldt_x = wts[0:DG, 20868:20996].rearrange("p (a m) -> p a m", a=2)
        modrow = mr[:, :].rearrange("p (r n) -> p r n", r=3)
        LP = lam[:, :].rearrange("p (k r g) -> p k r g", k=9, r=2)
        PW = pws[:, :].rearrange("p (d r g s) -> p d r g s", d=2, r=2, g=GP)
        silc = sil[:, :].rearrange("p (k m) -> p k m", k=KD)
        MC = mcol[:, :].rearrange("p (v k q) -> p v k q", v=6, k=KD)
        wrt = ut[:, 1024:1024 + KD * NE].rearrange("p (k e) -> p k e", k=KD)

        ysb = rc[:, 0:1024]
        ysum = rc[:, 1024:2048].rearrange("p (q t c) -> p q t c", q=4, t=L)
        G = rc[:, 2048:3072].rearrange("p (q t c) -> p q t c", q=4, t=L)
        sg = rc[:, 3072:4096].rearrange("p (q t c) -> p q t c", q=4, t=L)
        g1b = rc[:, 4096:5120]
        g2b = rc[:, 5120:6144]
        gfb = rc[:, 6144:7168]
        x2 = r2[:, :].rearrange("p (t d) -> p t d", t=NT)

        xn2 = ra[:, 0:2048].rearrange("p (t d) -> p t d", t=NT)
        h2T = ra[:, 2048:4096].rearrange("p (k t) -> p k t", k=KD)
        gu = ra[:, 4096:5120].rearrange("p (b f) -> p b f", b=2)
        xg = ra[:, 5120:6144]
        xm = ra[:, 6144:7168].rearrange("p (k s) -> p k s", k=KD)
        hid = ra[:, 7168:7680].rearrange("p (b f s) -> p b f s", b=2, f=FC)
        silg = ra[:, 7680:8192].rearrange("p (b f s) -> p b f s", b=2, f=FC)
        PT = cb[:, 0:256]
        oS = cb[:, 256:1280]
        Pm = cb[:, 1280:1536].rearrange("p (t b s) -> p t b s", t=NT, b=2)
        PG = cb[:, 1536:1792].rearrange("p (t b s) -> p t b s", t=NT, b=2)
        rt = cb[:, 2048:4096]
        NCOL = 4 * NE + 4
        posx = ut[:, 0:NT * NCOL].rearrange("p (t e) -> p t e", t=NT)
        wx = ut[:, 512:512 + NT * NCOL].rearrange("p (t e) -> p t e", t=NT)
        A1 = aux[:, 0:16].rearrange("p (k q) -> p k q", q=2)
        A2, sh2 = aux[:, 16:24], aux[:, 24:32]
        tmp32 = [aux[:, 32 + 32 * n:64 + 32 * n] for n in range(4)]
        CBv = cb[:, 2048:4096].rearrange("p (d r g m) -> p d r g m", d=2, r=2, g=GP)
        SSv = SS.rearrange("p (n w) -> p n w", w=64)
        small_pw = pws
        (T_ARE, T_AIM, T_LDT, T_DT, T_ADT, T_MAG, T_SIN, T_SHF, T_ANG, T_TH, T_K, T_D1, T_D2, T_T1, T_T2, T_KR,
         T_KI) = range(17)

        def tv(n):
            return tmpv[:, n, :]

        brb = rt[:, 0:NE]
        sc = rt[:, 32:96].rearrange("p (t e) -> p t e", t=NT)
        sel = rt[:, 96:160].rearrange("p (t e) -> p t e", t=NT)
        one1 = rt[:, 160:224].rearrange("p (t e) -> p t e", t=NT)
        one2 = rt[:, 224:288].rearrange("p (t e) -> p t e", t=NT)
        msk = rt[:, 288:352].rearrange("p (t e) -> p t e", t=NT)
        gw = rt[:, 352:416].rearrange("p (t e) -> p t e", t=NT)
        top8 = rt[:, 416:480].rearrange("p (t g n) -> p t g n", t=NT, g=NGRP)
        gs = rt[:, 480:488].rearrange("p (t g) -> p t g", t=NT)
        gm = rt[:, 488:496].rearrange("p (t g) -> p t g", t=NT)
        rank = rt[:, 496:528]
        best = rt[:, 528:530]
        pcount = rt[:, 530:531]
        lgT = rt[0:NE, 544:800]
        Wg = [wts[:, 12288 * b:12288 * b + 4096].rearrange("p (k f) -> p k f", k=KD) for b in range(2)]
        Wu = [wts[:, 12288 * b + 4096:12288 * b + 8192].rearrange("p (k f) -> p k f", k=KD) for b in range(2)]
        Wd = [wts[:, 12288 * b + 8192:12288 * b + 12288].rearrange("p (k d) -> p k d", k=FC) for b in range(2)]

        u_dram = nc.dram_tensor("u_scratch", [P, 2048], F32).ap()

        block = stack.enter_context(nc.Block())

        def expert_load(eng, b, e, what):
            if what == "gate":
                eng.dma_start(Wg[b], w_gate[0, e].rearrange("(k p) f -> p k f", p=P)).then_inc(S(f"gate_in{b}"), 16)
            elif what == "up":
                eng.dma_start(Wu[b], w_up[0, e].rearrange("(k p) f -> p k f", p=P)).then_inc(S(f"up_in{b}"), 16)
            else:
                eng.dma_start(Wd[b], w_down[0, e].rearrange("(k p) d -> p k d", p=P)).then_inc(S(f"down_in{b}"), 16)

        @block.sync
        def _(sp):
            sp.dma_start(vrow[V_C:V_C + 8, :], c.rearrange("a (k p) -> (a k) p", p=P)).then_inc(S("vec_in"), 16)
            sp.dma_start(vrow[V_CC:V_CC + 8, :], c_ctx.rearrange("(k p) -> k p", p=P)).then_inc(S("vec_in"), 16)
            for n, src in enumerate((a_re, a_im)):
                sp.dma_start(par_rows[:, n, :], src[0].rearrange("d (g a) p -> (d g) (a p)", a=2)).then_inc(S("par_in"), 16)
            sp.dma_start(ldt_rows, log_dt[0].rearrange("d (g a) -> (d g) a", a=2)).then_inc(S("par_in"), 16)
            sp.dma_start(cst[:, :], consts).then_inc(S("cst_in"), 16)
            for at, ap1 in ((V_GM, g_mix[0]), (V_GF, g_ffn[0]), (V_SP, s_pool[0]), (V_D, ssm_d[0]), (V_BG, b_glu[0])):
                n = ap1.shape[0] // P
                sp.dma_start(vrow[at:at + n, :], ap1.rearrange("(k p) -> k p", p=P)).then_inc(S("vec_in"), 16)

            def mod_chunk(r, k):
                n = r * KD + k
                if n >= 3:
                    sp.wait_ge(S("mod_used"), n - 2)
                sp.dma_start(wm[n % 3], w_mod[0, k * P:(k + 1) * P, 2048 * r:2048 * (r + 1)]).then_inc(S(f"wmod_in{n % 3}"), 16)

            w_in_v = w_in[0].rearrange("(k p) n -> p k n", p=P)
            for k in range(3):
                mod_chunk(0, k)
            xv = [ctx[0, 0:P], ctx[0, P:2 * P], x[0, 0:P], x[0, P:2 * P]]
            for t in range(4):
                sp.dma_start(xc[:, t, :], xv[t]).then_inc(S(f"x_in{t}"), 16)
            for k in range(3, KD):
                mod_chunk(0, k)
            sp.dma_start(WB[:, :, 512:1024], w_in_v[:, :, 512:1024]).then_inc(S("win_ssm_in"), 16)
            sp.dma_start(WB[:, :, 0:512], w_in_v[:, :, 0:512]).then_inc(S("win_pool_in"), 16)
            for k in range(3):
                mod_chunk(1, k)
            sp.wait_ge(S("u_out"), 16 * 4)
            for s in range(L):
                sp.dma_start(ra[SG * s:SG * (s + 1), 0:2048].rearrange("i (g n) -> i g n", g=8),
                             u_dram.rearrange("(g i) (s n) -> s i g n", g=8, s=L)[s]).then_inc(S("u8_in"), 16)
            sp.wait_ge(S("s_mm"), 8)
            w_out_v = w_out[0].rearrange("(k p) n -> p k n", p=P)
            sp.dma_start(wpool, w_pool[0].rearrange("g c d -> c g d")).then_inc(S("wpool_in"), 16)
            sp.dma_start(wo_pool, w_out_v[:, 0:4, :]).then_inc(S("wo_pool_in"), 16)
            sp.wait_ge(S("u_pool_mm"), 4)
            sp.wait_ge(S("kt_ready"), 2)
            for t in range(L):
                if t:
                    sp.dma_start(TT[0:SG * t, t, :], KT[SG * (L - 1 - t):SG * (L - 1), 0, :]).then_inc(S("toep_in"), 16)
                sp.dma_start(TT[SG * t:P, t, :], KT[0:SG * (L - t), 1, :]).then_inc(S("toep_in"), 16)
            for k in range(3, KD):
                mod_chunk(1, k)
            sp.dma_start(wglu, w_glu[0].rearrange("(k p) n -> p k n", p=P)).then_inc(S("wglu_in"), 16)
            sp.dma_start(wo_ssm, w_out_v[:, 4:8, :]).then_inc(S("wo_ssm_in"), 16)
            for k in range(3):
                mod_chunk(2, k)
            sp.wait_ge(S("mix_pool"), 1)
            sp.wait_ge(S("hp_ready"), 1)
            expert_load(sp, 0, 0, "up")
            for k in range(3, KD):
                mod_chunk(2, k)
            sp.wait_ge(S("mod_used"), 3 * KD)
            for t in range(NT):
                sp.dma_start(x2[:, t, :], x[0, t * P:(t + 1) * P]).then_inc(S(f"xres_in{t}"), 16)
            expert_load(sp, 0, 0, "gate")
            expert_load(sp, 0, 0, "down")
            expert_load(sp, 1, 1, "down")
            sp.wait_ge(S("mix_mm"), 4)
            expert_load(sp, 1, 1, "gate")
            expert_load(sp, 1, 1, "up")
            sp.wait_ge(S("passes_ready"), 1)
            n2 = sp.value_load(npair[0:1, 0:1], min_val=NE // 2, max_val=2 * NE)
            with sp.Fori(0, n2 - 1) as i:
                for b in range(2):
                    nxt = (2 * i + b + 2) % NE
                    sp.wait_ge(S("gu_mm"), 2 * i + b + 1)
                    expert_load(sp, b, nxt, "gate")
                    expert_load(sp, b, nxt, "up")
                sp.wait_ge(S("down_mm"), 2 * i + 2)
                for b in range(2):
                    expert_load(sp, b, (2 * i + b + 2) % NE, "down")
            for t in range(2 * NT):
                sp.wait_ge(S("fin_ready"), t + 1)
                tt, h = t // 2, t % 2
                sp.dma_start(out[0, tt * P:(tt + 1) * P, 512 * h:512 * (h + 1)],
                             xn2[:, tt, 512 * h:512 * (h + 1)]).then_inc(S("out_done"), 16)
            sp.wait_ge(S("out_done"), 16 * 2 * NT)

        @block.gpsimd
        def _(gp):
            gp.wait_ge(S("modrow_zero"), 1)
            for j in range(4):
                gp.dma_start(modrow[32 * j:32 * j + 1, :, :],
                             b_mod[0].rearrange("(r j n) -> j r n", r=3, j=4)[j:j + 1]).then_inc(S("bmod_in"), 16)

            gp.wait_ge(S("mhalf_set"), 1)
            for t in range(4):
                gp.wait_ge(S("ms_ready"), t + 1)
                gp.tensor_tensor(rstd[:, t:t + 1], ms[:, t:t + 1], mhalf, ALU.pow).then_inc(S("rstd_ready"), 1)

            gp.wait_ge(S("mod_col"), 1)
            gv = vt[:, V_GM:V_GM + 8].unsqueeze(2).broadcast_to([P, KD, 2])
            gp.tensor_tensor(A1, MC[:, 1, :, :], gv, ALU.mult).then_inc(S("a1_part"), 1)
            gp.wait_ge(S("a1_part"), 1)
            gp.tensor_tensor(A1, A1, gv, ALU.add).then_inc(S("a1_ready"), 1)

            gp.wait_ge(S("u_pool_ev"), 4)
            reach = ((1, 0), (1, 1), (2, 2), (4, 4))
            span = ((1, 80), (2, 79), (4, 77), (8, 72))
            for i in range(4):
                src, dst = pad[i % 2], pad[1 - i % 2]
                (lo, hi), (a, b) = reach[i], span[i]
                gp.tensor_tensor(dst[:, i:4, :, a:b], src[:, i:4, :, a - lo:b - lo],
                                 src[:, i:4, :, a + hi:b + hi], ALU.add).then_inc(S("win"), 1)
                gp.wait_ge(S("win"), 3 * i + 1)
                cnt = cst[:, C_CNT + i * GRID:C_CNT + (i + 1) * GRID].unsqueeze(1).broadcast_to([P, 4, GRID])
                mid = dst[:, i, :, 8:8 + GRID]
                gp.tensor_tensor(mid, mid, cnt, ALU.mult).then_inc(S("win"), 1)
                gp.wait_ge(S("win"), 3 * i + 2)
                pv = pT[:, i].rearrange("p (r t) -> p r t", r=4)
                gp.tensor_tensor(pv, pv, mid, ALU.add).then_inc(S("win"), 1)
            gp.wait_ge(S("y_mm"), 1)
            gp.dma_start(gfb, g_final.rearrange("(a d) -> a d", a=1).broadcast_to([P, D])).then_inc(S("gf_in"), 16)
            gp.dma_start(brb, b_router.rearrange("(a d) -> a d", a=1).broadcast_to([P, NE])).then_inc(S("br_in"), 16)
            gp.wait_ge(S("ysum_ready"), 4)
            gp.dma_start(wrt, w_router.rearrange("(k p) e -> p k e", p=P)).then_inc(S("wr_in"), 16)
            mh2 = mhalf.broadcast_to([P, 2])
            gp.wait_ge(S("ms2_ready"), 1)
            gp.tensor_tensor(rstd2[:, 0:2], ms2[:, 0:2], mh2, ALU.pow).then_inc(S("rstd2_ready"), 1)
            gp.wait_ge(S("ms2_ready"), 2)
            gp.tensor_tensor(rstd2[:, 2:4], ms2[:, 2:4], mh2, ALU.pow).then_inc(S("rstd2_ready"), 1)

        @block.tensor
        def _(pe):
            pe.wait_ge(S("cst_in"), 16)
            pe.wait_ge(S("vec_in"), 16 * 7)
            pe.transpose(ps[:, 0, 0:V_ROWS], vrow[0:V_ROWS, :], ident[0:V_ROWS, 0:V_ROWS]).then_inc(S("vec_t"), 1)
            pe.wait_ge(S("par_in"), 16 * 3)
            pe.wait_ge(S("ldt_x"), 1)
            for n in range(2):
                pe.transpose(ps[:, 1, 32 * n:32 * n + 32], par_rows[:, n, :], ident[0:DG, 0:DG])
            pe.transpose(ps[:, 1, 64:96], ldt_x.rearrange("p a m -> p (a m)"), ident[0:DG, 0:DG]).then_inc(S("par_t"), 1)
            pe.wait_ge(S("c_in"), 16 * 8)
            pe.wait_ge(S("col_copy"), 1)
            for n in range(4):
                d, r = n // 2, n % 2
                for q in range(4):
                    mm = pe.transpose(ps[:, (0, 1, 5, 6)[n], P * q:P * q + P],
                                      Craw[:, d, r, q, :], ident)
                mm.then_inc(S("c_t"), 1)

            def mod_chunk(r, k, bank):
                n = r * KD + k
                if k == 0:
                    pe.wait_ge(S("bmod_in"), 16 * 4)
                    for j in range(4):
                        pe.matmul(ps[32 * j:32 * j + 32, bank, :], ident[:, 32 * j:32 * j + 1].broadcast_to([P, 32]),
                                  modrow[:, r, :], start=True, stop=False)
                pe.wait_ge(S(f"wmod_in{n % 3}"), 16 * (n // 3 + 1))
                for j in range(4):
                    mm = pe.matmul(ps[32 * j:32 * j + 32, bank, :], silc[:, k, :], wm[n % 3][:, 512 * j:512 * j + 512],
                                   start=False, stop=(k == KD - 1))
                mm.then_inc(S("mod_used"), 1)

            def mod_turn(r, bank):
                pe.wait_ge(S("modrow"), r + 1)
                for b in range(4):
                    mm = pe.transpose(ps[:, bank, 128 * b:128 * b + 128], modrow[:, r, 128 * b:128 * b + 128], ident)
                mm.then_inc(S("mod_t"), 1)

            pe.wait_ge(S("sil_ready"), 1)
            for k in range(KD):
                mod_chunk(0, k, 4)
            pe.wait_ge(S("ct_copy"), 4)
            mod_turn(0, 0)

            pe.wait_ge(S("xn_ready"), 4)
            for k in range(KD):
                if k == 1:
                    pe.wait_ge(S("mod_col"), 1)
                elif k >= 2:
                    pe.wait_ge(S("ht_ready"), 2 * (k - 1))
                for t in range(4):
                    mm = pe.transpose(ps[:, (k + 1) % 2, 128 * t:128 * t + 128], xc[:, t, P * k:P * k + P], ident)
                mm.then_inc(S("x_t"), 1)

            def turn_sa(d):
                pe.wait_ge(S("sa_ready"), d + 1)
                for r in range(2):
                    for g4 in range(4):
                        n = 8 * d + 4 * r + g4
                        if n < 2:
                            pe.wait_ge(S("ht_ready"), 2 * (7 + n))
                        else:
                            pe.wait_ge(S("st_copy"), n - 1)
                        for g in range(4):
                            mm = pe.transpose(ps[:, (n + 1) % 2, 128 * g:128 * g + 128],
                                              SA[:, d, r, 4 * g4 + g].rearrange("p s j -> p (s j)"), ident)
                        mm.then_inc(S("sa_t"), 1)

            def lag_kernels():
                pe.wait_ge(S("cb_ready"), 1)
                pe.wait_ge(S("st_copy"), 16)
                for d in range(2):
                    for q in range(4):
                        for r in range(2):
                            for g in range(4):
                                mm = pe.matmul(ps[32 * g:32 * g + 32, d, 128 * q:128 * q + 128], CBv[:, d, r, 4 * q + g, :],
                                               SA[:, d, r, 4 * q + g].rearrange("p s j -> p (s j)"),
                                               start=(r == 0), stop=(r == 1), skip_group_check=True)
                    mm.then_inc(S("kk_mm"), 1)

            def turn_kernels():
                pe.wait_ge(S("ks_ready"), 2)
                for d in range(2):
                    for q in range(4):
                        mm = pe.transpose(ps[:, d, 128 * q:128 * q + 128], KS[:, d, q].rearrange("p s j -> p (s j)"), ident)
                    mm.then_inc(S("kt_t"), 1)

            def u_ssm(q):
                for k in range(KD):
                    mm = pe.matmul(ps[:, 4 + q, :], WB[:, k, 512 + P * q:512 + P * q + P], hT[:, k, :],
                                   start=(k == 0), stop=(k == KD - 1))
                mm.then_inc(S("u_ssm_mm"), 1)

            pe.wait_ge(S("ht_ready"), 2 * KD)
            pe.wait_ge(S("win_ssm_in"), 16)
            turn_sa(0)
            u_ssm(0)
            u_ssm(1)
            turn_sa(1)
            lag_kernels()
            u_ssm(2)
            turn_kernels()
            u_ssm(3)
            def u_pool(b):
                for g in (2 * b, 2 * b + 1):
                    for k in range(KD):
                        mm = pe.matmul(ps[:, b, 256 * (g % 2):256 * (g % 2) + 256], WB[:, k, P * g:P * g + P],
                                       hT[:, k, 256:512], start=(k == 0), stop=(k == KD - 1), skip_group_check=True)
                    mm.then_inc(S("u_pool_mm"), 1)

            pe.wait_ge(S("kt_ready"), 2)
            pe.wait_ge(S("win_pool_in"), 16)
            u_pool(0)

            pe.wait_ge(S("st_copy"), 16)
            pe.wait_ge(S("u8_in"), 16 * L)
            n = 0
            for d in range(2):
                for r in range(2):
                    for h in range(2):
                        if n < 4:
                            pe.wait_ge(S("u_ssm_ev"), n + 1)
                        else:
                            pe.wait_ge(S("s_ev"), n - 3)
                        for g in range(8):
                            gpair = 8 * h + g
                            for a in range(2):
                                grp = 2 * gpair + a
                                mm = pe.matmul(ps[64 * a:64 * a + 64, 4 + n % 4, 64 * g:64 * g + 64],
                                               ST[:, d, r, gpair, 64 * a:64 * a + 64],
                                               U8[:, grp % 8, grp // 8].rearrange("p h c -> p (h c)"),
                                               start=True, stop=True, skip_group_check=True)
                        mm.then_inc(S("s_mm"), 1)
                        n += 1

            u_pool(1)
            pe.wait_ge(S("s_ev"), 8)
            for k in range(3):
                mod_chunk(1, k, 6)

            pe.wait_ge(S("toep_in"), 16 * (2 * L - 1))
            for g in range(8):
                for q in range(4):
                    grp = 8 * q + g
                    pe.matmul(ps[32 * q:32 * q + 32, 4 + g % 2, 128 * (g // 2):128 * (g // 2) + 128], U8[:, g, q, 1, :],
                              TT[:, :, SG * grp:SG * grp + SG], start=(g < 2), stop=False, skip_group_check=True)
            mod_chunk(1, 3, 6)
            mod_chunk(1, 4, 6)
            pe.wait_ge(S("wpool_in"), 16)
            pe.wait_ge(S("win"), 12)
            pe.wait_ge(S("mo_ready"), 1)
            for g in range(4):
                mm = pe.matmul(ps[:, 2 + g // 2, 256 * (g % 2):256 * (g % 2) + 256], wpool[:, g, :], pT[:, g, :],
                               start=True, stop=True, skip_group_check=True)
            mm.then_inc(S("pool_mm"), 1)
            for k in range(5, KD):
                mod_chunk(1, k, 6)
            pe.wait_ge(S("wo_pool_in"), 16)
            pe.wait_ge(S("cat_pool"), 1)
            for n in range(4):
                for k in range(4):
                    mm = pe.matmul(ps[:, n, :], cat[:, k, P * (n // 2):P * (n // 2) + P],
                                   wo_pool[:, k, 512 * (n % 2):512 * (n % 2) + 512], start=(k == 0), stop=False)
            mm.then_inc(S("mix_pool"), 1)
            mod_turn(1, 7)

            pe.wait_ge(S("hp_ready"), 1)
            for g in range(8):
                for d in range(2):
                    for r in range(2):
                        for q in range(4):
                            grp = 8 * q + g
                            gpair, a = grp // 2, grp % 2
                            mm = pe.matmul(ps[32 * q:32 * q + 32, 4 + g % 2, 128 * (g // 2):128 * (g // 2) + 128],
                                           HP[64 * a:64 * a + 64, r, 16 * d + gpair, :],
                                           MO[64 * a:64 * a + 64, d, r, gpair, :],
                                           start=False, stop=(d == 1 and r == 1), skip_group_check=True)
            mm.then_inc(S("y_mm"), 1)
            pe.wait_ge(S("ysb_ready"), 1)
            pe.wait_ge(S("mod_col"), 2)
            for t in range(L):
                mm = pe.transpose(ps[:, 6 + t // 4, 128 * (t % 4):128 * (t % 4) + 128], ysb[:, P * t:P * t + P], ident)
            mm.then_inc(S("y_t"), 1)

            def spread(v_r, j0):
                for h in range(2):
                    j = j0 + h
                    mm = pe.matmul(ps[:, 4 + h, :], ones[32 * j:32 * j + 1, :], modrow[32 * j:32 * j + 1, v_r, :],
                                   start=True, stop=True)
                mm.then_inc(S("spread_mm"), 1)

            spread(1, 0)
            pe.wait_ge(S("wglu_in"), 16)
            pe.wait_ge(S("gelu"), 1)
            for m in range(4):
                for q in range(4):
                    mm = pe.matmul(ps[:, 6 + m // 2, 256 * (m % 2):256 * (m % 2) + 256], wglu[:, q, P * m:P * m + P],
                                   G[:, q].rearrange("p t c -> p (t c)"), start=(q == 0), stop=(q == 3),
                                   skip_group_check=True)
            mm.then_inc(S("glu_mm"), 1)
            pe.wait_ge(S("g1_ready"), 1)
            for k in range(3):
                mod_chunk(2, k, 4)
            pe.wait_ge(S("wo_ssm_in"), 16)
            pe.wait_ge(S("cat_ssm"), 4)
            for n in range(4):
                for k in range(4):
                    mm = pe.matmul(ps[:, n, :], cat[:, 4 + k, P * (n // 2):P * (n // 2) + P],
                                   wo_ssm[:, k, 512 * (n % 2):512 * (n % 2) + 512], start=False, stop=(k == 3))
                mm.then_inc(S("mix_mm"), 1)
                mod_chunk(2, 3 + n, 4)
            mod_chunk(2, 7, 4)
            mod_turn(2, 5)

            pe.wait_ge(S("xn2_ready"), 1)
            pe.wait_ge(S("mod_col"), 3)
            for k in range(KD):
                for t in range(NT):
                    mm = pe.transpose(ps[:, 4 + k // 2, 256 * (k % 2) + P * t:256 * (k % 2) + P * t + P],
                                      xn2[:, t, P * k:P * k + P], ident)
                mm.then_inc(S("h2_t"), 1)
            pe.wait_ge(S("wr_in"), 16)
            for k in range(KD):
                pe.wait_ge(S("h2_ready"), k + 1)
                mm = pe.matmul(ps[0:NE, 0, 0:T], wrt[:, k, :], h2T[:, k, :], start=(k == 0), stop=(k == KD - 1))
            mm.then_inc(S("logit_mm"), 1)
            pe.wait_ge(S("logit_copy"), 1)
            for t in range(NT):
                mm = pe.transpose(ps[:, 1, NE * t:NE * t + NE], lgT[:, P * t:P * t + P], ident[0:NE, 0:NE])
            mm.then_inc(S("logit_t"), 1)
            spread(2, 2)
            pe.wait_ge(S("chosen"), 1)
            pe.matmul(ps[:, 2, 0:NE], upper, msk[:, 0, :], start=True, stop=True, skip_group_check=True)
            pe.matmul(ps[:, 2, NE:2 * NE], upper, msk[:, 1, :], start=True, stop=False, skip_group_check=True)
            pe.matmul(ps[:, 2, NE:2 * NE], ones, msk[:, 0, :], start=False, stop=True, skip_group_check=True)
            pe.matmul(ps[:, 2, 2 * NE:3 * NE], ones, msk[:, 0, :], start=True, stop=False, skip_group_check=True)
            pe.matmul(ps[:, 2, 2 * NE:3 * NE], ones, msk[:, 1, :], start=False, stop=True, skip_group_check=True).then_inc(S("count_mm"), 1)

            def gather():
                for h in range(2):
                    for t in range(NT):
                        mm = pe.matmul(ps[:, 6 + h, :], Pm[:, t].rearrange("p b s -> p (b s)"), xn2[:, t, 512 * h:512 * h + 512],
                                       start=(t == 0), stop=(t == NT - 1))
                mm.then_inc(S("gather_mm"), 1)

            def turn_x(h):
                for k in range(4):
                    mm = pe.transpose(ps[:, 6 + h, P * k:P * k + P], xg[:, 512 * h + P * k:512 * h + P * k + P], ident)
                return mm

            def scatter():
                for t in range(NT):
                    for h in range(2):
                        mm = pe.matmul(ps[:, 2 * t + h, :], PT[:, P * t:P * t + P], oS[:, 512 * h:512 * h + 512], start=False,
                                       stop=False, skip_group_check=True)
                mm.then_inc(S("scatter_mm"), 1)

            pe.wait_ge(S("h2_ready"), KD)
            pe.wait_ge(S("slots"), 1)
            gather()
            pe.wait_ge(S("zeroed"), 1)
            pe.wait_ge(S("pos_ready"), 1)
            for n in range(4):
                mm = pe.matmul(ps[:, n, :], PT[:, 0:P], oS[:, 0:512], start=True, stop=False, skip_group_check=True)
            mm.then_inc(S("zero_mm"), 1)
            pe.wait_ge(S("xg_copy"), 1)
            turn_x(0)
            turn_x(1).then_inc(S("x_turn"), 1)
            pe.wait_ge(S("g2_ready"), 1)
            pe.wait_ge(S("passes_ready"), 1)
            n2 = pe.value_load(npair[0:1, 0:1], min_val=NE // 2, max_val=2 * NE)
            with pe.Fori(0, n2) as i:
                for b in range(2):
                    pe.wait_ge(S(f"gate_in{b}"), 16 * i + 16)
                    pe.wait_ge(S(f"up_in{b}"), 16 * i + 16)
                    pe.wait_ge(S("xm_ready"), i + 1)
                    pe.wait_ge(S("out_copy"), 2 * i + b + 1)
                    for k in range(KD):
                        st = xm[:, k, SLOTS * b:SLOTS * b + SLOTS]
                        pe.matmul(ps[0:64, 4 + b, :], st, Wg[b][:, k, :], start=(k == 0), stop=(k == KD - 1))
                        mm = pe.matmul(ps[64:128, 4 + b, :], st, Wu[b][:, k, :], start=(k == 0), stop=(k == KD - 1))
                    mm.then_inc(S("gu_mm"), 1)
                pe.wait_ge(S("slots"), i + 2)
                gather()
                for b in range(2):
                    pe.wait_ge(S("gu_copy"), 2 * i + b + 1)
                    for f in range(FC):
                        mm = pe.transpose(ps[:, 4 + b, P * f:P * f + P], gu[:, b, P * f:P * f + P], ident)
                    mm.then_inc(S("hid_turn"), 1)
                pe.wait_ge(S("pt_copy"), i + 1)
                scatter()
                pe.wait_ge(S("xg_copy"), i + 2)
                for t in range(NT):
                    mm = pe.transpose(ps[:, 6, P * t:P * t + P], PG[:, t].rearrange("p b s -> p (b s)"), ident)
                mm.then_inc(S("pt_turn"), 1)
                turn_x(1)
                pe.wait_ge(S("pt_copy"), i + 2)
                turn_x(0).then_inc(S("x_turn"), 1)
                for b in range(2):
                    pe.wait_ge(S(f"down_in{b}"), 16 * i + 16)
                pe.wait_ge(S("hid_ready"), 2 * i + 2)
                for h in range(2):
                    for f in range(FC):
                        for b in range(2):
                            mm = pe.matmul(ps[64 * b:64 * b + 64, 4 + h, :], hid[:, b, f, :], Wd[b][:, f, 512 * h:512 * h + 512],
                                           start=(f == 0), stop=(f == FC - 1))
                    mm.then_inc(S("down_mm"), 1)
            pe.wait_ge(S("out_copy"), 2 * n2 + 2)
            pe.wait_ge(S("pt_copy"), n2 + 1)
            scatter()

        @block.scalar
        def _(act):
            for r, src in enumerate((c_re, c_im)):
                for d in range(2):
                    for a in range(2):
                        act.dma_start(Craw[:, d, r, :, 64 * a:64 * a + 64],
                                     src[0, d].rearrange("(q g) i p -> (g i) q p", q=4)).then_inc(S("c_in"), 16)
            for r, src in enumerate((b_re, b_im)):
                for d in range(2):
                    act.dma_start(Br[:, d, r], src[0, d].rearrange("(g a) p j -> (a p) g j", a=2)).then_inc(S("b_in"), 16)
            act.wait_ge(S("par_copy"), 1)
            act.activation(tv(T_DT), tv(T_LDT), ACT.Exp).then_inc(S("dt_ready"), 1)
            act.wait_ge(S("adt_ready"), 1)
            act.activation(tv(T_MAG), tv(T_ADT), ACT.Exp).then_inc(S("mag_ready"), 1)
            act.wait_ge(S("ang_ready"), 1)
            act.activation(tv(T_SIN), tv(T_ANG), ACT.Sin)
            act.activation(tv(T_SHF), tv(T_ANG), ACT.Sin, scale=0.5).then_inc(S("sin_ready"), 1)
            act.wait_ge(S("sil_zero"), 1)
            act.wait_ge(S("vec_copy"), 1)
            act.activation(silc[:, :, 0:2].rearrange("p k q -> p q k"), vt[:, V_C:V_C + 16].rearrange("p (q k) -> p q k", q=2),
                           ACT.Silu).then_inc(S("sil_ready"), 1)
            for t in range(4):
                act.wait_ge(S(f"x_in{t}"), 16)
                if t:
                    act.wait_ge(S("ss_ready"), t)
                act.activation(hT[:, 0:2, :], xc[:, t, :].rearrange("p (a b) -> p a b", a=2), ACT.Square, accum_out=ms[:, t:t + 1]).then_inc(S("ss_ready"), 1)
            def mod_evacuate(r, bank, turned):
                act.wait_ge(S("mod_used"), KD * (r + 1))
                act.copy(modrow[:, r, :], ps[:, bank, :]).then_inc(S("modrow"), 1)
                act.wait_ge(S("mod_t"), r + 1)
                v = ps[:, turned, :].rearrange("p (b j m) -> p b j m", b=4, j=4)[:, :, :, 0:2]
                o = mcol[:, 32 * r:32 * r + 32].rearrange("p (j b q) -> p b j q", j=4, b=4)
                act.copy(o, v).then_inc(S("mod_col"), 1)

            mod_evacuate(0, 4, 0)
            act.wait_ge(S("a1_ready"), 1)
            for k in range(KD):
                act.wait_ge(S("x_t"), k + 1)
                for q in (1, 0):
                    act.activation(hT[:, k, 256 * (1 - q):256 * (2 - q)], ps[:, (k + 1) % 2, 256 * (1 - q):256 * (2 - q)],
                                   ACT.Identity, bias=MC[:, 0, k, q:q + 1], scale=A1[:, k, q:q + 1]).then_inc(S("ht_ready"), 1)

            def copy_st(d):
                for n in range(8 * d, 8 * d + 8):
                    act.wait_ge(S("sa_t"), n + 1)
                    act.copy(ST[:, d, n // 4 % 2, 4 * (n % 4):4 * (n % 4) + 4, :],
                             ps[:, (n + 1) % 2, :].rearrange("p (g m) -> p g m", g=4)).then_inc(S("st_copy"), 1)

            def u_evacuate(q):
                act.wait_ge(S("u_ssm_mm"), q + 1)
                for h in range(2):
                    mm = act.copy(UTs[:, :, q, h, :], ps[:, 4 + q, 256 * h:256 * h + 256].rearrange("p (c s) -> p s c", s=L))
                mm.then_inc(S("u_ssm_ev"), 1)
                act.wait_ge(S("u_ssm_ev"), q + 1)
                act.dma_start(u_dram.rearrange("p (s q n) -> p s q n", s=L, q=4)[:, :, q],
                              ut[:, :].rearrange("p (s q n) -> p s q n", s=L, q=4)[:, :, q]).then_inc(S("u_out"), 16)

            act.wait_ge(S("bbar_ready"), 1)
            copy_st(0)
            u_evacuate(0)
            u_evacuate(1)
            copy_st(1)
            u_evacuate(2)
            for d in range(2):
                act.wait_ge(S("kt_t"), d + 1)
                act.copy(KT[:, d, :], ps[:, d, :]).then_inc(S("kt_ready"), 1)
            u_evacuate(3)
            for n in range(8):
                act.wait_ge(S("s_mm"), n + 1)
                d, r, h = n // 4, n // 2 % 2, n % 2
                v = ps[:, 4 + n % 4, :].rearrange("p (g n) -> p g n", g=8)
                at = 32 * r + 16 * d + 8 * h
                dst = SSv[:, :, at:at + 8].rearrange("p n g -> p g n")
                if d == 0:
                    mm = act.copy(dst, v)
                else:
                    act.copy(dst[:, :, 0:NC], v[:, :, 0:NC][:, :, ::-1])
                    mm = act.copy(dst[:, :, NC:2 * NC], v[:, :, NC:2 * NC][:, :, ::-1])
                mm.then_inc(S("s_ev"), 1)
            act.wait_ge(S("pad_zero"), 1)
            for g in range(4):
                act.wait_ge(S("u_pool_mm"), 2 * (g // 2) + 2)
                v = ps[:, g // 2, 256 * (g % 2):256 * (g % 2) + 256]
                act.copy(pad[0][:, g, :, 8:8 + GRID], v.rearrange("p (r t) -> p r t", r=4))
                act.mul(pT[:, g, :], v, -1.0).then_inc(S("u_pool_ev"), 1)
            act.wait_ge(S("pool_mm"), 1)
            for g in range(4):
                mm = act.activation(cat[:, g, :], ps[:, 2 + g // 2, 256 * (g % 2):256 * (g % 2) + 256], ACT.Copy,
                                    scale=vt[:, V_SP + g:V_SP + g + 1])
            mm.then_inc(S("cat_pool"), 1)
            mod_evacuate(1, 6, 7)
            act.wait_ge(S("y_mm"), 1)
            for a in range(2):
                mm = act.copy(ysb.rearrange("p (t g a i) -> p a g t i", g=4, a=2, t=L)[:, a],
                              ps[:, 4 + a, :].rearrange("p (g t i) -> p g t i", g=4, t=L))
            mm.then_inc(S("ysb_ready"), 1)
            act.wait_ge(S("ysum_ready"), 4)
            act.activation(G, ysum, ACT.Gelu_apprx_tanh).then_inc(S("gelu"), 1)
            act.wait_ge(S("spread_mm"), 1)
            act.copy(g1b, ps[:, 4:6, :].rearrange("p a n -> p (a n)")).then_inc(S("g1_ready"), 1)
            act.wait_ge(S("glu_mm"), 1)
            for m in range(4):
                act.activation(sg[:, m], ps[:, 6 + m // 2, 256 * (m % 2):256 * (m % 2) + 256].rearrange("p (t c) -> p t c", t=L),
                               ACT.Sigmoid, bias=vt[:, V_BG + m:V_BG + m + 1]).then_inc(S("sig_ready"), 1)
            mod_evacuate(2, 4, 5)
            for t in range(NT):
                act.wait_ge(S("x2_ready"), t + 1)
                if t:
                    act.wait_ge(S("ss2_ready"), t)
                act.activation(ra[:, 4096:5120], x2[:, t, :], ACT.Square, accum_out=ms2[:, t:t + 1]).then_inc(S("ss2_ready"), 1)
            act.wait_ge(S("a2_ready"), 1)
            for k in range(KD):
                act.wait_ge(S("h2_t"), 2 * (k // 2) + 2)
                act.activation(h2T[:, k, :], ps[:, 4 + k // 2, 256 * (k % 2):256 * (k % 2) + 256], ACT.Identity,
                               bias=MC[:, 3, k, 0:1], scale=A2[:, k:k + 1]).then_inc(S("h2_ready"), 1)
            act.wait_ge(S("logit_mm"), 1)
            act.copy(lgT, ps[0:NE, 0, 0:T]).then_inc(S("logit_copy"), 1)
            act.wait_ge(S("logit_t"), 1)
            act.activation(sc.rearrange("p t e -> p (t e)"), ps[:, 1, 0:2 * NE], ACT.Sigmoid).then_inc(S("score"), 1)
            act.wait_ge(S("spread_mm"), 2)
            act.copy(g2b, ps[:, 4:6, :].rearrange("p a n -> p (a n)")).then_inc(S("g2_ready"), 1)
            act.wait_ge(S("passes_ready"), 1)
            n2 = act.value_load(npair[0:1, 0:1], min_val=NE // 2, max_val=2 * NE)
            act.sem_inc(S("out_copy"), 2)
            act.wait_ge(S("zeroed"), 1)
            act.sem_inc(S("pt_copy"), 1)
            with act.Fori(0, n2) as i:
                for b in range(2):
                    act.wait_ge(S("gu_mm"), 2 * i + b + 1)
                    act.copy(gu[:, b, :], ps[:, 4 + b, :]).then_inc(S("gu_copy"), 1)
                for b in range(2):
                    act.wait_ge(S("hid_turn"), 2 * i + b + 1)
                    act.activation(silg[:, b], ps[:, 4 + b, :].rearrange("p (f n) -> p f n", f=FC)[:, :, 0:SLOTS],
                                   ACT.Silu).then_inc(S("silg_ready"), 1)
                act.wait_ge(S("pt_turn"), i + 1)
                act.copy(PT, ps[:, 6, 0:T]).then_inc(S("pt_copy"), 1)
                for h in range(2):
                    act.wait_ge(S("down_mm"), 2 * i + h + 1)
                    act.copy(oS[:, 512 * h:512 * h + 512], ps[:, 4 + h, :]).then_inc(S("out_copy"), 1)
            for t in range(NT):
                act.wait_ge(S("x3_ready"), t + 1)
                if t:
                    act.wait_ge(S("ss3_ready"), t)
                act.activation(ra[:, 4096:5120], x2[:, t, :], ACT.Square, accum_out=ms2[:, 2 + t:3 + t]).then_inc(S("ss3_ready"), 1)

        @block.vector
        def _(dve):
            chain = [0]

            def link(ins):
                chain[0] += 1
                ins.then_inc(S("dve_link"), 1)
                dve.wait_ge(S("dve_link"), chain[0])

            def tt(o, a, b, op):
                return dve.tensor_tensor(o, a, b, op)

            dve.memset(sil[:, :], 0.0).then_inc(S("sil_zero"), 1)
            dve.memset(mr[:, :], 0.0).then_inc(S("modrow_zero"), 1)
            dve.memset(mhalf, -0.5).then_inc(S("mhalf_set"), 1)
            dve.memset(cb[:, 2048:4096], 0.0).then_inc(S("cb_zero"), 1)
            dve.wait_ge(S("par_in"), 48)
            dve.tensor_copy(ldt_x, ldt_rows.unsqueeze(2).broadcast_to([DG, 2, 64])).then_inc(S("ldt_x"), 1)
            dve.wait_ge(S("vec_t"), 1)
            dve.tensor_copy(vt[:, :], ps[:, 0, 0:V_ROWS]).then_inc(S("vec_copy"), 1)
            dve.wait_ge(S("vec_copy"), 1)
            dve.wait_ge(S("par_t"), 1)
            dve.tensor_copy(tmpv[:, 0:3, :], ps[:, 1, 0:96].rearrange("p (n w) -> p n w", n=3)).then_inc(S("par_copy"), 1)
            dve.wait_ge(S("par_copy"), 1)
            dve.sem_inc(S("col_copy"), 1)
            link(dve.tensor_scalar(tv(T_ARE), tv(T_ARE), -1e-4, None, ALU.min))
            dve.wait_ge(S("dt_ready"), 1)
            tt(tv(T_ADT), tv(T_ARE), tv(T_DT), ALU.mult).then_inc(S("adt_ready"), 1)
            link(tt(tv(T_TH), tv(T_AIM), tv(T_DT), ALU.mult))
            link(dve.tensor_scalar(tv(T_K), tv(T_TH), 1.0 / TWO_PI, MAGIC, ALU.mult, ALU.add))
            link(dve.tensor_scalar(tv(T_K), tv(T_K), -MAGIC, None, ALU.add))
            for part in (PI_A, PI_B, PI_C):
                link(dve.scalar_tensor_tensor(tv(T_TH), tv(T_K), -part, tv(T_TH), ALU.mult, ALU.add))
            dve.tensor_scalar(tv(T_ANG), tv(T_TH), 3.1415925, -3.1415925, ALU.min, ALU.max).then_inc(S("ang_ready"), 1)
            link(tt(tv(T_D1), tv(T_ARE), tv(T_ARE), ALU.mult))
            link(tt(tv(T_D2), tv(T_AIM), tv(T_AIM), ALU.mult))
            link(tt(tv(T_D1), tv(T_D1), tv(T_D2), ALU.add))
            link(dve.reciprocal(tv(T_D1), tv(T_D1)))
            dve.wait_ge(S("mag_ready"), 1)
            dve.wait_ge(S("sin_ready"), 1)
            link(tt(tv(T_D2), tv(T_SHF), tv(T_SHF), ALU.mult))
            link(dve.tensor_scalar(tv(T_D2), tv(T_D2), -2.0, 1.0, ALU.mult, ALU.add))
            link(dve.memset(LP[:, 0, 0, :], 1.0))
            link(dve.memset(LP[:, 0, 1, :], 0.0))
            link(tt(LP[:, 1, 0, :], tv(T_MAG), tv(T_D2), ALU.mult))
            link(tt(LP[:, 1, 1, :], tv(T_MAG), tv(T_SIN), ALU.mult))
            link(dve.tensor_scalar(tv(T_K), LP[:, 1, 0, :], -1.0, None, ALU.add))
            link(tt(tv(T_T1), tv(T_K), tv(T_ARE), ALU.mult))
            link(tt(tv(T_T2), LP[:, 1, 1, :], tv(T_AIM), ALU.mult))
            link(tt(tv(T_T1), tv(T_T1), tv(T_T2), ALU.add))
            link(tt(tv(T_KR), tv(T_T1), tv(T_D1), ALU.mult))
            link(tt(tv(T_T1), LP[:, 1, 1, :], tv(T_ARE), ALU.mult))
            link(tt(tv(T_T2), tv(T_K), tv(T_AIM), ALU.mult))
            link(tt(tv(T_T1), tv(T_T1), tv(T_T2), ALU.subtract))
            link(tt(tv(T_KI), tv(T_T1), tv(T_D1), ALU.mult))
            for lo, n in ((1, 1), (2, 2), (4, 4)):
                a_r, a_i = LP[:, 1:1 + n, 0, :], LP[:, 1:1 + n, 1, :]
                b_r = LP[:, lo, 0, :].unsqueeze(1).broadcast_to([P, n, DG])
                b_i = LP[:, lo, 1, :].unsqueeze(1).broadcast_to([P, n, DG])
                o_r, o_i = LP[:, lo + 1:lo + 1 + n, 0, :], LP[:, lo + 1:lo + 1 + n, 1, :]
                t = ps[:, 2, 0:n * DG].rearrange("p (n g) -> p n g", n=n)
                u = ps[:, 2, 256:256 + n * DG].rearrange("p (n g) -> p n g", n=n)
                tt(o_r, a_r, b_r, ALU.mult)
                tt(o_i, a_r, b_i, ALU.mult)
                tt(t, a_i, b_i, ALU.mult)
                link(tt(u, a_i, b_r, ALU.mult))
                tt(o_r, o_r, t, ALU.subtract)
                link(tt(o_i, o_i, u, ALU.add))
            LPv = LP.rearrange("p k r (d g) -> p d r g k", d=2)
            for r in range(2):
                dve.tensor_copy(PW[:, 0, r], LPv[:, 0, r, :, 0:L][:, :, ::-1])
                link(dve.tensor_copy(PW[:, 1, r], LPv[:, 1, r, :, 0:L]))

            for n in range(4):
                d, r = n // 2, n % 2
                dve.wait_ge(S("c_t"), n + 1)
                v = ps[:, (0, 1, 5, 6)[n], :].rearrange("p (g a i) -> p a g i", g=GP, a=2)
                for a in range(2):
                    mm = dve.tensor_copy(CT[64 * a:64 * a + 64, d, r], v[64 * a:64 * a + 64, a])
                mm.then_inc(S("ct_copy"), 1)
            dve.wait_ge(S("ct_copy"), 4)
            dve.wait_ge(S("cb_zero"), 1)
            for a in range(2):
                for r in range(2):
                    for d in range(2):
                        mm = dve.tensor_scalar(CBv[64 * a:64 * a + 64, d, r, :, 16 * a:16 * a + 16],
                                               CT[64 * a:64 * a + 64, d, r], 1.0 if r == 0 else -1.0, None, ALU.mult)
            mm.then_inc(S("cb_ready"), 1)

            for t in range(4):
                dve.wait_ge(S("ss_ready"), t + 1)
                dve.tensor_scalar(ms[:, t:t + 1], ms[:, t:t + 1], 1.0 / D, EPS, ALU.mult, ALU.add).then_inc(S("ms_ready"), 1)
            for t in range(4):
                dve.wait_ge(S("rstd_ready"), t + 1)
                dve.tensor_scalar(xc[:, t, :], xc[:, t, :], rstd[:, t:t + 1], None, ALU.mult).then_inc(S("xn_ready"), 1)

            dve.wait_ge(S("b_in"), 16 * 4)
            for d in range(2):
                kr = tv(T_KR)[:, 16 * d:16 * d + 16].unsqueeze(2).broadcast_to([P, GP, SG])
                ki = tv(T_KI)[:, 16 * d:16 * d + 16].unsqueeze(2).broadcast_to([P, GP, SG])
                br_, bi_ = Br[:, d, 0], Br[:, d, 1]
                t = ps[:, 2, 0:256].rearrange("p (g j) -> p g j", g=GP)
                u = ps[:, 2, 256:512].rearrange("p (g j) -> p g j", g=GP)
                tt(t, bi_, ki, ALU.mult)
                link(tt(u, br_, ki, ALU.mult))
                tt(br_, br_, kr, ALU.mult)
                link(tt(bi_, bi_, kr, ALU.mult))
                tt(br_, br_, t, ALU.subtract)
                link(tt(bi_, bi_, u, ALU.add))
            dve.sem_inc(S("bbar_ready"), 1)

            def powers_times(dst, pw, m, r, sign_im, done):
                for d in range(2):
                    for rr in r:
                        for h in range(2):
                            g = slice(8 * h, 8 * h + 8)
                            pr = pw[:, d, 0, g].unsqueeze(3).broadcast_to([P, 8, L, SG])
                            pi = pw[:, d, 1, g].unsqueeze(3).broadcast_to([P, 8, L, SG])
                            mr_ = m[:, d, 0, g].unsqueeze(2).broadcast_to([P, 8, L, SG])
                            mi_ = m[:, d, 1, g].unsqueeze(2).broadcast_to([P, 8, L, SG])
                            o = dst[:, d, rr, g]
                            t = ps[:, 2:4, :].rearrange("p a (g s j) -> p (a g) s j", g=4, s=L)
                            if rr == 0:
                                tt(o, pr, mr_, ALU.mult)
                                link(tt(t, pi, mi_, ALU.mult))
                                ins = tt(o, o, t, ALU.subtract)
                            else:
                                tt(o, pr, mi_, ALU.mult)
                                link(tt(t, pi, mr_, ALU.mult))
                                if sign_im > 0:
                                    ins = tt(o, o, t, ALU.add)
                                else:
                                    ins = dve.scalar_tensor_tensor(o.rearrange("p g s j -> p (g s j)"), o.rearrange("p g s j -> p (g s j)"), -1.0,
                                                                   t.rearrange("p g s j -> p (g s j)"), ALU.mult, ALU.subtract)
                            if (rr, h) != (1, 1):
                                link(ins)
                    ins.then_inc(S(done), 1)
                    dve.wait_ge(S(done), d + 1)

            powers_times(SA, PW, Br, (0, 1), 1, "sa_ready")

            for d in range(2):
                dve.wait_ge(S("kk_mm"), d + 1)
                link(dve.tensor_copy(KS[:, d].rearrange("p q s j -> p (q s j)"), ps[:, d, :]))
                if d == 0:
                    dve.sem_inc(S("ks_ready"), 1)
            tt(KS[:, 1, :, 0, :], KS[:, 1, :, 0, :], KS[:, 0, :, L - 1, :], ALU.add).then_inc(S("ks_ready"), 1)

            for r in range(2):
                dve.tensor_copy(PW[:, 0, r], LPv[:, 0, r, :, 1:L + 1])
                link(dve.tensor_copy(PW[:, 1, r], LPv[:, 1, r, :, 1:L + 1][:, :, ::-1]))
            dve.wait_ge(S("sa_t"), 16)
            powers_times(MO.rearrange("p d r g (s j) -> p d r g s j", s=L), PW, CT, (0, 1), -1, "mo_half")
            dve.wait_ge(S("mo_half"), 2)
            dve.sem_inc(S("mo_ready"), 1)
            dve.memset(cb[:, 0:1280], 0.0).then_inc(S("pad_zero"), 1)

            pw_re = [small_pw[:, 128 * k:128 * k + 64] for k in range(4)]
            pw_im = [small_pw[:, 128 * k + 64:128 * k + 128] for k in range(4)]

            dve.wait_ge(S("sa_t"), 16)
            pr, pi = LP[:, 8, 0, :], LP[:, 8, 1, :]
            for k in range(4):
                if k:
                    a_r, a_i = pw_re[k - 1][:, 0:32], pw_im[k - 1][:, 32:64]
                    tt(tmp32[0], a_r, LP[:, 8, 0, :], ALU.mult)
                    tt(tmp32[1], a_i, LP[:, 8, 1, :], ALU.mult)
                    tt(tmp32[2], a_r, LP[:, 8, 1, :], ALU.mult)
                    link(tt(tmp32[3], a_i, LP[:, 8, 0, :], ALU.mult))
                    tt(tmp32[0], tmp32[0], tmp32[1], ALU.subtract)
                    link(tt(tmp32[2], tmp32[2], tmp32[3], ALU.add))
                    pr, pi = tmp32[0], tmp32[2]
                dve.tensor_copy(pw_re[k][:, 0:32], pr)
                dve.tensor_copy(pw_re[k][:, 32:64], pr)
                dve.tensor_scalar(pw_im[k][:, 0:32], pi, -1.0, None, ALU.mult)
                link(dve.tensor_copy(pw_im[k][:, 32:64], pi))

            def pair(v):
                return v.rearrange("p n (r g) -> p n r g", r=2)

            dve.wait_ge(S("s_mm"), 8)
            link(dve.memset(E[:, 0:64], 0.0))
            dve.wait_ge(S("s_ev"), 8)
            S4 = SSv.rearrange("p (b k) w -> p k b w", k=4)
            tAv = tA.rearrange("p (n w) -> p n w", w=64)
            tBv = tB.rearrange("p (n w) -> p n w", w=64)
            for k in range(1, 4):
                prev = S4[:, k - 1]
                pre = pw_re[0].unsqueeze(1).broadcast_to([P, 16, 64])
                for r in range(2):
                    tt(tBv[:, :, 32 * r:32 * r + 32], prev[:, :, 32 * (1 - r):32 * (1 - r) + 32],
                       pw_im[0][:, 32 * r:32 * r + 32].unsqueeze(1).broadcast_to([P, 16, 32]), ALU.mult)
                link(tt(tAv, prev, pre, ALU.mult))
                link(tt(tAv, tAv, S4[:, k], ALU.add))
                link(tt(S4[:, k], tAv, tBv, ALU.add))
            Ev = E.rearrange("p (n w) -> p n w", w=64)
            for n in range(15):
                prev = Ev[:, n]
                tt(tB[:, 0:64].rearrange("p (r g) -> p r g", r=2), prev.rearrange("p (r g) -> p r g", r=2)[:, ::-1, :],
                   pw_im[3].rearrange("p (r g) -> p r g", r=2), ALU.mult)
                link(tt(tA[:, 0:64], prev, pw_re[3], ALU.mult))
                link(tt(tA[:, 0:64], tA[:, 0:64], S4[:, 3, n], ALU.add))
                link(tt(Ev[:, n + 1], tA[:, 0:64], tB[:, 0:64], ALU.add))
            dve.wait_ge(S("toep_in"), 16 * (2 * L - 1))
            HPd = [HP[:, :, 0:16, :].rearrange("p r g (b k) -> p k b r g", k=4),
                   HP[:, :, 16:32, ::-1].rearrange("p r g (b k) -> p k b r g", k=4)]
            x8 = Ev[:, 8:16]
            for k in range(4):
                if k == 0:
                    for d in range(2):
                        ins = dve.tensor_copy(HPd[d][:, 0], pair(x8)[:, :, :, 16 * d:16 * d + 16])
                    continue
                a8, b8 = tAv[:, 0:8], tBv[:, 0:8]
                for r in range(2):
                    tt(b8[:, :, 32 * r:32 * r + 32], x8[:, :, 32 * (1 - r):32 * (1 - r) + 32],
                       pw_im[k - 1][:, 32 * r:32 * r + 32].unsqueeze(1).broadcast_to([P, 8, 32]), ALU.mult)
                link(tt(a8, x8, pw_re[k - 1].unsqueeze(1).broadcast_to([P, 8, 64]), ALU.mult))
                link(tt(a8, a8, S4[:, k - 1, 8:16], ALU.add))
                for d in range(2):
                    ins = tt(HPd[d][:, k], pair(a8)[:, :, :, 16 * d:16 * d + 16], pair(b8)[:, :, :, 16 * d:16 * d + 16], ALU.add)
                if k < 3:
                    link(ins)
            ins.then_inc(S("hp_ready"), 1)

            dve.wait_ge(S("y_t"), 1)
            yv = ps[:, 6:8, :].rearrange("p a (t q c) -> p q (a t) c", t=4, q=4)
            for q in range(4):
                dve.scalar_tensor_tensor(ysum[:, q], UTs[:, :, q, 1, :], vt[:, V_D + q:V_D + q + 1], yv[:, q],
                                         ALU.mult, ALU.add).then_inc(S("ysum_ready"), 1)
            for m in range(4):
                dve.wait_ge(S("sig_ready"), m + 1)
                tt(cat[:, 4 + m, :].rearrange("p (c t) -> p t c", t=L), G[:, m], sg[:, m], ALU.mult).then_inc(S("cat_ssm"), 1)

            dve.wait_ge(S("g1_ready"), 1)
            for t in range(NT):
                dve.wait_ge(S("mix_mm"), 2 * t + 2)
                dve.wait_ge(S(f"xres_in{t}"), 16)
                tmp = ra[:, 5120 + 1024 * t:6144 + 1024 * t]
                link(tt(tmp, ps[:, 2 * t:2 * t + 2, :].rearrange("p a n -> p (a n)"), g1b, ALU.mult))
                tt(x2[:, t, :], x2[:, t, :], tmp, ALU.add).then_inc(S("x2_ready"), 1)
            dve.wait_ge(S("mod_col"), 3)
            dve.scalar_tensor_tensor(A2, MC[:, 4, :, 0], 1.0, vt[:, V_GF:V_GF + 8], ALU.add, ALU.mult).then_inc(S("a2_ready"), 1)
            dve.wait_ge(S("ss2_ready"), 2)
            dve.tensor_scalar(ms2[:, 0:2], ms2[:, 0:2], 1.0 / D, EPS, ALU.mult, ALU.add).then_inc(S("ms2_ready"), 1)
            dve.wait_ge(S("rstd2_ready"), 1)
            dve.wait_ge(S("x2_ready"), 2)
            for t in range(NT):
                ins = dve.tensor_scalar(xn2[:, t, :], x2[:, t, :], rstd2[:, t:t + 1], None, ALU.mult)
            ins.then_inc(S("xn2_ready"), 1)
            dve.memset(PT, 0.0)
            dve.memset(oS, 0.0).then_inc(S("zeroed"), 1)

            dve.wait_ge(S("br_in"), 16)
            dve.wait_ge(S("score"), 1)
            link(tt(sel, sc, brb.unsqueeze(1).broadcast_to([P, NT, NE]), ALU.add))
            for t in range(NT):
                for g in range(NGRP):
                    ins = dve.max(top8[:, t, g, :], sel[:, t, EPG * g:EPG * g + EPG])
            link(ins)
            link(tt(gs, top8[:, :, :, 0], top8[:, :, :, 1], ALU.add))

            def first_best(dst, score, rank, n):
                link(dve.tensor_reduce(best, score, AX.X, ALU.max))
                link(tt(dst, score, best.unsqueeze(2).broadcast_to([P, NT, n]), ALU.is_equal))
                link(tt(dst, dst, rank.unsqueeze(1).broadcast_to([P, NT, n]), ALU.mult))
                link(dve.tensor_reduce(best, dst, AX.X, ALU.max))
                link(tt(dst, dst, best.unsqueeze(2).broadcast_to([P, NT, n]), ALU.is_equal))

            link(dve.tensor_scalar(rank, iota[:, 0:NE], -1.0, float(NE), ALU.mult, ALU.add))
            first_best(gm, gs, rank[:, 0:NGRP], NGRP)
            gmx = gm.unsqueeze(3).broadcast_to([P, NT, NGRP, EPG])
            sel4 = sel.rearrange("p t (g e) -> p t g e", g=NGRP)
            link(tt(sel4, sel4, gmx, ALU.mult))
            link(dve.tensor_scalar(gm, gm, HUGE, -HUGE, ALU.mult, ALU.add))
            link(tt(sel4, sel4, gmx, ALU.add))
            first_best(one1, sel, rank, NE)
            link(dve.scalar_tensor_tensor(sel.rearrange("p t e -> p (t e)"), one1.rearrange("p t e -> p (t e)"), -HUGE * 4,
                                          sel.rearrange("p t e -> p (t e)"), ALU.mult, ALU.add))
            first_best(one2, sel, rank, NE)
            tt(msk, one1, one2, ALU.add).then_inc(S("chosen"), 1)
            dve.wait_ge(S("chosen"), 1)
            link(tt(gw, msk, sc, ALU.mult))
            link(dve.tensor_reduce(best, gw, AX.X, ALU.add))
            link(dve.reciprocal(best, best))
            link(tt(gw, gw, best.unsqueeze(2).broadcast_to([P, NT, NE]), ALU.mult))
            dve.wait_ge(S("count_mm"), 1)
            link(dve.tensor_scalar(sel, msk, -BIG, BIG, ALU.mult, ALU.add))
            link(tt(sel, sel, ps[:, 2, 0:2 * NE].rearrange("p (t e) -> p t e", t=NT), ALU.add))
            for n in range(4):
                dve.tensor_scalar(posx[:, :, NE * n:NE * n + NE], sel, float(-SLOTS * n), None, ALU.add)
                dve.tensor_copy(wx[:, :, NE * n:NE * n + NE], gw)
            dve.memset(posx[:, :, 4 * NE:NCOL], BIG)
            link(dve.memset(wx[:, :, 4 * NE:NCOL], 0.0))
            link(dve.tensor_reduce(best[:, 0:1], ps[:, 2, 2 * NE:3 * NE], AX.X, ALU.max))
            link(dve.tensor_scalar(best[:, 1:2], best[:, 0:1], float(SLOTS), None, ALU.is_gt))
            for n in (2, 3):
                link(dve.tensor_scalar(pcount, best[:, 0:1], float(SLOTS * n), None, ALU.is_gt))
                link(tt(best[:, 1:2], best[:, 1:2], pcount, ALU.add))
            dve.tensor_scalar(npair[:, 0:1], best[:, 1:2], float(NE // 2), float(NE // 2), ALU.mult, ALU.add).then_inc(S("passes_ready"), 1)

            iota4 = iota.rearrange("p (b s) -> p b s", b=2).unsqueeze(1).broadcast_to([P, NT, 2, SLOTS])

            def columns(v, at):
                return v[:, :, at].unsqueeze(3).broadcast_to([P, NT, 2, SLOTS])

            def modulate(n):
                v = ps[:, 6:8, :].rearrange("p a (k s) -> p (a k) s", k=4)
                tt(xm, v, A2.unsqueeze(2).broadcast_to([P, KD, 2 * SLOTS]), ALU.mult).then_inc(S("xm_scaled"), 1)
                dve.wait_ge(S("xm_scaled"), n)
                tt(xm, xm, sh2.unsqueeze(2).broadcast_to([P, KD, 2 * SLOTS]), ALU.add).then_inc(S("xm_ready"), 1)

            dve.tensor_copy(sh2, MC[:, 3, :, 0]).then_inc(S("pos_ready"), 1)
            dve.wait_ge(S("pos_ready"), 1)
            tt(Pm, iota4, columns(posx, slice(0, 2)), ALU.is_equal).then_inc(S("slots"), 1)
            dve.wait_ge(S("gather_mm"), 1)
            dve.tensor_copy(xg, ps[:, 6:8, :].rearrange("p a n -> p (a n)")).then_inc(S("xg_copy"), 1)
            dve.wait_ge(S("x_turn"), 1)
            modulate(1)
            dve.wait_ge(S("passes_ready"), 1)
            n2 = dve.value_load(npair[0:1, 0:1], min_val=NE // 2, max_val=2 * NE)
            with dve.Fori(0, n2) as i:
                tt(PG, iota4, columns(posx, bass.ds(2 * i, 2)), ALU.is_equal).then_inc(S("onehot"), 1)
                tt(Pm, iota4, columns(posx, bass.ds(2 * i + 2, 2)), ALU.is_equal)
                dve.wait_ge(S("onehot"), i + 1)
                tt(PG, PG, columns(wx, bass.ds(2 * i, 2)), ALU.mult).then_inc(S("slots"), 1)
                dve.wait_ge(S("gather_mm"), i + 2)
                dve.tensor_copy(xg, ps[:, 6:8, :].rearrange("p a n -> p (a n)")).then_inc(S("xg_copy"), 1)
                for b in range(2):
                    dve.wait_ge(S("silg_ready"), 2 * i + b + 1)
                    tt(hid[:, b], silg[:, b], ps[:, 4 + b, :].rearrange("p (f n) -> p f n", f=FC)[:, :, SLOTS:2 * SLOTS],
                       ALU.mult).then_inc(S("hid_ready"), 1)
                dve.wait_ge(S("x_turn"), i + 2)
                modulate(i + 2)

            dve.wait_ge(S("scatter_mm"), n2 + 1)
            dve.wait_ge(S("g2_ready"), 1)
            for t in range(NT):
                tmp = rc[:, 1024 * t:1024 * t + 1024]
                link(tt(tmp, ps[:, 2 * t:2 * t + 2, :].rearrange("p a n -> p (a n)"), g2b, ALU.mult))
                tt(x2[:, t, :], x2[:, t, :], tmp, ALU.add).then_inc(S("x3_ready"), 1)
            dve.wait_ge(S("ss3_ready"), 2)
            dve.tensor_scalar(ms2[:, 2:4], ms2[:, 2:4], 1.0 / D, EPS, ALU.mult, ALU.add).then_inc(S("ms2_ready"), 1)
            dve.wait_ge(S("rstd2_ready"), 2)
            dve.wait_ge(S("gf_in"), 16)
            dve.wait_ge(S("x3_ready"), 2)
            for t in range(NT):
                for h in range(2):
                    c0 = slice(512 * h, 512 * h + 512)
                    dve.scalar_tensor_tensor(xn2[:, t, c0], x2[:, t, c0], rstd2[:, 2 + t:3 + t], gfb[:, c0],
                                             ALU.mult, ALU.mult).then_inc(S("fin_ready"), 1)


_INS = ["x", "c", "ctx", "c_ctx", "w_mod", "b_mod", "g_mix", "g_ffn", "w_in", "w_out", "w_pool", "s_pool",
        "ssm_a_re", "ssm_a_im", "ssm_log_dt", "ssm_b_re", "ssm_b_im", "ssm_c_re", "ssm_c_im", "ssm_d",
        "w_glu", "b_glu", "w_router", "b_router", "w_gate", "w_up", "w_down", "g_final"]


def kernel(**inputs):
    import concourse.bacc as bacc
    from concourse.bass_utils import run_bass_kernel_spmd

    nc = bacc.Bacc("TRN2", target_bir_lowering=False, num_devices=1)
    arrays, args = {}, []
    for name in _INS:
        a = np.ascontiguousarray(inputs[name])
        arrays[f"in_{name}"] = a
        args.append(nc.dram_tensor(f"in_{name}", a.shape, mybir.dt.from_np(a.dtype), kind="ExternalInput").ap())
    arrays["in_constants"] = shape_constants()
    args.append(nc.dram_tensor("in_constants", arrays["in_constants"].shape, F32, kind="ExternalInput").ap())
    shape = inputs["x"].shape
    args.append(nc.dram_tensor("out_x", shape, F32, kind="ExternalOutput").ap())
    hybrid_block(nc, *args)
    r = run_bass_kernel_spmd(nc, [arrays], core_ids=[0])
    return r.results[0]["out_x"]
```

```python
from contextlib import ExitStack

import numpy as np
import concourse.bass as bass
from concourse import mybir

ALU = mybir.AluOpType
ACT = mybir.ActivationFunctionType
AX = mybir.AxisListType
F32 = mybir.dt.float32
I32 = mybir.dt.int32

P = 128
GRID = 64
WINDOWS = (2, 4, 8, 16)
L = 8
SG = 16
SLOTS = 64
BIG = 65536.0
HUGE = 1e30
EPS = 1e-6
MAGIC = 12582912.0
TWO_PI = 6.283185307179586
PI_A = 6.28125
PI_B = float(np.float32(int((TWO_PI - PI_A) * 2 ** 21) / 2 ** 21))
PI_C = float(np.float32(TWO_PI - PI_A - PI_B))

C_ID, C_UP, C_ONE, C_IOTA, C_STACK, C_COLS = 0, 128, 256, 384, 512, 544
V_C, V_CC, V_GM, V_GF, V_SP, V_D, V_BG, V_B2, V_A = 0, 8, 16, 24, 32, 36, 40, 44, 52
V_COLS = V_A + 3 * 32


def shape_constants():
    k = np.zeros((P, C_COLS), np.float32)
    k[:, C_ID:C_ID + P] = np.eye(P)
    k[:, C_UP:C_UP + P] = np.triu(np.ones((P, P)), 1)
    k[:, C_ONE:C_ONE + P] = 1.0
    k[:, C_IOTA:C_IOTA + 2 * SLOTS] = np.arange(2 * SLOTS) % SLOTS
    k[:, C_STACK:C_STACK + 32] = np.tile(np.eye(32), (4, 1))
    return k


def pooling_matrices():
    t = np.arange(P)
    m = np.zeros((P, len(WINDOWS), P), np.float32)
    for g, w in enumerate(WINDOWS):
        row, at = t // GRID, t % GRID
        lo, hi = np.maximum(at - w // 2, 0), np.minimum(at + w // 2, GRID)
        inside = (row[:, None] == row[None, :]) & (at[:, None] >= lo[None, :]) & (at[:, None] < hi[None, :])
        m[:, g] = inside / (hi - lo)[None, :].astype(np.float32) - np.eye(P)
    return m.reshape(P, -1)


def hybrid_block(nc, x, ctx, w_mod, columns, ssm_bc, b_mod_rows, w_in, w_out, w_pool, w_glu, w_router, b_router,
                 w_gate, w_up, w_down, g_final, consts, pool_consts, out):
    D = x.shape[2]
    KD = D // P
    T = x.shape[1]
    NT = T // P
    NE = w_router.shape[1]
    NGRP = 4
    EPG = NE // NGRP
    F = w_gate.shape[3]
    FC = F // P
    NC = T // L
    DG = 32
    GP = 16

    with ExitStack() as stack:
        def sb(name, floats, dt=F32):
            return stack.enter_context(nc.sbuf_tensor(name, [P, floats], dt))

        sems = {}

        def S(name):
            if name not in sems:
                sems[name] = stack.enter_context(nc.semaphore(name))
            return sems[name]

        wts = sb("wts", 2 * 12288)
        ra = sb("ra", 8192)
        rc = sb("rc", 8192)
        cb = sb("cb", 4096)
        ut = sb("ut", 2048)
        r2 = sb("r2", 2048)
        mr = sb("mr", 1536)
        cst = sb("cst", C_COLS)
        vt = sb("vt", V_COLS)
        mcol = sb("mcol", 96)
        lam = sb("lam", 9 * 64)
        pws = sb("pws", 512)
        sil = sb("sil", KD * 32)
        aux = sb("aux", 160)
        small = sb("small", 48)
        pairs = sb("pairs", 2, I32)
        ms, rstd, mhalf = small[:, 0:4], small[:, 4:8], small[:, 8:9]
        ms2, rstd2 = small[:, 12:16], small[:, 16:20]
        ps = stack.enter_context(nc.psum_tensor("ps", [P, 8, 512], F32))

        ident = cst[:, C_ID:C_ID + P]
        upper = cst[:, C_UP:C_UP + P]
        ones = cst[:, C_ONE:C_ONE + P]
        iota = cst[:, C_IOTA:C_IOTA + 2 * SLOTS]
        stack4 = cst[:, C_STACK:C_STACK + NE]

        wm = [wts[:, 0:2048], wts[:, 2048:4096], r2[:, :]]
        ST = wts[:, 4096:12288].rearrange("p (d r g m) -> p d r g m", d=2, r=2, g=GP)
        WB = wts[:, 12288:12288 + 8192].rearrange("p (k n) -> p k n", k=KD)
        TT = ra[:, 4096:8192].rearrange("p (t n) -> p t n", t=L)
        E = wts[:, 4096:4608]
        tA, tB = cb[:, 1024:1536], cb[:, 1536:2048]
        tC, tD = ra[:, 3072:3328], ra[:, 3328:3584]
        wpool = wts[:, 7232:7744].rearrange("p (g n) -> p g n", g=4)
        wo_pool = wts[:, 7744:11840].rearrange("p (k n) -> p k n", k=4)
        wo_ssm = wts[:, 12288:16384].rearrange("p (k n) -> p k n", k=4)
        wglu = wts[:, 16384:18432].rearrange("p (k n) -> p k n", k=4)
        cat = wts[:, 18432:20480].rearrange("p (k t) -> p k t", k=KD)

        xc = ra[:, 0:4096].rearrange("p (t d) -> p t d", t=4)
        hT = ra[:, 4096:8192].rearrange("p (k t) -> p k t", k=KD)
        U8 = ra[:, 0:2048].rearrange("p (g q h c) -> p g q h c", g=8, q=4, h=2)
        SS = wts[:, 20480:24576]
        HP = ra[:, 2048:4096].rearrange("p (r g c) -> p r g c", r=2, g=DG)

        SA = rc[:, :].rearrange("p (d r g s j) -> p d r g s j", d=2, r=2, g=GP, s=L)
        MO = rc[:, :].rearrange("p (d r g n) -> p d r g n", d=2, r=2, g=GP)
        Br = cb[:, 0:1024].rearrange("p (d r g j) -> p d r g j", d=2, r=2, g=GP)
        CT = cb[:, 1024:2048].rearrange("p (d r g j) -> p d r g j", d=2, r=2, g=GP)
        BC = cb[:, 0:2048]
        pmat = cb[:, 0:512].rearrange("p (g t) -> p g t", g=4)
        uP = cb[:, 2048:3072].rearrange("p (t n) -> p t n", t=NT)
        pT = cb[:, 3072:4096].rearrange("p (g t) -> p g t", g=4)
        tmpv = ut[:, 1024:2048].rearrange("p (n w) -> p n w", w=32)
        UTs = ut[:, :].rearrange("p (s q h c) -> p s q h c", s=L, q=4, h=2)
        KS = wts[:, 20480:21504].rearrange("p (d q s j) -> p d q s j", d=2, q=4, s=L)
        KT = ra[:, 2048:3072].rearrange("p (d n) -> p d n", d=2)
        modrow = mr[:, :].rearrange("p (r n) -> p r n", r=3)
        LP = lam[:, :].rearrange("p (k r g) -> p k r g", k=9, r=2)
        PW = pws[:, :].rearrange("p (d r g s) -> p d r g s", d=2, r=2, g=GP)
        silc = sil[:, :].rearrange("p (k m) -> p k m", k=KD)
        MC = mcol[:, :].rearrange("p (v k q) -> p v k q", v=6, k=KD)
        wrt = ut[:, 1024:1024 + KD * NE].rearrange("p (k e) -> p k e", k=KD)

        acc = cb[:, 0:2048]

        ysb = rc[:, 0:1024]
        ysum = rc[:, 1024:2048].rearrange("p (q t c) -> p q t c", q=4, t=L)
        G = rc[:, 2048:3072].rearrange("p (q t c) -> p q t c", q=4, t=L)
        sg = rc[:, 3072:4096].rearrange("p (q t c) -> p q t c", q=4, t=L)
        g1b = cb[:, 3072:4096]
        g2b = rc[:, 5120:6144]
        gfb = r2[:, 0:1024]
        x2 = rc[:, 6144:8192].rearrange("p (t d) -> p t d", t=NT)

        xn2 = ra[:, 0:2048].rearrange("p (t d) -> p t d", t=NT)
        h2T = ra[:, 2048:4096].rearrange("p (k t) -> p k t", k=KD)
        gu = ra[:, 4096:5120].rearrange("p (b f) -> p b f", b=2)
        xm = ra[:, 6144:7168].rearrange("p (k s) -> p k s", k=KD)
        hid = ra[:, 7168:7680].rearrange("p (b f s) -> p b f s", b=2, f=FC)
        silg = ra[:, 7680:8192].rearrange("p (b f s) -> p b f s", b=2, f=FC)
        PT = cb[:, 0:256]
        oS = cb[:, 256:1280]
        Pm = cb[:, 1280:1536].rearrange("p (t b s) -> p t b s", t=NT, b=2)
        PG = cb[:, 1536:1792].rearrange("p (t b s) -> p t b s", t=NT, b=2)
        rt = cb[:, 2048:4096]
        NCOL = 4 * NE + 4
        posx = ut[:, 0:NT * NCOL].rearrange("p (t e) -> p t e", t=NT)
        wx = ut[:, 512:512 + NT * NCOL].rearrange("p (t e) -> p t e", t=NT)
        A1 = aux[:, 0:16].rearrange("p (k q) -> p k q", q=2)
        A2, sh2 = aux[:, 16:24], aux[:, 24:32]
        tmp32 = [aux[:, 32 + 32 * n:64 + 32 * n] for n in range(4)]
        CBv = cb[:, 2048:4096].rearrange("p (d r g m) -> p d r g m", d=2, r=2, g=GP)
        SSv = SS.rearrange("p (n w) -> p n w", w=64)
        (T_ARE, T_AIM, T_LDT, T_DT, T_ADT, T_MAG, T_SIN, T_SHF, T_ANG, T_TH, T_K, T_D1, T_D2, T_T1, T_T2, T_KR,
         T_KI) = range(17)

        def tv(n):
            return vt[:, V_A + 32 * n:V_A + 32 * n + 32] if n <= T_LDT else tmpv[:, n, :]

        brb = rt[:, 0:NE]
        sc = rt[:, 32:96].rearrange("p (t e) -> p t e", t=NT)
        sel = rt[:, 96:160].rearrange("p (t e) -> p t e", t=NT)
        one1 = rt[:, 160:224].rearrange("p (t e) -> p t e", t=NT)
        one2 = rt[:, 224:288].rearrange("p (t e) -> p t e", t=NT)
        msk = rt[:, 288:352].rearrange("p (t e) -> p t e", t=NT)
        gw = rt[:, 352:416].rearrange("p (t e) -> p t e", t=NT)
        top8 = rt[:, 416:480].rearrange("p (t g n) -> p t g n", t=NT, g=NGRP)
        gs = rt[:, 480:488].rearrange("p (t g) -> p t g", t=NT)
        gm = rt[:, 488:496].rearrange("p (t g) -> p t g", t=NT)
        rank = rt[:, 496:528]
        best = rt[:, 528:530]
        pcount = rt[:, 530:531]
        lgT = rt[:, 544:800]
        Wg = [wts[:, 12288 * b:12288 * b + 4096].rearrange("p (k f) -> p k f", k=KD) for b in range(2)]
        Wu = [wts[:, 12288 * b + 4096:12288 * b + 8192].rearrange("p (k f) -> p k f", k=KD) for b in range(2)]
        Wd = [wts[:, 12288 * b + 8192:12288 * b + 12288].rearrange("p (k d) -> p k d", k=FC) for b in range(2)]

        u_dram = nc.dram_tensor("u_scratch", [P, 2048], F32).ap()

        block = stack.enter_context(nc.Block())

        def gu_load(eng, b, e, half, which="gate up"):
            k = slice(4 * half, 4 * half + 4)
            for name, dst, src in (("gate", Wg, w_gate), ("up", Wu, w_up)):
                if name in which:
                    eng.dma_start(dst[b][:, k, :],
                                  src[0, e].rearrange("(k p) f -> p k f", p=P)[:, k, :]).then_inc(S(f"gu_in{b}{half}"), 16)

        def down_load(eng, pair):
            for h in range(2):
                for b in range(2):
                    eng.dma_start(Wd[b][:, :, 512 * h:512 * h + 512],
                                  w_down[0, pair(b), :, 512 * h:512 * h + 512].rearrange("(k p) d -> p k d", p=P)).then_inc(S(f"down_in{h}"), 16)

        @block.sync
        def _(sp):
            sp.dma_start(vt[:, :], columns).then_inc(S("vec_in"), 16)
            sp.dma_start(modrow[0:97:32], b_mod_rows.rearrange("j (r n) -> j r n", r=3)).then_inc(S("bmod_in"), 16)

            sp.dma_start(cst[:, :], consts).then_inc(S("cst_in"), 16)

            def mod_chunk(r, k):
                n = r * KD + k
                if n >= 2 * KD + 3:
                    sp.wait_ge(S("mod2_used"), n - 2 * KD - 2)
                elif n >= 3:
                    sp.wait_ge(S("mod_used"), n - 2)
                sp.dma_start(wm[n % 3], w_mod[0, k * P:(k + 1) * P, 2048 * r:2048 * (r + 1)]).then_inc(S(f"wmod_in{n % 3}"), 16)

            w_in_v = w_in[0].rearrange("(k p) n -> p k n", p=P)
            mod_chunk(0, 0)
            sp.dma_start(BC, ssm_bc).then_inc(S("bc_in"), 16)
            mod_chunk(0, 1)
            mod_chunk(0, 2)
            xv = [ctx[0, 0:P], ctx[0, P:2 * P], x[0, 0:P], x[0, P:2 * P]]
            for t in range(4):
                sp.dma_start(xc[:, t, :], xv[t]).then_inc(S(f"x_in{t}"), 16)
            for k in range(3, KD):
                mod_chunk(0, k)
            sp.dma_start(WB[:, :, 512:1024], w_in_v[:, :, 512:1024]).then_inc(S("win_ssm_in"), 16)
            sp.dma_start(WB[:, :, 0:512], w_in_v[:, :, 0:512]).then_inc(S("win_pool_in"), 16)
            for k in range(5):
                mod_chunk(1, k)
            sp.wait_ge(S("u_out"), 16 * 4)
            for s in range(L):
                sp.dma_start(ra[SG * s:SG * (s + 1), 0:2048].rearrange("i (g n) -> i g n", g=8),
                             u_dram.rearrange("(g i) (s n) -> s i g n", g=8, s=L)[s]).then_inc(S("u8_in"), 16)
            for k in range(5, KD):
                mod_chunk(1, k)
            sp.wait_ge(S("s_mm"), 8)
            w_out_v = w_out[0].rearrange("(k p) n -> p k n", p=P)
            sp.dma_start(wpool, w_pool[0].rearrange("g c d -> c g d")).then_inc(S("wpool_in"), 16)
            sp.dma_start(wo_pool, w_out_v[:, 0:4, :]).then_inc(S("wo_pool_in"), 16)
            sp.wait_ge(S("u_pool_mm"), NT)
            sp.wait_ge(S("kt_ready"), 2)
            for t in range(L):
                if t:
                    sp.dma_start(TT[0:SG * t, t, :], KT[SG * (L - 1 - t):SG * (L - 1), 0, :]).then_inc(S("toep_in"), 16)
                sp.dma_start(TT[SG * t:P, t, :], KT[0:SG * (L - t), 1, :]).then_inc(S("toep_in"), 16)
            sp.dma_start(wglu, w_glu[0].rearrange("(k p) n -> p k n", p=P)).then_inc(S("wglu_in"), 16)
            sp.dma_start(wo_ssm, w_out_v[:, 4:8, :]).then_inc(S("wo_ssm_in"), 16)
            for k in range(3):
                mod_chunk(2, k)
            sp.wait_ge(S("mix_pool"), 1)
            sp.wait_ge(S("hp_ready"), 1)
            gu_load(sp, 0, 0, 0, "up")
            gu_load(sp, 0, 0, 1, "up")
            down_load(sp, lambda b: b)
            sp.wait_ge(S("y_mm"), 1)
            for t in range(NT):
                sp.dma_start(x2[:, t, :], x[0, t * P:(t + 1) * P]).then_inc(S(f"xres_in{t}"), 16)
            for k in range(3, KD):
                mod_chunk(2, k)
            sp.wait_ge(S("mod2_used"), KD)
            gu_load(sp, 0, 0, 0, "gate")
            gu_load(sp, 0, 0, 1, "gate")
            sp.wait_ge(S("mix_mm"), 4)
            gu_load(sp, 1, 1, 0)
            gu_load(sp, 1, 1, 1)
            sp.wait_ge(S("passes_ready"), 1)
            last_pair = sp.value_load(pairs[0:1, 0:1], min_val=NE // 2 - 1, max_val=2 * NE - 1)
            with sp.Fori(0, last_pair) as i:
                for b in range(2):
                    nxt = (2 * i + b + 2) % NE
                    for half in range(2):
                        sp.wait_ge(S("gu_half"), 4 * i + 2 * b + half + 1)
                        gu_load(sp, b, nxt, half)
                sp.wait_ge(S("down_mm"), 2 * i + 2)
                down_load(sp, lambda b: (2 * i + b + 2) % NE)
            for t in range(2 * NT):
                sp.wait_ge(S("fin_ready"), t + 1)
                tt, h = t // 2, t % 2
                sp.dma_start(out[0, tt * P:(tt + 1) * P, 512 * h:512 * (h + 1)],
                             xn2[:, tt, 512 * h:512 * (h + 1)]).then_inc(S("out_done"), 16)
            sp.wait_ge(S("out_done"), 16 * 2 * NT)

        @block.gpsimd
        def _(gp):
            gp.memset(cb[:, 2048:4096], 0.0).then_inc(S("cb_zero"), 1)
            gp.wait_ge(S("mhalf_set"), 1)
            for t in range(4):
                gp.wait_ge(S("ss_ready"), t + 1)
                gp.tensor_scalar(ms[:, t:t + 1], ms[:, t:t + 1], 1.0 / D, EPS, ALU.mult, ALU.add).then_inc(S("ms_ready"), 1)
                gp.wait_ge(S("ms_ready"), t + 1)
                gp.tensor_tensor(rstd[:, t:t + 1], ms[:, t:t + 1], mhalf, ALU.pow).then_inc(S("rstd_ready"), 1)

            gp.wait_ge(S("bc_in"), 16)
            gp.wait_ge(S("cb_zero"), 1)
            for a in range(2):
                for r in range(2):
                    for d in range(2):
                        gp.tensor_scalar(CBv[64 * a:64 * a + 64, d, r, :, 16 * a:16 * a + 16], CT[64 * a:64 * a + 64, d, r],
                                         1.0 if r == 0 else -1.0, None, ALU.mult).then_inc(S("cb_part"), 1)
                        gp.wait_ge(S("cb_part"), 4 * a + 2 * r + d + 1)
            gp.sem_inc(S("cb_ready"), 1)

            gp.wait_ge(S("mod_col"), 1)
            gv = vt[:, V_GM:V_GM + 8].unsqueeze(2).broadcast_to([P, KD, 2])
            gp.tensor_tensor(A1, MC[:, 1, :, :], gv, ALU.mult).then_inc(S("a1_part"), 1)
            gp.wait_ge(S("a1_part"), 1)
            gp.tensor_tensor(A1, A1, gv, ALU.add).then_inc(S("a1_ready"), 1)

            gp.wait_ge(S("sa_ready"), 4)
            gp.dma_start(pmat, pool_consts.rearrange("p (g t) -> p g t", g=4)).then_inc(S("pmat_in"), 16)
            gp.wait_ge(S("pool_mm"), 1)
            gp.dma_start(brb, b_router.rearrange("(a d) -> a d", a=1).broadcast_to([P, NE])).then_inc(S("br_in"), 16)
            gp.wait_ge(S("ysum_ready"), 4)
            gp.dma_start(wrt, w_router.rearrange("(k p) e -> p k e", p=P)).then_inc(S("wr_in"), 16)
            for t in range(2 * NT):
                if t == NT:
                    gp.wait_ge(S("mod2_used"), KD)
                    gp.dma_start(gfb, g_final.rearrange("(a d) -> a d", a=1).broadcast_to([P, D])).then_inc(S("gf_in"), 16)
                gp.wait_ge(S("ms2_ready"), t + 1)
                gp.tensor_tensor(rstd2[:, t:t + 1], ms2[:, t:t + 1], mhalf, ALU.pow).then_inc(S("rstd2_ready"), 1)

        @block.tensor
        def _(pe):
            def mod_chunk(r, k, bank):
                n = r * KD + k
                if k == 0:
                    pe.wait_ge(S("bmod_in"), 16)
                    for j in range(4):
                        pe.matmul(ps[32 * j:32 * j + 32, bank, :], ones[32 * j:32 * j + 1, 0:32],
                                  modrow[32 * j:32 * j + 1, r, :], start=True, stop=False)
                pe.wait_ge(S(f"wmod_in{n % 3}"), 16 * (n // 3 + 1))
                for j in range(4):
                    mm = pe.matmul(ps[32 * j:32 * j + 32, bank, :], silc[:, k, :], wm[n % 3][:, 512 * j:512 * j + 512],
                                   start=False, stop=(k == KD - 1))
                mm.then_inc(S("mod_used"), 1)

            def mod_turn(r, bank):
                pe.wait_ge(S("modrow"), r + 1)
                for b in range(4):
                    mm = pe.transpose(ps[:, bank, 128 * b:128 * b + 128], modrow[:, r, 128 * b:128 * b + 128], ident)
                mm.then_inc(S("mod_t"), 1)

            def turn_sa(d, r):
                pe.wait_ge(S("sa_ready"), 2 * d + r + 1)
                for g4 in range(4):
                    n = 8 * d + 4 * r + g4
                    if n in (8, 9):
                        pe.wait_ge(S("ht_ready_dve" if n % 2 else "ht_ready"), KD)
                    elif n >= 2:
                        pe.wait_ge(S("st_copy"), n - 1)
                    for g in range(4):
                        mm = pe.transpose(ps[:, (n + 1) % 2, 128 * g:128 * g + 128],
                                          SA[:, d, r, 4 * g4 + g].rearrange("p s j -> p (s j)"), ident)
                    mm.then_inc(S("sa_t"), 1)

            pe.wait_ge(S("cst_in"), 16)
            pe.wait_ge(S("sil_ready"), 1)
            for k in range(KD):
                if k >= 6:
                    turn_sa(0, k - 6)
                mod_chunk(0, k, 4)
            pe.wait_ge(S("st_copy"), 8)
            mod_turn(0, 0)

            pe.wait_ge(S("xn_ready"), 4)
            for k in range(KD):
                if k == 1:
                    pe.wait_ge(S("mod_col"), 1)
                elif k >= 2:
                    pe.wait_ge(S("ht_ready_dve" if k % 2 else "ht_ready"), 2 * (k // 2))
                for t in range(4):
                    mm = pe.transpose(ps[:, (k + 1) % 2, 128 * t:128 * t + 128], xc[:, t, P * k:P * k + P], ident)
                mm.then_inc(S("x_t"), 1)

            def lag_kernels():
                pe.wait_ge(S("cb_ready"), 1)
                pe.wait_ge(S("st_copy"), 16)
                for d in range(2):
                    for q in range(4):
                        for r in range(2):
                            for g in range(4):
                                mm = pe.matmul(ps[32 * g:32 * g + 32, d, 128 * q:128 * q + 128], CBv[:, d, r, 4 * q + g, :],
                                               SA[:, d, r, 4 * q + g].rearrange("p s j -> p (s j)"),
                                               start=(r == 0), stop=(r == 1), skip_group_check=True)
                    mm.then_inc(S("kk_mm"), 1)

            def turn_kernels():
                pe.wait_ge(S("ks_ready"), 2)
                for d in range(2):
                    for q in range(4):
                        mm = pe.transpose(ps[:, d, 128 * q:128 * q + 128], KS[:, d, q].rearrange("p s j -> p (s j)"), ident)
                    mm.then_inc(S("kt_t"), 1)

            def u_ssm(q):
                if q == 3:
                    pe.wait_ge(S("u_ssm_ev"), 1)
                for k in range(KD):
                    mm = pe.matmul(ps[:, 4 + q % 3, :], WB[:, k, 512 + P * q:512 + P * q + P], hT[:, k, :],
                                   start=(k == 0), stop=(k == KD - 1))
                mm.then_inc(S("u_ssm_mm"), 1)

            def u_pool(t):
                for k in range(KD):
                    mm = pe.matmul(ps[:, t, :], hT[:, k, 256 + P * t:256 + P * t + P], WB[:, k, 0:512],
                                   start=(k == 0), stop=(k == KD - 1))
                mm.then_inc(S("u_pool_mm"), 1)

            pe.wait_ge(S("ht_ready"), KD)
            pe.wait_ge(S("ht_ready_dve"), KD)
            pe.wait_ge(S("win_ssm_in"), 16)
            turn_sa(1, 0)
            u_ssm(0)
            turn_sa(1, 1)
            lag_kernels()
            mod_chunk(1, 0, 7)
            u_ssm(1)
            mod_chunk(1, 1, 7)
            u_ssm(2)
            turn_kernels()
            u_ssm(3)
            mod_chunk(1, 2, 7)
            pe.wait_ge(S("kt_ready"), 2)
            pe.wait_ge(S("win_pool_in"), 16)
            u_pool(0)
            mod_chunk(1, 3, 7)

            pe.wait_ge(S("st_copy"), 16)
            pe.wait_ge(S("u8_in"), 16 * L)
            for n in range(8):
                h, d, r = n // 4, n // 2 % 2, n % 2
                if n < 3:
                    pe.wait_ge(S("u_ssm_ev"), (4, 2, 3)[n])
                else:
                    pe.wait_ge(S("s_ev"), n - 2)
                for g in range(8):
                    gpair = 8 * h + g
                    for a in range(2):
                        grp = 2 * gpair + a
                        mm = pe.matmul(ps[64 * a:64 * a + 64, 4 + n % 3, 64 * g:64 * g + 64],
                                       ST[:, d, r, gpair, 64 * a:64 * a + 64],
                                       U8[:, grp % 8, grp // 8].rearrange("p h c -> p (h c)"),
                                       start=True, stop=True, skip_group_check=True)
                mm.then_inc(S("s_mm"), 1)
                if n == 3:
                    mod_chunk(1, 4, 7)
            mod_chunk(1, 5, 7)
            u_pool(1)
            mod_chunk(1, 6, 7)
            mod_chunk(1, 7, 7)
            pe.wait_ge(S("pmat_in"), 16)
            pe.wait_ge(S("uP_copy"), NT)
            pe.wait_ge(S("mo_ready"), 1)
            for g in range(4):
                for t in range(NT):
                    at = 256 * (g % 2) + P * t
                    mm = pe.matmul(ps[:, 2 + g // 2, at:at + P], uP[:, t, P * g:P * g + P], pmat[:, g, :],
                                   start=True, stop=True, skip_group_check=True)
            mm.then_inc(S("window_mm"), 1)
            pe.wait_ge(S("s_ev"), 8)
            mod_turn(1, 6)
            pe.wait_ge(S("wpool_in"), 16)
            pe.wait_ge(S("pT_copy"), 1)
            for g in range(4):
                mm = pe.matmul(ps[:, g // 2, 256 * (g % 2):256 * (g % 2) + 256], wpool[:, g, :], pT[:, g, :],
                               start=True, stop=True, skip_group_check=True)
            mm.then_inc(S("pool_mm"), 1)

            pe.wait_ge(S("wo_pool_in"), 16)
            pe.wait_ge(S("cat_pool"), 1)
            for n in range(4):
                for k in range(4):
                    mm = pe.matmul(ps[:, n, :], cat[:, k, P * (n // 2):P * (n // 2) + P],
                                   wo_pool[:, k, 512 * (n % 2):512 * (n % 2) + 512], start=(k == 0), stop=False)
            mm.then_inc(S("mix_pool"), 1)

            pe.wait_ge(S("toep_in"), 16 * (2 * L - 1))
            for g in range(8):
                for q in range(4):
                    grp = 8 * q + g
                    pe.matmul(ps[32 * q:32 * q + 32, 4 + g % 2, 128 * (g // 2):128 * (g // 2) + 128], U8[:, g, q, 1, :],
                              TT[:, :, SG * grp:SG * grp + SG], start=(g < 2), stop=False, skip_group_check=True)
            def spread(v_r, j0, bank):
                for h in range(2):
                    j = j0 + h
                    mm = pe.matmul(ps[:, bank + h, :], ones[32 * j:32 * j + 1, :], modrow[32 * j:32 * j + 1, v_r, :],
                                   start=True, stop=True)
                mm.then_inc(S("spread_mm"), 1)

            pe.wait_ge(S("mod_col"), 2)
            spread(1, 0, 6)
            pe.wait_ge(S("hp_ready"), 1)
            for m in range(4):
                for d in range(2):
                    for r in range(2):
                        for q in range(4):
                            for a in range(2):
                                g = 2 * m + a
                                mm = pe.matmul(ps[32 * q:32 * q + 32, 4 + a, 128 * m:128 * m + 128],
                                               HP[64 * a:64 * a + 64, r, 16 * d + 4 * q + m, :],
                                               MO[64 * a:64 * a + 64, d, r, 4 * q + m, :],
                                               start=False, stop=(d == 1 and r == 1), skip_group_check=True)
            mm.then_inc(S("y_mm"), 1)
            pe.wait_ge(S("ysb_ready"), 1)
            for t in range(L):
                mm = pe.transpose(ps[:, 4 + t // 4, 128 * (t % 4):128 * (t % 4) + 128], ysb[:, P * t:P * t + P], ident)
            mm.then_inc(S("y_t"), 1)
            pe.wait_ge(S("wglu_in"), 16)
            for q in range(4):
                pe.wait_ge(S("gelu"), q + 1)
                if q == 0:
                    pe.wait_ge(S("ysum_ready"), 4)
                for m in range(4):
                    mm = pe.matmul(ps[:, 4 + m // 2, 256 * (m % 2):256 * (m % 2) + 256], wglu[:, q, P * m:P * m + P],
                                   G[:, q].rearrange("p t c -> p (t c)"), start=(q == 0 and m % 2 == 0), stop=(q == 3),
                                   skip_group_check=True)
                    if q == 3 and m % 2:
                        mm.then_inc(S("glu_mm"), 1)
            pe.wait_ge(S("wo_ssm_in"), 16)
            for n in range(4):
                for k in range(4):
                    if n == 0:
                        pe.wait_ge(S("cat_ssm"), k + 1)
                    mm = pe.matmul(ps[:, n, :], cat[:, 4 + k, P * (n // 2):P * (n // 2) + P],
                                   wo_ssm[:, k, 512 * (n % 2):512 * (n % 2) + 512], start=False, stop=(k == 3))
                mm.then_inc(S("mix_mm"), 1)
            pe.wait_ge(S("mod2_used"), KD)
            pe.wait_ge(S("sig_ready"), 4)
            for k in range(KD):
                mm = pe.matmul(ps[:, 5, k:k + 1], acc[:, P * k:P * k + P], ones[:, 0:1], start=True, stop=True,
                               skip_group_check=True)
            mm.then_inc(S("scale_mm"), 1)
            def start_outputs(t):
                pe.wait_ge(S("x2_ready"), t + 1)
                for n in (2 * t, 2 * t + 1):
                    pe.matmul(ps[:, n, :], ident, x2[:, t, 512 * (n % 2):512 * (n % 2) + 512], start=True, stop=False,
                              skip_group_check=True)

            pe.wait_ge(S("a2_ready"), 1)
            for t in range(NT):
                pe.wait_ge(S("xn2_ready"), t + 1)
                for k in range(KD):
                    if t == 0 and k == 4:
                        pe.wait_ge(S("g1_ready"), 1)
                    mm = pe.transpose(ps[:, 4 + k // 2, 256 * (k % 2) + P * t:256 * (k % 2) + P * t + P],
                                      xn2[:, t, P * k:P * k + P], ident)
                    if t == NT - 1:
                        mm.then_inc(S("h2_t"), 1)
                if t == 0:
                    start_outputs(0)
            pe.wait_ge(S("wr_in"), 16)
            pe.wait_ge(S("h2_ready_act"), 2)
            for n in range(KD):
                j = n % 4
                pe.wait_ge(S("h2_ready_act" if n < 4 else "h2_ready_dve"), j + 1)
                mm = pe.matmul(ps[32 * j:32 * j + 32, 4, 0:T], wrt[:, n, :], h2T[:, n, :], start=(n < 4), stop=(n >= 4))
            mm.then_inc(S("logit_mm"), 1)
            pe.wait_ge(S("h2_ready_act"), 4)
            pe.wait_ge(S("logit_copy"), 1)
            for t in range(NT):
                mm = pe.matmul(ps[:, 5, NE * t:NE * t + NE], lgT[:, P * t:P * t + P], stack4, start=True, stop=True,
                               skip_group_check=True)
            mm.then_inc(S("logit_sum"), 1)
            start_outputs(1)
            pe.wait_ge(S("h2_ready_dve"), 4)
            for h in range(2):
                j = 2 + h
                pe.matmul(ps[:, 6 + h, :], ones, acc[:, 1024 + 512 * h:1536 + 512 * h], start=True, stop=False)
                mm = pe.matmul(ps[:, 6 + h, :], ones[32 * j:32 * j + 1, :], modrow[32 * j:32 * j + 1, 2, :], start=False, stop=True)
            mm.then_inc(S("gate_mm"), 1)
            pe.wait_ge(S("score"), 1)
            pe.wait_ge(S("chosen"), 1)
            m0, m1 = msk[:, 0, :], msk[:, 1, :]
            counts = ps[:, 5, 0:3 * NE]
            pe.matmul(counts[:, 0:2 * NE], upper, msk.rearrange("p t e -> p (t e)"), start=True, stop=False, skip_group_check=True)
            pe.matmul(counts[:, NE:3 * NE], ones, m0.unsqueeze(1).broadcast_to([P, 2, NE]), start=False, stop=False,
                      skip_group_check=True)
            pe.matmul(counts[:, 2 * NE:3 * NE], ones, m1, start=False, stop=True, skip_group_check=True).then_inc(S("count_mm"), 1)

            def gather(h):
                for k in range(4):
                    c0 = 512 * h + P * k
                    for t in range(NT):
                        mm = pe.matmul(ps[:, 6 + h, P * k:P * k + P], xn2[:, t, c0:c0 + P], Pm[:, t].rearrange("p b s -> p (b s)"),
                                       start=(t == 0), stop=(t == NT - 1), skip_group_check=True)
                mm.then_inc(S("gather_mm"), 1)

            def scatter():
                for t in range(NT):
                    for h in range(2):
                        pe.matmul(ps[:, 2 * t + h, :], PT[:, P * t:P * t + P], oS[:, 512 * h:512 * h + 512], start=False,
                                  stop=False, skip_group_check=True)

            pe.wait_ge(S("g2_ready"), 1)
            pe.wait_ge(S("slots"), 1)
            gather(0)
            gather(1)
            pe.wait_ge(S("passes_ready"), 1)
            last_pair = pe.value_load(pairs[0:1, 0:1], min_val=NE // 2 - 1, max_val=2 * NE - 1)

            def pair(i, last):
                if last:
                    pe.wait_ge(S("out_copy"), 2 * i + 2)
                    pe.wait_ge(S("pt_copy"), i + 1)
                    scatter()
                for b in range(2):
                    pe.wait_ge(S("out_copy"), 2 * i + b + 1)
                    for k in range(KD):
                        if k % 4 == 0:
                            pe.wait_ge(S(f"gu_in{b}{k // 4}"), 32 * i + 32)
                            if b == 0:
                                pe.wait_ge(S("xm_ready"), 2 * i + k // 4 + 1)
                        st = xm[:, k, SLOTS * b:SLOTS * b + SLOTS]
                        pe.matmul(ps[0:64, 4 + b, :], st, Wg[b][:, k, :], start=(k == 0), stop=(k == KD - 1))
                        mm = pe.matmul(ps[64:128, 4 + b, :], st, Wu[b][:, k, :], start=(k == 0), stop=(k == KD - 1))
                        if k % 4 == 3:
                            mm.then_inc(S("gu_half"), 1)
                if not last:
                    pe.wait_ge(S("pt_copy"), i + 1)
                    scatter()
                for b in range(2):
                    pe.wait_ge(S("gu_copy"), 2 * i + b + 1)
                    for f in range(FC):
                        mm = pe.transpose(ps[:, 4 + b, P * f:P * f + P], gu[:, b, P * f:P * f + P], ident)
                    mm.then_inc(S("hid_turn"), 1)
                pe.wait_ge(S("gates"), i + 1)
                for t in range(NT):
                    mm = pe.transpose(ps[:, 7, P * t:P * t + P], PG[:, t].rearrange("p b s -> p (b s)"), ident)
                mm.then_inc(S("pt_turn"), 1)
                if not last:
                    pe.wait_ge(S("slots"), i + 2)
                    gather(0)
                    pe.wait_ge(S("pt_copy"), i + 2)
                    gather(1)
                pe.wait_ge(S("hid_ready"), 2 * i + 2)
                for h in range(2):
                    pe.wait_ge(S(f"down_in{h}"), 32 * i + 32)
                    for f in range(FC):
                        for b in range(2):
                            mm = pe.matmul(ps[64 * b:64 * b + 64, 4 + h, :], hid[:, b, f, :], Wd[b][:, f, 512 * h:512 * h + 512],
                                           start=(f == 0), stop=(f == FC - 1))
                    mm.then_inc(S("down_mm"), 1)

            with pe.Fori(0, last_pair) as i:
                pair(i, False)
            pair(last_pair, True)
            pe.wait_ge(S("out_copy"), 2 * last_pair + 4)
            pe.wait_ge(S("pt_copy"), last_pair + 2)
            for t in range(NT):
                for h in range(2):
                    mm = pe.matmul(ps[:, 2 * t + h, :], PT[:, P * t:P * t + P], oS[:, 512 * h:512 * h + 512], start=False,
                                   stop=True, skip_group_check=True)
                mm.then_inc(S("y_ready"), 1)

        @block.scalar
        def _(act):
            act.wait_ge(S("vec_in"), 16)
            act.wait_ge(S("sil_zero"), 1)
            act.activation(tv(T_DT), tv(T_LDT), ACT.Exp).then_inc(S("dt_ready"), 1)
            act.wait_ge(S("adt_ready"), 1)
            act.activation(tv(T_MAG), tv(T_ADT), ACT.Exp).then_inc(S("mag_ready"), 1)
            act.wait_ge(S("ang_ready"), 1)
            act.activation(tv(T_SIN), tv(T_ANG), ACT.Sin)
            act.activation(tv(T_SHF), tv(T_ANG), ACT.Sin, scale=0.5).then_inc(S("sin_ready"), 1)
            act.activation(silc[:, :, 0:2].rearrange("p k q -> p q k"), vt[:, V_C:V_C + 16].rearrange("p (q k) -> p q k", q=2),
                           ACT.Silu).then_inc(S("sil_ready"), 1)
            for t in range(4):
                act.wait_ge(S(f"x_in{t}"), 16)
                if t:
                    act.wait_ge(S("ss_ready"), t)
                act.activation(hT[:, 0:2, :], xc[:, t, :].rearrange("p (a b) -> p a b", a=2), ACT.Square, accum_out=ms[:, t:t + 1]).then_inc(S("ss_ready"), 1)
            for t in range(4):
                act.wait_ge(S("rstd_ready"), t + 1)
                act.mul(xc[:, t, :], xc[:, t, :], rstd[:, t:t + 1]).then_inc(S("xn_ready"), 1)

            def copy_st(d, r):
                for n in range(8 * d + 4 * r, 8 * d + 4 * r + 4):
                    act.wait_ge(S("sa_t"), n + 1)
                    act.copy(ST[:, d, r, 4 * (n % 4):4 * (n % 4) + 4, :],
                             ps[:, (n + 1) % 2, :].rearrange("p (g m) -> p g m", g=4)).then_inc(S("st_copy"), 1)

            copy_st(0, 0)
            copy_st(0, 1)

            def mod_rows(r, bank):
                act.wait_ge(S("mod_used"), KD * (r + 1))
                act.copy(modrow[:, r, :], ps[:, bank, :]).then_inc(S("modrow"), 1)

            def mod_columns(r, bank):
                act.wait_ge(S("mod_t"), r + 1)
                v = ps[:, bank, :].rearrange("p (b j m) -> p b j m", b=4, j=4)[:, :, :, 0:2]
                o = mcol[:, 32 * r:32 * r + 32].rearrange("p (j b q) -> p b j q", j=4, b=4)
                act.copy(o, v).then_inc(S("mod_col"), 1)

            mod_rows(0, 4)
            mod_columns(0, 0)
            act.wait_ge(S("a1_ready"), 1)
            for k in range(0, KD, 2):
                act.wait_ge(S("x_t"), k + 1)
                for q in (1, 0):
                    act.activation(hT[:, k, 256 * (1 - q):256 * (2 - q)], ps[:, (k + 1) % 2, 256 * (1 - q):256 * (2 - q)],
                                   ACT.Identity, bias=MC[:, 0, k, q:q + 1], scale=A1[:, k, q:q + 1]).then_inc(S("ht_ready"), 1)

            def u_evacuate(q):
                act.wait_ge(S("u_ssm_mm"), q + 1)
                for h in range(2):
                    mm = act.copy(UTs[:, :, q, h, :], ps[:, 4 + q % 3, 256 * h:256 * h + 256].rearrange("p (c s) -> p s c", s=L))
                mm.then_inc(S("u_ssm_ev"), 1)
                act.wait_ge(S("u_ssm_ev"), q + 1)
                act.dma_start(u_dram.rearrange("p (s q n) -> p s q n", s=L, q=4)[:, :, q],
                              ut[:, :].rearrange("p (s q n) -> p s q n", s=L, q=4)[:, :, q]).then_inc(S("u_out"), 16)

            act.wait_ge(S("bbar_ready"), 1)
            copy_st(1, 0)
            u_evacuate(0)
            copy_st(1, 1)
            u_evacuate(1)
            u_evacuate(2)
            for d in range(2):
                act.wait_ge(S("kt_t"), d + 1)
                act.copy(KT[:, d, :], ps[:, d, :]).then_inc(S("kt_ready"), 1)
            u_evacuate(3)

            def up_copy(t):
                act.wait_ge(S("u_pool_mm"), t + 1)
                act.copy(uP[:, t, :], ps[:, t, :]).then_inc(S("uP_copy"), 1)

            up_copy(0)
            for n in range(8):
                act.wait_ge(S("s_mm"), n + 1)
                h, d, r = n // 4, n // 2 % 2, n % 2
                v = ps[:, 4 + n % 3, :].rearrange("p (g n) -> p g n", g=8)
                at = 32 * r + 16 * d + 8 * h
                dst = SSv[:, :, at:at + 8].rearrange("p n g -> p g n")
                if d == 0:
                    mm = act.copy(dst, v)
                else:
                    act.copy(dst[:, :, 0:NC], v[:, :, 0:NC][:, :, ::-1])
                    mm = act.copy(dst[:, :, NC:2 * NC], v[:, :, NC:2 * NC][:, :, ::-1])
                mm.then_inc(S("s_ev"), 1)
            up_copy(1)
            mod_rows(1, 7)
            act.wait_ge(S("window_mm"), 1)
            act.copy(pT, ps[:, 2:4, :].rearrange("p a (g t) -> p (a g) t", g=2)).then_inc(S("pT_copy"), 1)
            mod_columns(1, 6)
            act.wait_ge(S("pool_mm"), 1)
            for g in range(4):
                mm = act.activation(cat[:, g, :], ps[:, g // 2, 256 * (g % 2):256 * (g % 2) + 256], ACT.Copy,
                                    scale=vt[:, V_SP + g:V_SP + g + 1])
            mm.then_inc(S("cat_pool"), 1)
            act.wait_ge(S("spread_mm"), 1)
            act.copy(g1b, ps[:, 6:8, :].rearrange("p a n -> p (a n)")).then_inc(S("g1_ready"), 1)
            act.wait_ge(S("y_mm"), 1)
            for a in range(2):
                mm = act.copy(ysb.rearrange("p (t g a i) -> p a g t i", g=4, a=2, t=L)[:, a],
                              ps[:, 4 + a, :].rearrange("p (g t i) -> p g t i", g=4, t=L))
            mm.then_inc(S("ysb_ready"), 1)
            for q in range(4):
                act.wait_ge(S("ysum_ready"), q + 1)
                act.activation(G[:, q], ysum[:, q], ACT.Gelu_apprx_tanh).then_inc(S("gelu"), 1)
            for m in range(4):
                act.wait_ge(S("glu_mm"), m // 2 + 1)
                act.activation(sg[:, m], ps[:, 4 + m // 2, 256 * (m % 2):256 * (m % 2) + 256].rearrange("p (t c) -> p t c", t=L),
                               ACT.Sigmoid, bias=vt[:, V_BG + m:V_BG + m + 1]).then_inc(S("sig_ready"), 1)
            for t in range(NT):
                act.wait_ge(S("x2_ready"), t + 1)
                if t:
                    act.wait_ge(S("ss2_ready"), t)
                act.activation(ra[:, 4096:5120], x2[:, t, :], ACT.Square, accum_out=ms2[:, t:t + 1]).then_inc(S("ss2_ready"), 1)
            act.wait_ge(S("a2_ready"), 1)
            for k in range(KD // 2):
                act.wait_ge(S("h2_t"), 2 * (k // 2) + 2)
                act.activation(h2T[:, k, :], ps[:, 4 + k // 2, 256 * (k % 2):256 * (k % 2) + 256], ACT.Identity,
                               bias=MC[:, 3, k, 0:1], scale=A2[:, k:k + 1]).then_inc(S("h2_ready_act"), 1)
            act.wait_ge(S("logit_mm"), 1)
            act.copy(lgT, ps[:, 4, 0:T]).then_inc(S("logit_copy"), 1)
            act.wait_ge(S("logit_sum"), 1)
            act.activation(sc.rearrange("p t e -> p (t e)"), ps[:, 5, 0:2 * NE], ACT.Sigmoid).then_inc(S("score"), 1)
            act.wait_ge(S("gate_mm"), 1)
            act.copy(g2b, ps[:, 6:8, :].rearrange("p a n -> p (a n)")).then_inc(S("g2_ready"), 1)
            act.wait_ge(S("passes_ready"), 1)
            last_pair = act.value_load(pairs[0:1, 0:1], min_val=NE // 2 - 1, max_val=2 * NE - 1)
            act.wait_ge(S("zeroed"), 1)
            act.sem_inc(S("pt_copy"), 1)
            with act.Fori(0, last_pair + 1) as i:
                for b in range(2):
                    act.wait_ge(S("gu_half"), 4 * i + 2 * b + 2)
                    act.copy(gu[:, b, :], ps[:, 4 + b, :]).then_inc(S("gu_copy"), 1)
                for b in range(2):
                    act.wait_ge(S("hid_turn"), 2 * i + b + 1)
                    act.activation(silg[:, b], ps[:, 4 + b, :].rearrange("p (f n) -> p f n", f=FC)[:, :, 0:SLOTS],
                                   ACT.Silu).then_inc(S("silg_ready"), 1)
                act.wait_ge(S("pt_turn"), i + 1)
                act.copy(PT, ps[:, 7, 0:T]).then_inc(S("pt_copy"), 1)
            for t in range(NT):
                act.wait_ge(S("y_ready"), t + 1)
                if t:
                    act.wait_ge(S("ss3_ready"), t)
                act.activation(ra[:, 4096:5120], ps[:, 2 * t:2 * t + 2, :].rearrange("p a n -> p (a n)"), ACT.Square,
                               accum_out=ms2[:, 2 + t:3 + t]).then_inc(S("ss3_ready"), 1)

        @block.vector
        def _(dve):
            chain = [0]

            def link(ins):
                chain[0] += 1
                ins.then_inc(S("dve_link"), 1)
                dve.wait_ge(S("dve_link"), chain[0])

            def tt(o, a, b, op):
                return dve.tensor_tensor(o, a, b, op)

            dve.memset(sil[:, :], 0.0).then_inc(S("sil_zero"), 1)
            dve.memset(mhalf, -0.5).then_inc(S("mhalf_set"), 1)
            dve.wait_ge(S("vec_in"), 16)
            link(dve.tensor_scalar(tv(T_ARE), tv(T_ARE), -1e-4, None, ALU.min))
            dve.wait_ge(S("dt_ready"), 1)
            tt(tv(T_ADT), tv(T_ARE), tv(T_DT), ALU.mult).then_inc(S("adt_ready"), 1)
            link(tt(tv(T_TH), tv(T_AIM), tv(T_DT), ALU.mult))
            link(dve.tensor_scalar(tv(T_K), tv(T_TH), 1.0 / TWO_PI, MAGIC, ALU.mult, ALU.add))
            link(dve.tensor_scalar(tv(T_K), tv(T_K), -MAGIC, None, ALU.add))
            for part in (PI_A, PI_B, PI_C):
                link(dve.scalar_tensor_tensor(tv(T_TH), tv(T_K), -part, tv(T_TH), ALU.mult, ALU.add))
            dve.tensor_scalar(tv(T_ANG), tv(T_TH), 3.1415925, -3.1415925, ALU.min, ALU.max).then_inc(S("ang_ready"), 1)
            link(tt(tv(T_D1), tv(T_ARE), tv(T_ARE), ALU.mult))
            link(tt(tv(T_D2), tv(T_AIM), tv(T_AIM), ALU.mult))
            link(tt(tv(T_D1), tv(T_D1), tv(T_D2), ALU.add))
            link(dve.reciprocal(tv(T_D1), tv(T_D1)))
            dve.wait_ge(S("mag_ready"), 1)
            dve.wait_ge(S("sin_ready"), 1)
            link(tt(tv(T_D2), tv(T_SHF), tv(T_SHF), ALU.mult))
            link(dve.tensor_scalar(tv(T_D2), tv(T_D2), -2.0, 1.0, ALU.mult, ALU.add))
            link(dve.memset(LP[:, 0, 0, :], 1.0))
            link(dve.memset(LP[:, 0, 1, :], 0.0))
            link(tt(LP[:, 1, 0, :], tv(T_MAG), tv(T_D2), ALU.mult))
            link(tt(LP[:, 1, 1, :], tv(T_MAG), tv(T_SIN), ALU.mult))
            link(dve.tensor_scalar(tv(T_K), LP[:, 1, 0, :], -1.0, None, ALU.add))
            link(tt(tv(T_T1), tv(T_K), tv(T_ARE), ALU.mult))
            link(tt(tv(T_T2), LP[:, 1, 1, :], tv(T_AIM), ALU.mult))
            link(tt(tv(T_T1), tv(T_T1), tv(T_T2), ALU.add))
            link(tt(tv(T_KR), tv(T_T1), tv(T_D1), ALU.mult))
            link(tt(tv(T_T1), LP[:, 1, 1, :], tv(T_ARE), ALU.mult))
            link(tt(tv(T_T2), tv(T_K), tv(T_AIM), ALU.mult))
            link(tt(tv(T_T1), tv(T_T1), tv(T_T2), ALU.subtract))
            link(tt(tv(T_KI), tv(T_T1), tv(T_D1), ALU.mult))
            for lo, n in ((1, 1), (2, 2), (4, 4)):
                a_r, a_i = LP[:, 1:1 + n, 0, :], LP[:, 1:1 + n, 1, :]
                b_r = LP[:, lo, 0, :].unsqueeze(1).broadcast_to([P, n, DG])
                b_i = LP[:, lo, 1, :].unsqueeze(1).broadcast_to([P, n, DG])
                o_r, o_i = LP[:, lo + 1:lo + 1 + n, 0, :], LP[:, lo + 1:lo + 1 + n, 1, :]
                t = ps[:, 2, 0:n * DG].rearrange("p (n g) -> p n g", n=n)
                u = ps[:, 2, 256:256 + n * DG].rearrange("p (n g) -> p n g", n=n)
                tt(o_r, a_r, b_r, ALU.mult)
                tt(o_i, a_r, b_i, ALU.mult)
                tt(t, a_i, b_i, ALU.mult)
                link(tt(u, a_i, b_r, ALU.mult))
                tt(o_r, o_r, t, ALU.subtract)
                link(tt(o_i, o_i, u, ALU.add))
            LPv = LP.rearrange("p k r (d g) -> p d r g k", d=2)
            for r in range(2):
                dve.tensor_copy(PW[:, 0, r], LPv[:, 0, r, :, 0:L][:, :, ::-1])
                link(dve.tensor_copy(PW[:, 1, r], LPv[:, 1, r, :, 0:L]))

            dve.wait_ge(S("bc_in"), 16)

            for d in range(2):
                kr = tv(T_KR)[:, 16 * d:16 * d + 16].unsqueeze(2).broadcast_to([P, GP, SG])
                ki = tv(T_KI)[:, 16 * d:16 * d + 16].unsqueeze(2).broadcast_to([P, GP, SG])
                br_, bi_ = Br[:, d, 0], Br[:, d, 1]
                t = ps[:, 2, 0:256].rearrange("p (g j) -> p g j", g=GP)
                u = ps[:, 2, 256:512].rearrange("p (g j) -> p g j", g=GP)
                tt(t, bi_, ki, ALU.mult)
                link(tt(u, br_, ki, ALU.mult))
                tt(br_, br_, kr, ALU.mult)
                link(tt(bi_, bi_, kr, ALU.mult))
                tt(br_, br_, t, ALU.subtract)
                link(tt(bi_, bi_, u, ALU.add))
            dve.sem_inc(S("bbar_ready"), 1)

            def powers_times(dst, pw, m, r, sign_im, done, between=None):
                for d in range(2):
                    for rr in r:
                        for h in range(2):
                            if between and (d, rr, h) == (1, 1, 1):
                                between()
                            g = slice(8 * h, 8 * h + 8)
                            pr = pw[:, d, 0, g].unsqueeze(3).broadcast_to([P, 8, L, SG])
                            pi = pw[:, d, 1, g].unsqueeze(3).broadcast_to([P, 8, L, SG])
                            mr_ = m[:, d, 0, g].unsqueeze(2).broadcast_to([P, 8, L, SG])
                            mi_ = m[:, d, 1, g].unsqueeze(2).broadcast_to([P, 8, L, SG])
                            o = dst[:, d, rr, g]
                            t = ps[:, 2:4, :].rearrange("p a (g s j) -> p (a g) s j", g=4, s=L)
                            if rr == 0:
                                tt(o, pr, mr_, ALU.mult)
                                link(tt(t, pi, mi_, ALU.mult))
                                ins = tt(o, o, t, ALU.subtract)
                            else:
                                tt(o, pr, mi_, ALU.mult)
                                link(tt(t, pi, mr_, ALU.mult))
                                if sign_im > 0:
                                    ins = tt(o, o, t, ALU.add)
                                else:
                                    ins = dve.scalar_tensor_tensor(o.rearrange("p g s j -> p (g s j)"), o.rearrange("p g s j -> p (g s j)"), -1.0,
                                                                   t.rearrange("p g s j -> p (g s j)"), ALU.mult, ALU.subtract)
                            if h == 0:
                                link(ins)
                        ins.then_inc(S(done), 1)
                        dve.wait_ge(S(done), 2 * d + rr + 1)

            def modulate_tokens():
                dve.wait_ge(S("a1_ready"), 1)
                for k in range(1, KD, 2):
                    dve.wait_ge(S("x_t"), k + 1)
                    for q in (1, 0):
                        dve.tensor_scalar(hT[:, k, 256 * (1 - q):256 * (2 - q)], ps[:, (k + 1) % 2, 256 * (1 - q):256 * (2 - q)],
                                          A1[:, k, q:q + 1], MC[:, 0, k, q:q + 1], ALU.mult, ALU.add).then_inc(S("ht_ready_dve"), 1)

            powers_times(SA, PW, Br, (0, 1), 1, "sa_ready", modulate_tokens)

            dve.wait_ge(S("x_t"), KD)
            pw_re = [cb[:, 512 + 128 * k:576 + 128 * k] for k in range(4)] + [ra[:, 3584:3648], ra[:, 3712:3776]]
            pw_im = [cb[:, 576 + 128 * k:640 + 128 * k] for k in range(4)] + [ra[:, 3648:3712], ra[:, 3776:3840]]
            pr, pi = LP[:, 8, 0, :], LP[:, 8, 1, :]
            for k in range(6):
                if k:
                    a_r, a_i = pw_re[k - 1][:, 0:32], pw_im[k - 1][:, 32:64]
                    m_r, m_i = (LP[:, 8, 0, :], LP[:, 8, 1, :]) if k < 4 else (a_r, a_i)
                    tt(tmp32[0], a_r, m_r, ALU.mult)
                    tt(tmp32[1], a_i, m_i, ALU.mult)
                    tt(tmp32[2], a_r, m_i, ALU.mult)
                    link(tt(tmp32[3], a_i, m_r, ALU.mult))
                    tt(tmp32[0], tmp32[0], tmp32[1], ALU.subtract)
                    link(tt(tmp32[2], tmp32[2], tmp32[3], ALU.add))
                    pr, pi = tmp32[0], tmp32[2]
                dve.tensor_copy(pw_re[k][:, 0:32], pr)
                dve.tensor_copy(pw_re[k][:, 32:64], pr)
                dve.tensor_scalar(pw_im[k][:, 0:32], pi, -1.0, None, ALU.mult)
                link(dve.tensor_copy(pw_im[k][:, 32:64], pi))

            for d in range(2):
                dve.wait_ge(S("kk_mm"), d + 1)
                link(dve.tensor_copy(KS[:, d].rearrange("p q s j -> p (q s j)"), ps[:, d, :]))
                if d == 0:
                    dve.sem_inc(S("ks_ready"), 1)
            tt(KS[:, 1, :, 0, :], KS[:, 1, :, 0, :], KS[:, 0, :, L - 1, :], ALU.add).then_inc(S("ks_ready"), 1)

            for r in range(2):
                dve.tensor_copy(PW[:, 0, r], LPv[:, 0, r, :, 1:L + 1])
                link(dve.tensor_copy(PW[:, 1, r], LPv[:, 1, r, :, 1:L + 1][:, :, ::-1]))
            dve.wait_ge(S("sa_t"), 16)
            powers_times(MO.rearrange("p d r g (s j) -> p d r g s j", s=L), PW, CT, (0, 1), -1, "mo_half")
            dve.wait_ge(S("mo_half"), 4)
            dve.sem_inc(S("mo_ready"), 1)

            def half(v, h):
                return v.rearrange("p n (x h g) -> p n x h g", x=4, h=2)[:, :, :, h, :]

            def factor(v, h, n):
                return v.rearrange("p (x h g) -> p x h g", x=4, h=2)[:, :, h, :].unsqueeze(1).broadcast_to([P, n, 4, 8])

            def advance(steps, h):
                views = []
                for prev, cur, k, n, a, b in steps:
                    pv, cv = half(prev, h), half(cur, h)
                    av = a[:, 0:32 * n].rearrange("p (n x g) -> p n x g", n=n, x=4)
                    bv = b[:, 0:32 * n].rearrange("p (n x g) -> p n x g", n=n, x=4)
                    fi = factor(pw_im[k], h, n)
                    for r in range(2):
                        tt(bv[:, :, 2 * r:2 * r + 2], pv[:, :, 2 * (1 - r):2 * (1 - r) + 2], fi[:, :, 2 * r:2 * r + 2], ALU.mult)
                    ins = tt(av, pv, factor(pw_re[k], h, n), ALU.mult)
                    views.append((av, bv, cv))
                link(ins)
                for av, bv, cv in views:
                    ins = tt(av, av, cv, ALU.add)
                link(ins)
                for av, bv, cv in views:
                    ins = tt(cv, av, bv, ALU.add)
                link(ins)

            S4 = SSv.rearrange("p (b k) w -> p k b w", k=4)
            for h in range(2):
                dve.wait_ge(S("s_ev"), 4 * h + 4)
                for lv in range(5):
                    n, st = 16 >> lv, 1 << lv
                    steps = [(SSv[:, st - 1:32:2 * st], SSv[:, 2 * st - 1:32:2 * st], (0, 1, 3, 4, 5)[lv], n, tA, tB)]
                    if lv < 3:
                        steps.append((S4[:, lv, 8:16], S4[:, lv + 1, 8:16], 0, 8, tC, tD))
                    advance(steps, h)

            def pair(v):
                return v.rearrange("p n (r g) -> p n r g", r=2)

            dve.wait_ge(S("s_mm"), 8)
            Ev = E.rearrange("p (n w) -> p n w", w=64)
            link(dve.tensor_copy(Ev[:, 0], SSv[:, 31]))
            for n in range(7):
                prev = Ev[:, n]
                tt(tB[:, 0:64].rearrange("p (r g) -> p r g", r=2), prev.rearrange("p (r g) -> p r g", r=2)[:, ::-1, :],
                   pw_im[3].rearrange("p (r g) -> p r g", r=2), ALU.mult)
                link(tt(tA[:, 0:64], prev, pw_re[3], ALU.mult))
                link(tt(tA[:, 0:64], tA[:, 0:64], S4[:, 3, 8 + n], ALU.add))
                link(tt(Ev[:, n + 1], tA[:, 0:64], tB[:, 0:64], ALU.add))
            dve.wait_ge(S("toep_in"), 16 * (2 * L - 1))
            HPd = [HP[:, :, 0:16, :].rearrange("p r g (b k) -> p k b r g", k=4),
                   HP[:, :, 16:32, ::-1].rearrange("p r g (b k) -> p k b r g", k=4)]
            a8, b8 = tA.rearrange("p (n w) -> p n w", w=64), tB.rearrange("p (n w) -> p n w", w=64)
            for k in range(4):
                if k == 0:
                    for d in range(2):
                        ins = dve.tensor_copy(HPd[d][:, 0], pair(Ev)[:, :, :, 16 * d:16 * d + 16])
                    continue
                for r in range(2):
                    tt(b8[:, :, 32 * r:32 * r + 32], Ev[:, :, 32 * (1 - r):32 * (1 - r) + 32],
                       pw_im[k - 1][:, 32 * r:32 * r + 32].unsqueeze(1).broadcast_to([P, 8, 32]), ALU.mult)
                link(tt(a8, Ev, pw_re[k - 1].unsqueeze(1).broadcast_to([P, 8, 64]), ALU.mult))
                link(tt(a8, a8, S4[:, k - 1, 8:16], ALU.add))
                for d in range(2):
                    ins = tt(HPd[d][:, k], pair(a8)[:, :, :, 16 * d:16 * d + 16], pair(b8)[:, :, :, 16 * d:16 * d + 16], ALU.add)
                if k < 3:
                    link(ins)
            ins.then_inc(S("hp_ready"), 1)

            def mod_sum(k):
                n = 2 * KD + k
                dve.wait_ge(S(f"wmod_in{n % 3}"), 16 * (n // 3 + 1))
                w = silc[:, k, 0:1]
                if k == 0:
                    dve.tensor_scalar(acc, wm[n % 3], w, None, ALU.mult).then_inc(S("mod2_used"), 1)
                else:
                    dve.wait_ge(S("mod2_used"), k)
                    dve.scalar_tensor_tensor(acc, wm[n % 3], w, acc, ALU.mult, ALU.add).then_inc(S("mod2_used"), 1)

            dve.wait_ge(S("window_mm"), 1)
            dve.wait_ge(S("hp_ready"), 1)
            for k in range(3):
                mod_sum(k)

            dve.wait_ge(S("y_t"), 1)
            yv = ps[:, 4:6, :].rearrange("p a (t q c) -> p q (a t) c", t=4, q=4)
            for q in range(4):
                dve.scalar_tensor_tensor(ysum[:, q], UTs[:, :, q, 1, :], vt[:, V_D + q:V_D + q + 1], yv[:, q],
                                         ALU.mult, ALU.add).then_inc(S("ysum_ready"), 1)
            for k in range(3, 6):
                mod_sum(k)
            for m in range(4):
                dve.wait_ge(S("sig_ready"), m + 1)
                tt(cat[:, 4 + m, :].rearrange("p (c t) -> p t c", t=L), G[:, m], sg[:, m], ALU.mult).then_inc(S("cat_ssm"), 1)

            for k in range(6, KD):
                mod_sum(k)

            dve.wait_ge(S("g1_ready"), 1)

            def residual(t, at, n):
                tmp = ra[:, 5120 + 1024 * t + at:5120 + 1024 * t + at + n]
                v = ps[:, 2 * t:2 * t + 2, :].rearrange("p a n -> p (a n)")[:, at:at + n]
                link(tt(tmp, v, g1b[:, at:at + n], ALU.mult))
                return tt(x2[:, t, at:at + n], x2[:, t, at:at + n], tmp, ALU.add)

            def norm(t):
                dve.wait_ge(S("ss2_ready"), t + 1)
                dve.tensor_scalar(ms2[:, t:t + 1], ms2[:, t:t + 1], 1.0 / D, EPS, ALU.mult, ALU.add).then_inc(S("ms2_ready"), 1)
                dve.wait_ge(S("rstd2_ready"), t + 1)
                dve.tensor_scalar(xn2[:, t, :], x2[:, t, :], rstd2[:, t:t + 1], None, ALU.mult).then_inc(S("xn2_ready"), 1)

            dve.wait_ge(S("mix_mm"), 2)
            dve.wait_ge(S("xres_in0"), 16)
            residual(0, 0, D).then_inc(S("x2_ready"), 1)
            norm(0)
            dve.wait_ge(S("mix_mm"), 3)
            dve.wait_ge(S("xres_in1"), 16)
            link(residual(1, 0, 512))
            dve.wait_ge(S("mix_mm"), 4)
            residual(1, 512, 512).then_inc(S("x2_ready"), 1)
            dve.wait_ge(S("scale_mm"), 1)
            dve.tensor_copy(sh2, MC[:, 3, :, 0]).then_inc(S("sh2_ready"), 1)
            link(tt(A2, ps[:, 5, 0:KD], vt[:, V_B2:V_B2 + KD], ALU.add))
            dve.scalar_tensor_tensor(A2, A2, 1.0, vt[:, V_GF:V_GF + 8], ALU.add, ALU.mult).then_inc(S("a2_ready"), 1)
            norm(1)
            dve.wait_ge(S("a2_ready"), 1)
            dve.wait_ge(S("sh2_ready"), 1)
            for k in range(KD // 2, KD):
                dve.wait_ge(S("h2_t"), 2 * (k // 2) + 2)
                dve.tensor_scalar(h2T[:, k, :], ps[:, 4 + k // 2, 256 * (k % 2):256 * (k % 2) + 256], A2[:, k:k + 1], sh2[:, k:k + 1], ALU.mult,
                                  ALU.add).then_inc(S("h2_ready_dve"), 1)

            link(dve.tensor_scalar(rank, iota[:, 0:NE], -1.0, float(NE), ALU.mult, ALU.add))
            dve.wait_ge(S("br_in"), 16)
            dve.wait_ge(S("score"), 1)
            link(tt(sel, sc, brb.unsqueeze(1).broadcast_to([P, NT, NE]), ALU.add))
            for t in range(NT):
                for g in range(NGRP):
                    ins = dve.max(top8[:, t, g, :], sel[:, t, EPG * g:EPG * g + EPG])
            link(ins)
            link(tt(gs, top8[:, :, :, 0], top8[:, :, :, 1], ALU.add))

            def first_best(dst, score, rank, n):
                link(dve.tensor_reduce(best, score, AX.X, ALU.max))
                for t in range(NT):
                    ins = dve.scalar_tensor_tensor(dst[:, t], score[:, t], best[:, t:t + 1], rank, ALU.is_equal, ALU.mult)
                link(ins)
                link(dve.tensor_reduce(best, dst, AX.X, ALU.max))
                link(tt(dst, dst, best.unsqueeze(2).broadcast_to([P, NT, n]), ALU.is_equal))

            first_best(gm, gs, rank[:, 0:NGRP], NGRP)
            gmx = gm.unsqueeze(3).broadcast_to([P, NT, NGRP, EPG])
            sel4 = sel.rearrange("p t (g e) -> p t g e", g=NGRP)
            link(tt(sel4, sel4, gmx, ALU.mult))
            link(dve.tensor_scalar(gm, gm, HUGE, -HUGE, ALU.mult, ALU.add))
            link(tt(sel4, sel4, gmx, ALU.add))
            first_best(one1, sel, rank, NE)
            link(dve.scalar_tensor_tensor(sel.rearrange("p t e -> p (t e)"), one1.rearrange("p t e -> p (t e)"), -HUGE * 4,
                                          sel.rearrange("p t e -> p (t e)"), ALU.mult, ALU.add))
            first_best(one2, sel, rank, NE)
            tt(msk, one1, one2, ALU.add).then_inc(S("chosen"), 1)
            dve.wait_ge(S("chosen"), 1)
            link(tt(gw, msk, sc, ALU.mult))
            link(dve.tensor_reduce(best, gw, AX.X, ALU.add))
            link(dve.reciprocal(best, best))
            link(tt(gw, gw, best.unsqueeze(2).broadcast_to([P, NT, NE]), ALU.mult))
            iota4 = iota.rearrange("p (b s) -> p b s", b=2).unsqueeze(1).broadcast_to([P, NT, 2, SLOTS])

            def columns(v, at):
                return v[:, :, at].unsqueeze(3).broadcast_to([P, NT, 2, SLOTS])

            def modulate(n):
                for h in range(2):
                    k = slice(4 * h, 4 * h + 4)
                    dve.wait_ge(S("gather_mm"), n + h + 1)
                    tt(xm[:, k], ps[:, 6 + h, :].rearrange("p (k s) -> p k s", k=4),
                       A2[:, k].unsqueeze(2).broadcast_to([P, 4, 2 * SLOTS]), ALU.mult).then_inc(S("xm_scaled"), 1)
                    dve.wait_ge(S("xm_scaled"), n + h + 1)
                    tt(xm[:, k], xm[:, k], sh2[:, k].unsqueeze(2).broadcast_to([P, 4, 2 * SLOTS]), ALU.add).then_inc(S("xm_ready"), 1)

            link(dve.tensor_scalar(sel, msk, -BIG, BIG, ALU.mult, ALU.add))
            dve.wait_ge(S("count_mm"), 1)
            link(tt(posx[:, :, 0:NE], sel, ps[:, 5, 0:2 * NE].rearrange("p (t e) -> p t e", t=NT), ALU.add))
            dve.wait_ge(S("gate_mm"), 1)
            tt(Pm, iota4, columns(posx, slice(0, 2)), ALU.is_equal).then_inc(S("slots"), 1)
            dve.memset(PT, 0.0)
            link(dve.memset(oS, 0.0))
            dve.sem_inc(S("zeroed"), 1)
            for n in range(4):
                if n:
                    dve.tensor_scalar(posx[:, :, NE * n:NE * n + NE], posx[:, :, 0:NE], float(-SLOTS * n), None, ALU.add)
                dve.tensor_copy(wx[:, :, NE * n:NE * n + NE], gw)
            dve.memset(posx[:, :, 4 * NE:NCOL], BIG)
            link(dve.memset(wx[:, :, 4 * NE:NCOL], 0.0))
            link(dve.tensor_reduce(best[:, 0:1], ps[:, 5, 2 * NE:3 * NE], AX.X, ALU.max))
            link(dve.tensor_scalar(best[:, 1:2], best[:, 0:1], float(SLOTS), None, ALU.is_gt))
            for n in (2, 3):
                link(dve.tensor_scalar(pcount, best[:, 0:1], float(SLOTS * n), None, ALU.is_gt))
                link(tt(best[:, 1:2], best[:, 1:2], pcount, ALU.add))
            dve.tensor_scalar(pairs[:, 0:1], best[:, 1:2], float(NE // 2), float(NE // 2 - 1), ALU.mult, ALU.add).then_inc(S("passes_ready"), 1)
            modulate(0)
            dve.wait_ge(S("passes_ready"), 1)
            last_pair = dve.value_load(pairs[0:1, 0:1], min_val=NE // 2 - 1, max_val=2 * NE - 1)
            def pair_slots(i, last):
                tt(PG, iota4, columns(posx, bass.ds(2 * i, 2)), ALU.is_equal).then_inc(S("onehot"), 1)
                if not last:
                    tt(Pm, iota4, columns(posx, bass.ds(2 * i + 2, 2)), ALU.is_equal).then_inc(S("slots"), 1)
                dve.wait_ge(S("onehot"), i + 1)
                tt(PG, PG, columns(wx, bass.ds(2 * i, 2)), ALU.mult).then_inc(S("gates"), 1)

            def pair_hidden(i):
                for b in range(2):
                    dve.wait_ge(S("silg_ready"), 2 * i + b + 1)
                    tt(hid[:, b], silg[:, b], ps[:, 4 + b, :].rearrange("p (f n) -> p f n", f=FC)[:, :, SLOTS:2 * SLOTS],
                       ALU.mult).then_inc(S("hid_ready"), 1)

            def pair_out(i):
                for h in range(2):
                    dve.wait_ge(S("down_mm"), 2 * i + h + 1)
                    tt(oS[:, 512 * h:512 * h + 512], ps[:, 4 + h, :], g2b[:, 512 * h:512 * h + 512], ALU.mult).then_inc(S("out_copy"), 1)

            dve.sem_inc(S("out_copy"), 2)
            dve.wait_ge(S("g2_ready"), 1)
            with dve.Fori(0, last_pair) as i:
                pair_slots(i, False)
                pair_hidden(i)
                modulate(2 * i + 2)
                pair_out(i)
            pair_slots(last_pair, True)
            pair_hidden(last_pair)
            pair_out(last_pair)

            dve.wait_ge(S("gf_in"), 16)
            for t in range(NT):
                dve.wait_ge(S("ss3_ready"), t + 1)
                dve.tensor_scalar(ms2[:, 2 + t:3 + t], ms2[:, 2 + t:3 + t], 1.0 / D, EPS, ALU.mult, ALU.add).then_inc(S("ms2_ready"), 1)
                dve.wait_ge(S("rstd2_ready"), 3 + t)
                for h in range(2):
                    c0 = slice(512 * h, 512 * h + 512)
                    dve.scalar_tensor_tensor(xn2[:, t, c0], ps[:, 2 * t + h, :], rstd2[:, 2 + t:3 + t], gfb[:, c0],
                                             ALU.mult, ALU.mult).then_inc(S("fin_ready"), 1)


_AS_THEY_COME = ("x", "ctx", "w_mod", "w_in", "w_out", "w_pool", "w_glu", "w_router", "b_router", "w_gate", "w_up",
                 "w_down", "g_final")
_ORDER = ("x", "ctx", "w_mod", "columns", "ssm_bc", "b_mod_rows", "w_in", "w_out", "w_pool", "w_glu", "w_router",
          "b_router", "w_gate", "w_up", "w_down", "g_final", "constants", "pooling")


def lay_out(inputs):
    a = {n: np.asarray(v) for n, v in inputs.items()}
    r = {n: np.ascontiguousarray(a[n]) for n in _AS_THEY_COME}

    def by_state(v):
        return v.reshape(2, 16, 2, 64).transpose(2, 3, 0, 1).reshape(P, 32)

    cols = [a[n].reshape(-1, P).T for n in ("c", "c_ctx", "g_mix", "g_ffn", "s_pool", "ssm_d", "b_glu")]
    cols.append(a["b_mod"].reshape(6, -1, P)[4].T)
    cols += [by_state(a["ssm_a_re"]), by_state(a["ssm_a_im"])]
    cols.append(by_state(np.broadcast_to(a["ssm_log_dt"][0][:, :, None], (2, 32, 64))))
    r["columns"] = np.ascontiguousarray(np.concatenate(cols, axis=1))
    b = np.stack([a["ssm_b_re"][0], a["ssm_b_im"][0]])
    c = np.stack([a["ssm_c_re"][0], a["ssm_c_im"][0]]).transpose(0, 1, 2, 4, 3)
    bc = [v.reshape(2, 2, 16, 2, 64, SG).transpose(3, 4, 1, 0, 2, 5).reshape(P, 1024) for v in (b, c)]
    r["ssm_bc"] = np.ascontiguousarray(np.concatenate(bc, axis=1))
    r["b_mod_rows"] = np.ascontiguousarray(a["b_mod"].reshape(3, 4, 512).transpose(1, 0, 2).reshape(4, 1536))
    r["constants"] = shape_constants()
    r["pooling"] = pooling_matrices()
    return {n: r[n] for n in _ORDER}


def kernel(**inputs):
    import concourse.bacc as bacc
    from concourse.bass_utils import run_bass_kernel_spmd

    nc = bacc.Bacc("TRN2", target_bir_lowering=False, num_devices=1)
    arrays, args = {}, []
    for name, a in lay_out(inputs).items():
        arrays[f"in_{name}"] = a
        args.append(nc.dram_tensor(f"in_{name}", a.shape, mybir.dt.from_np(a.dtype), kind="ExternalInput").ap())
    shape = inputs["x"].shape
    args.append(nc.dram_tensor("out_x", shape, F32, kind="ExternalOutput").ap())
    hybrid_block(nc, *args)
    r = run_bass_kernel_spmd(nc, [arrays], core_ids=[0])
    return r.results[0]["out_x"]
```
